# Optimizing a Trainium2 kernel written in Bass

```python
import math
import jax, jax.numpy as jnp
from jax import lax
import numpy as np

D_MODEL = 1024
BATCH = 1
SEQ = 256
DEPTH = 2

N_HEADS = 8
HEAD_DIM = 128
N_KV_HEADS = 2
Q_PER_KV = N_HEADS // N_KV_HEADS
ATTN_WIDTH = N_HEADS * HEAD_DIM
KV_WIDTH = N_KV_HEADS * HEAD_DIM
IDX_HEADS = 8
IDX_DIM = 64
TOPK_MAX = 256
Q_BLOCK = 128
ROPE_THETA = 500000.0
ROPE_FRACTION = 4

SSD_EXPAND = 2
SSD_INNER = SSD_EXPAND * D_MODEL
SSD_HEAD_DIM = 64
SSD_HEADS = SSD_INNER // SSD_HEAD_DIM
SSD_GROUPS = 4
SSD_HEADS_PER_GROUP = SSD_HEADS // SSD_GROUPS
SSD_STATE = 128
SSD_CONV = 4
SSD_CHUNK = 128
SSD_CONV_DIM = SSD_INNER + 2 * SSD_GROUPS * SSD_STATE

FFN_DIM = 2816
FFN_CONV = 3
NORM_EPS = 1e-6

IN_SPLITS = (ATTN_WIDTH, KV_WIDTH, KV_WIDTH, IDX_HEADS * IDX_DIM, IDX_DIM, IDX_HEADS,
             SSD_INNER, SSD_CONV_DIM, SSD_HEADS, D_MODEL, D_MODEL)
IN_COLS = (ATTN_WIDTH + 2 * KV_WIDTH + IDX_HEADS * IDX_DIM + IDX_DIM + IDX_HEADS
           + SSD_INNER + SSD_CONV_DIM + SSD_HEADS + 2 * D_MODEL)


def rms_norm(x, w):
    xf = x.astype(jnp.float32)
    y = xf * lax.rsqrt(jnp.mean(xf * xf, axis=-1, keepdims=True) + NORM_EPS)
    return (y * w.astype(jnp.float32)).astype(x.dtype)

def rope_tables(seq, rot_dim):
    inv = ROPE_THETA ** (-jnp.arange(0, rot_dim, 2, dtype=jnp.float32) / rot_dim)
    ang = jnp.arange(seq, dtype=jnp.float32)[:, None] * inv[None, :]
    return jnp.cos(ang), jnp.sin(ang)

def apply_partial_rope(t, cos, sin):
    half = cos.shape[-1]
    rot = 2 * half
    c = cos[None, :, None, :]
    s = sin[None, :, None, :]
    tf = t[..., :rot].astype(jnp.float32)
    x1, x2 = tf[..., :half], tf[..., half:]
    r = jnp.concatenate([x1 * c - x2 * s, x2 * c + x1 * s], axis=-1).astype(t.dtype)
    return jnp.concatenate([r, t[..., rot:]], axis=-1)

def causal_dwconv(u, w, b):
    width = w.shape[0]
    seq = u.shape[1]
    up = jnp.pad(u, ((0, 0), (width - 1, 0), (0, 0)))
    out = b
    for j in range(width):
        out = out + up[:, j:j + seq] * w[j]
    return out

def dsa_attention(q, k, v, q_idx, k_idx, w_idx):
    bsz, seq = q.shape[0], q.shape[1]
    topk = min(TOPK_MAX, seq // 4)
    n_blk = seq // Q_BLOCK
    kv = jnp.concatenate([k, v], axis=-1)
    k_idx_f = k_idx.astype(jnp.float32)
    kpos = jnp.arange(seq)
    scale = HEAD_DIM ** -0.5

    def block(i):
        t0 = i * Q_BLOCK
        sl = lambda a: lax.dynamic_slice_in_dim(a, t0, Q_BLOCK, axis=1)
        qpos = t0 + jnp.arange(Q_BLOCK)
        qi = sl(q_idx).astype(jnp.float32)
        wi = sl(w_idx).astype(jnp.float32)
        rel = jax.nn.relu(jnp.einsum('bqhd,bsd->bqhs', qi, k_idx_f))
        score = jnp.einsum('bqhs,bqh->bqs', rel, wi)
        causal = kpos[None, :] <= qpos[:, None]
        score = jnp.where(causal[None], score, -jnp.inf)
        _, sel = lax.top_k(score, topk)
        valid = sel <= qpos[None, :, None]
        kv_sel = jax.vmap(lambda a, ix: a[ix])(kv, sel)
        k_sel, v_sel = kv_sel[..., :HEAD_DIM], kv_sel[..., HEAD_DIM:]
        qb = sl(q).reshape(bsz, Q_BLOCK, N_KV_HEADS, Q_PER_KV, HEAD_DIM)
        logits = jnp.einsum('bqhgd,bqkhd->bqhgk', qb, k_sel).astype(jnp.float32) * scale
        logits = jnp.where(valid[:, :, None, None, :], logits, -jnp.inf)
        p = jax.nn.softmax(logits, axis=-1).astype(v.dtype)
        o = jnp.einsum('bqhgk,bqkhd->bqhgd', p, v_sel)
        return o.reshape(bsz, Q_BLOCK, ATTN_WIDTH)

    out = lax.map(block, jnp.arange(n_blk))
    return out.transpose(1, 0, 2, 3).reshape(bsz, seq, ATTN_WIDTH)

def ssd_scan(xdt, adt, bm, cm):
    bsz, seq = xdt.shape[0], xdt.shape[1]
    nc = seq // SSD_CHUNK
    X = xdt.reshape(bsz, nc, SSD_CHUNK, SSD_GROUPS, SSD_HEADS_PER_GROUP, SSD_HEAD_DIM)
    Bc = bm.reshape(bsz, nc, SSD_CHUNK, SSD_GROUPS, SSD_STATE)
    Cc = cm.reshape(bsz, nc, SSD_CHUNK, SSD_GROUPS, SSD_STATE)
    A = adt.reshape(bsz, nc, SSD_CHUNK, SSD_GROUPS, SSD_HEADS_PER_GROUP).transpose(0, 3, 4, 1, 2)
    A_cs = jnp.cumsum(A, axis=-1)
    tril = jnp.tril(jnp.ones((SSD_CHUNK, SSD_CHUNK), dtype=bool))
    seg = A_cs[..., :, None] - A_cs[..., None, :]
    Lmat = jnp.exp(jnp.where(tril, seg, -jnp.inf))
    CB = jnp.einsum('bclgn,bcsgn->bcgls', Cc, Bc)
    y_diag = jnp.einsum('bcgls,bgecls,bcsgep->bclgep', CB, Lmat, X)
    decay_states = jnp.exp(A_cs[..., -1:] - A_cs)
    states = jnp.einsum('bclgn,bgecl,bclgep->bcgepn', Bc, decay_states, X)
    chunk_decay = jnp.exp(A_cs[..., -1])

    def step(h, inp):
        s_c, d_c = inp
        return h * d_c[..., None, None] + s_c, h

    h0 = jnp.zeros(states.shape[:1] + states.shape[2:], states.dtype)
    _, states_in = lax.scan(step, h0, (states.transpose(1, 0, 2, 3, 4, 5), chunk_decay.transpose(3, 0, 1, 2)))
    states_in = states_in.transpose(1, 0, 2, 3, 4, 5)
    y_off = jnp.einsum('bclgn,bcgepn,bgecl->bclgep', Cc, states_in, jnp.exp(A_cs))
    return (y_diag + y_off).reshape(bsz, seq, SSD_HEADS, SSD_HEAD_DIM)

def mamba2_branch(z, xbc, dt_raw, conv_w, conv_b, dt_bias, a_log, d_skip, norm_w):
    bsz, seq = z.shape[0], z.shape[1]
    xbc = jax.nn.silu(causal_dwconv(xbc, conv_w, conv_b))
    gn = SSD_GROUPS * SSD_STATE
    xs = xbc[..., :SSD_INNER].reshape(bsz, seq, SSD_HEADS, SSD_HEAD_DIM)
    bm = xbc[..., SSD_INNER:SSD_INNER + gn].reshape(bsz, seq, SSD_GROUPS, SSD_STATE)
    cm = xbc[..., SSD_INNER + gn:].reshape(bsz, seq, SSD_GROUPS, SSD_STATE)
    dt = jax.nn.softplus(dt_raw.astype(jnp.float32) + dt_bias.astype(jnp.float32))
    A = -jnp.exp(a_log.astype(jnp.float32))
    y = ssd_scan(xs * dt[..., None], dt * A, bm, cm) + xs * d_skip[:, None]
    y = y.reshape(bsz, seq, SSD_INNER) * jax.nn.silu(z.astype(jnp.float32))
    yg = y.astype(jnp.float32).reshape(bsz, seq, SSD_GROUPS, SSD_INNER // SSD_GROUPS)
    yg = yg * lax.rsqrt(jnp.mean(yg * yg, axis=-1, keepdims=True) + NORM_EPS)
    y = yg.reshape(bsz, seq, SSD_INNER) * norm_w.astype(jnp.float32)
    return y.astype(z.dtype)

def hybrid_mixer(h, w_in, ssd_conv_w, ssd_conv_b, ssd_dt_bias, ssd_a_log, ssd_d, ssd_norm_w,
                 w_proj_attn, w_proj_ssd, w_out):
    bsz, seq = h.shape[0], h.shape[1]
    proj = h @ w_in
    offsets = np.cumsum(np.array(IN_SPLITS))[:-1].tolist()
    (q, k, v, qi, ki, wi, z, xbc, dt_raw, g_attn, g_ssd) = jnp.split(proj, offsets, axis=-1)
    cos_a, sin_a = rope_tables(seq, HEAD_DIM // ROPE_FRACTION)
    cos_i, sin_i = rope_tables(seq, IDX_DIM // ROPE_FRACTION)
    q = apply_partial_rope(q.reshape(bsz, seq, N_HEADS, HEAD_DIM), cos_a, sin_a)
    k = apply_partial_rope(k.reshape(bsz, seq, N_KV_HEADS, HEAD_DIM), cos_a, sin_a)
    v = v.reshape(bsz, seq, N_KV_HEADS, HEAD_DIM)
    qi = apply_partial_rope(qi.reshape(bsz, seq, IDX_HEADS, IDX_DIM), cos_i, sin_i)
    ki = apply_partial_rope(ki.reshape(bsz, seq, 1, IDX_DIM), cos_i, sin_i)[:, :, 0]
    a = dsa_attention(q, k, v, qi, ki, wi)
    b = mamba2_branch(z, xbc, dt_raw, ssd_conv_w, ssd_conv_b, ssd_dt_bias, ssd_a_log, ssd_d, ssd_norm_w)
    merged = jax.nn.sigmoid(g_attn) * (a @ w_proj_attn) + jax.nn.sigmoid(g_ssd) * (b @ w_proj_ssd)
    return merged @ w_out

def conv_glu_ffn(h, w_up, conv_w, conv_b, w_down):
    u = causal_dwconv(h @ w_up, conv_w, conv_b)
    gate, val = u[..., :FFN_DIM], u[..., FFN_DIM:]
    return (jax.nn.silu(gate) * val) @ w_down

def first_inputs(seed: int = 0) -> dict:
    key = jax.random.key(seed)
    ks = jax.random.split(key, 20)
    nrm = lambda k, shape, s: jax.random.normal(k, shape, jnp.float32) * s
    x = nrm(ks[0], (BATCH, SEQ, D_MODEL), 1.0)
    norm_mix_w = 1.0 + nrm(ks[1], (DEPTH, D_MODEL), 0.02)
    w_in = nrm(ks[2], (DEPTH, D_MODEL, IN_COLS), D_MODEL ** -0.5)
    ssd_conv_w = nrm(ks[3], (DEPTH, SSD_CONV, SSD_CONV_DIM), SSD_CONV ** -0.5)
    ssd_conv_b = nrm(ks[4], (DEPTH, SSD_CONV_DIM), 0.01)
    u = jax.random.uniform(ks[5], (DEPTH, SSD_HEADS), jnp.float32)
    dt0 = jnp.exp(u * (math.log(0.1) - math.log(0.001)) + math.log(0.001))
    ssd_dt_bias = dt0 + jnp.log(-jnp.expm1(-dt0))
    ssd_a_log = jnp.log(jax.random.uniform(ks[6], (DEPTH, SSD_HEADS), jnp.float32, minval=1.0, maxval=16.0))
    ssd_d = 1.0 + nrm(ks[7], (DEPTH, SSD_HEADS), 0.1)
    ssd_norm_w = 1.0 + nrm(ks[8], (DEPTH, SSD_INNER), 0.02)
    w_proj_attn = nrm(ks[9], (DEPTH, ATTN_WIDTH, D_MODEL), ATTN_WIDTH ** -0.5)
    w_proj_ssd = nrm(ks[10], (DEPTH, SSD_INNER, D_MODEL), SSD_INNER ** -0.5)
    w_out = nrm(ks[11], (DEPTH, D_MODEL, D_MODEL), D_MODEL ** -0.5)
    norm_ffn_w = 1.0 + nrm(ks[12], (DEPTH, D_MODEL), 0.02)
    ffn_w_up = nrm(ks[13], (DEPTH, D_MODEL, 2 * FFN_DIM), D_MODEL ** -0.5)
    ffn_conv_w = nrm(ks[14], (DEPTH, FFN_CONV, 2 * FFN_DIM), FFN_CONV ** -0.5)
    ffn_conv_b = nrm(ks[15], (DEPTH, 2 * FFN_DIM), 0.01)
    ffn_w_down = nrm(ks[16], (DEPTH, FFN_DIM, D_MODEL), FFN_DIM ** -0.5)
    norm_final_w = 1.0 + nrm(ks[17], (D_MODEL,), 0.02)
    return {'x': x, 'norm_mix_w': norm_mix_w, 'w_in': w_in, 'ssd_conv_w': ssd_conv_w,
            'ssd_conv_b': ssd_conv_b, 'ssd_dt_bias': ssd_dt_bias, 'ssd_a_log': ssd_a_log,
            'ssd_d': ssd_d, 'ssd_norm_w': ssd_norm_w, 'w_proj_attn': w_proj_attn,
            'w_proj_ssd': w_proj_ssd, 'w_out': w_out, 'norm_ffn_w': norm_ffn_w,
            'ffn_w_up': ffn_w_up, 'ffn_conv_w': ffn_conv_w, 'ffn_conv_b': ffn_conv_b,
            'ffn_w_down': ffn_w_down, 'norm_final_w': norm_final_w}

def first_block(x, norm_mix_w, w_in, ssd_conv_w, ssd_conv_b, ssd_dt_bias, ssd_a_log, ssd_d, ssd_norm_w,
              w_proj_attn, w_proj_ssd, w_out, norm_ffn_w, ffn_w_up, ffn_conv_w, ffn_conv_b,
              ffn_w_down, norm_final_w):
    for l in range(DEPTH):
        h = rms_norm(x, norm_mix_w[l])
        x = x + hybrid_mixer(h, w_in[l], ssd_conv_w[l], ssd_conv_b[l], ssd_dt_bias[l], ssd_a_log[l],
                             ssd_d[l], ssd_norm_w[l], w_proj_attn[l], w_proj_ssd[l], w_out[l])
        h = rms_norm(x, norm_ffn_w[l])
        x = x + conv_glu_ffn(h, ffn_w_up[l], ffn_conv_w[l], ffn_conv_b[l], ffn_w_down[l])
    return rms_norm(x, norm_final_w)


GRID_W = 64
CTX_LEN = 256
HEAD_DIM_2 = 64
ROPE_THETA_2 = 10000.0
RMS_EPS = 1e-6
H_A = 8
NOPE_A = 64
ROPE_A = 32
V_A = 64
Q_LORA = 384
KV_LORA = 256
H_B = 8
KV_B = 2
G_B = H_B // KV_B
AB_IN = Q_LORA + KV_LORA + ROPE_A + H_B * HEAD_DIM_2 + 2 * KV_B * HEAD_DIM_2
AB_OUT = H_A * V_A + H_B * HEAD_DIM_2
H_C = 16
WIN_R = 8
WIN_C = 16
C_WIDTH = H_C * HEAD_DIM_2
N_GROUPS = 4
EXPERTS_PER_GROUP = 8
N_EXPERTS = N_GROUPS * EXPERTS_PER_GROUP
TOP_K = 2
D_EXPERT = 512
MOE_BLOCK = 128
N_EVEN = (DEPTH + 1) // 2
N_ODD = DEPTH // 2


def rmsnorm(x, g):
    xf = x.astype(jnp.float32)
    y = xf * lax.rsqrt(jnp.mean(xf * xf, axis=-1, keepdims=True) + RMS_EPS)
    return (y * g.astype(jnp.float32)).astype(x.dtype)

def modulate(x, g, shift, scale):
    return rmsnorm(x, g) * (1 + scale) + shift

def axial_rope_table(rows, cols, rot_dim):
    n = rot_dim // 4
    inv = ROPE_THETA_2 ** (-jnp.arange(n, dtype=jnp.float32) / n)
    ang = jnp.concatenate([rows[:, None] * inv, cols[:, None] * inv], axis=-1)
    return jnp.cos(ang), jnp.sin(ang)

def apply_rope(x, rope):
    cos, sin = rope
    cos = cos.astype(x.dtype)
    sin = sin.astype(x.dtype)
    x1 = x[..., 0::2]
    x2 = x[..., 1::2]
    return jnp.stack([x1 * cos - x2 * sin, x1 * sin + x2 * cos], axis=-1).reshape(x.shape)

def heads_to_tokens(o):
    b, h, t, d = o.shape
    return o.transpose(0, 2, 1, 3).reshape(b, t, h * d)

def attend(q, k, v):
    s = jnp.einsum('bhgqd,bhkd->bhgqk', q, k, preferred_element_type=jnp.float32)
    p = jax.nn.softmax(s, axis=-1).astype(v.dtype)
    return jnp.einsum('bhgqk,bhkd->bhgqd', p, v)

def prefix_attention(q, k_lat, v_lat, k_ctx, v_ctx):
    b, hk, g, s, d = q.shape
    nb = s // Q_BLOCK
    k_all = jnp.concatenate([k_ctx, k_lat], axis=2)
    v_all = jnp.concatenate([v_ctx, v_lat], axis=2)
    qb = q.reshape(b, hk, g, nb, Q_BLOCK, d).transpose(3, 0, 1, 2, 4, 5)
    o = lax.map(lambda qblk: attend(qblk, k_all, v_all), qb)
    return o.transpose(1, 2, 3, 0, 4, 5).reshape(b, hk, g, s, v_all.shape[-1])

def mixer_ab(h_ctx, h_lat, rope_a, rope_b, w_in, w_out, q_norm, w_q_up, kv_norm, w_kv_up, gq_norm, gk_norm, need_ctx):
    def project(h, ra, rb):
        bsz, t, _ = h.shape
        p = h @ w_in
        o0 = Q_LORA
        o1 = o0 + KV_LORA
        o2 = o1 + ROPE_A
        o3 = o2 + H_B * HEAD_DIM_2
        o4 = o3 + KV_B * HEAD_DIM_2
        cq, ckv, kr = p[..., :o0], p[..., o0:o1], p[..., o1:o2]
        gq, gk, gv = p[..., o2:o3], p[..., o3:o4], p[..., o4:]
        qa = (rmsnorm(cq, q_norm) @ w_q_up).reshape(bsz, t, H_A, NOPE_A + ROPE_A).transpose(0, 2, 1, 3)
        kva = (rmsnorm(ckv, kv_norm) @ w_kv_up).reshape(bsz, t, H_A, NOPE_A + V_A).transpose(0, 2, 1, 3)
        q_nope, q_rope = qa[..., :NOPE_A], qa[..., NOPE_A:]
        k_nope, va = kva[..., :NOPE_A], kva[..., NOPE_A:]
        k_rope = kr[:, None]
        if ra is not None:
            q_rope = apply_rope(q_rope, ra)
            k_rope = apply_rope(k_rope, ra)
        qa = jnp.concatenate([q_nope, q_rope], axis=-1) * ((NOPE_A + ROPE_A) ** -0.5)
        ka = jnp.concatenate([k_nope, jnp.broadcast_to(k_rope, (bsz, H_A, t, ROPE_A))], axis=-1)
        qb = rmsnorm(gq.reshape(bsz, t, H_B, HEAD_DIM_2).transpose(0, 2, 1, 3), gq_norm)
        kb = rmsnorm(gk.reshape(bsz, t, KV_B, HEAD_DIM_2).transpose(0, 2, 1, 3), gk_norm)
        vb = gv.reshape(bsz, t, KV_B, HEAD_DIM_2).transpose(0, 2, 1, 3)
        if rb is not None:
            qb = apply_rope(qb, rb)
            kb = apply_rope(kb, rb)
        qb = qb.reshape(bsz, KV_B, G_B, t, HEAD_DIM_2) * (HEAD_DIM_2 ** -0.5)
        return qa[:, :, None], ka, va, qb, kb, vb

    qa_l, ka_l, va_l, qb_l, kb_l, vb_l = project(h_lat, rope_a, rope_b)
    qa_c, ka_c, va_c, qb_c, kb_c, vb_c = project(h_ctx, None, None)
    bsz, s = h_lat.shape[0], h_lat.shape[1]
    oa = prefix_attention(qa_l, ka_l, va_l, ka_c, va_c).reshape(bsz, H_A, s, V_A)
    ob = prefix_attention(qb_l, kb_l, vb_l, kb_c, vb_c).reshape(bsz, H_B, s, HEAD_DIM_2)
    out_lat = jnp.concatenate([heads_to_tokens(oa), heads_to_tokens(ob)], axis=-1) @ w_out
    out_ctx = None
    if need_ctx:
        t = h_ctx.shape[1]
        oa_c = attend(qa_c, ka_c, va_c).reshape(bsz, H_A, t, V_A)
        ob_c = attend(qb_c, kb_c, vb_c).reshape(bsz, H_B, t, HEAD_DIM_2)
        out_ctx = jnp.concatenate([heads_to_tokens(oa_c), heads_to_tokens(ob_c)], axis=-1) @ w_out
    return out_ctx, out_lat

def mixer_na(h_ctx, h_lat, nbr_idx, rel_idx, w_in, w_out, rpb, need_ctx):
    def project(h):
        bsz, t, _ = h.shape
        p = (h @ w_in).reshape(bsz, t, 3, H_C, HEAD_DIM_2).transpose(2, 0, 3, 1, 4)
        return p[0] * (HEAD_DIM_2 ** -0.5), p[1], p[2]

    q_l, k_l, v_l = project(h_lat)
    q_c, k_c, v_c = project(h_ctx)
    bsz, s = h_lat.shape[0], h_lat.shape[1]
    nk = nbr_idx.shape[1]
    nb = s // Q_BLOCK
    rpb_flat = rpb.reshape(H_C, -1)
    qb = q_l.reshape(bsz, H_C, nb, Q_BLOCK, HEAD_DIM_2).transpose(2, 0, 1, 3, 4)
    idx_b = nbr_idx.reshape(nb, Q_BLOCK, nk)
    rel_b = rel_idx.reshape(nb, Q_BLOCK, nk)

    def one_block(args):
        qblk, ib, rb = args
        kg = jnp.take(k_l, ib, axis=2)
        vg = jnp.take(v_l, ib, axis=2)
        s_n = jnp.einsum('bhqd,bhqnd->bhqn', qblk, kg, preferred_element_type=jnp.float32) + rpb_flat[:, rb].astype(jnp.float32)
        s_c = jnp.einsum('bhqd,bhcd->bhqc', qblk, k_c, preferred_element_type=jnp.float32)
        p = jax.nn.softmax(jnp.concatenate([s_n, s_c], axis=-1), axis=-1).astype(v_l.dtype)
        return jnp.einsum('bhqn,bhqnd->bhqd', p[..., :nk], vg) + jnp.einsum('bhqc,bhcd->bhqd', p[..., nk:], v_c)

    o = lax.map(one_block, (qb, idx_b, rel_b))
    out_lat = o.transpose(1, 0, 3, 2, 4).reshape(bsz, s, C_WIDTH) @ w_out
    out_ctx = None
    if need_ctx:
        oc = attend(q_c[:, :, None], k_c, v_c)[:, :, 0]
        out_ctx = heads_to_tokens(oc) @ w_out
    return out_ctx, out_lat

def hier_moe(h, w_rg, b_rg, w_re, b_re, w_gate, w_up, w_down):
    n, d = h.shape
    hf = h.astype(jnp.float32)
    pg = jax.nn.softmax(hf @ w_rg.astype(jnp.float32) + b_rg.astype(jnp.float32), axis=-1)
    g_sel = jnp.argmax(pg, axis=-1)
    p_gsel = jnp.take_along_axis(pg, g_sel[:, None], axis=-1)
    le = (hf @ w_re.astype(jnp.float32) + b_re.astype(jnp.float32)).reshape(n, N_GROUPS, EXPERTS_PER_GROUP)
    le_sel = jnp.take_along_axis(le, g_sel[:, None, None], axis=1)[:, 0]
    top_p, top_i = lax.top_k(jax.nn.softmax(le_sel, axis=-1), TOP_K)
    gate_w = p_gsel * top_p / jnp.sum(top_p, axis=-1, keepdims=True)
    experts = g_sel[:, None] * EXPERTS_PER_GROUP + top_i

    nkk = n * TOP_K
    flat_e = experts.reshape(-1).astype(jnp.int32)
    flat_w = gate_w.reshape(-1)
    order = jnp.argsort(flat_e)
    sorted_e = flat_e[order]
    tok_sorted = (jnp.arange(nkk, dtype=jnp.int32) // TOP_K)[order]
    w_sorted = flat_w[order]
    counts = jnp.bincount(flat_e, length=N_EXPERTS)
    padded = ((counts + MOE_BLOCK - 1) // MOE_BLOCK) * MOE_BLOCK
    ends = jnp.cumsum(padded)
    pad_start = ends - padded
    start = jnp.cumsum(counts) - counts
    rank = jnp.arange(nkk, dtype=jnp.int32) - start[sorted_e]
    dest = pad_start[sorted_e] + rank
    total = -(-(nkk + N_EXPERTS * (MOE_BLOCK - 1)) // MOE_BLOCK) * MOE_BLOCK
    nblk = total // MOE_BLOCK
    buf_tok = jnp.full((total,), n, jnp.int32).at[dest].set(tok_sorted)
    h_pad = jnp.concatenate([h, jnp.zeros((1, d), h.dtype)], axis=0)
    x_buf = h_pad[buf_tok].reshape(nblk, MOE_BLOCK, d)
    blk_e = jnp.clip(jnp.searchsorted(ends, jnp.arange(nblk, dtype=ends.dtype) * MOE_BLOCK, side='right'), 0, N_EXPERTS - 1)

    def run_block(args):
        xb, e = args
        return (jax.nn.silu(xb @ w_gate[e]) * (xb @ w_up[e])) @ w_down[e]

    y = lax.map(run_block, (x_buf, blk_e)).reshape(total, d)
    return jnp.zeros((n, d), h.dtype).at[tok_sorted].add(y[dest] * w_sorted[:, None].astype(h.dtype))

def second_inputs(seed: int = 0) -> dict:
    key = jax.random.key(seed)
    ks = jax.random.split(key, 32)

    def nrm(k, shape, scale):
        return jax.random.normal(k, shape, jnp.float32) * scale

    def gain(k, shape):
        return 1.0 + nrm(k, shape, 0.1)

    D = D_MODEL
    return {
        "x": nrm(ks[0], (BATCH, SEQ, D), 1.0),
        "c": nrm(ks[1], (BATCH, D), 1.0),
        "ctx": nrm(ks[2], (BATCH, CTX_LEN, D), 1.0),
        "c_ctx": nrm(ks[3], (D,), 1.0),
        "w_ada": nrm(ks[4], (DEPTH, D, 6 * D), 0.02),
        "b_ada": nrm(ks[5], (DEPTH, 6 * D), 0.02),
        "norm_mix": gain(ks[6], (DEPTH, D)),
        "norm_ffn": gain(ks[7], (DEPTH, D)),
        "norm_final": gain(ks[8], (D,)),
        "ab_w_in": nrm(ks[9], (N_EVEN, D, AB_IN), D ** -0.5),
        "ab_w_out": nrm(ks[10], (N_EVEN, AB_OUT, D), AB_OUT ** -0.5),
        "mla_q_norm": gain(ks[11], (N_EVEN, Q_LORA)),
        "mla_w_q_up": nrm(ks[12], (N_EVEN, Q_LORA, H_A * (NOPE_A + ROPE_A)), Q_LORA ** -0.5),
        "mla_kv_norm": gain(ks[13], (N_EVEN, KV_LORA)),
        "mla_w_kv_up": nrm(ks[14], (N_EVEN, KV_LORA, H_A * (NOPE_A + V_A)), KV_LORA ** -0.5),
        "gqa_q_norm": gain(ks[15], (N_EVEN, HEAD_DIM_2)),
        "gqa_k_norm": gain(ks[16], (N_EVEN, HEAD_DIM_2)),
        "na_w_in": nrm(ks[17], (N_ODD, D, 3 * C_WIDTH), D ** -0.5),
        "na_w_out": nrm(ks[18], (N_ODD, C_WIDTH, D), C_WIDTH ** -0.5),
        "na_rpb": nrm(ks[19], (N_ODD, H_C, 2 * WIN_R - 1, 2 * WIN_C - 1), 0.1),
        "moe_w_rg": nrm(ks[20], (DEPTH, D, N_GROUPS), D ** -0.5),
        "moe_b_rg": nrm(ks[21], (DEPTH, N_GROUPS), 0.01),
        "moe_w_re": nrm(ks[22], (DEPTH, D, N_EXPERTS), D ** -0.5),
        "moe_b_re": nrm(ks[23], (DEPTH, N_EXPERTS), 0.01),
        "moe_w_gate": nrm(ks[24], (DEPTH, N_EXPERTS, D, D_EXPERT), D ** -0.5),
        "moe_w_up": nrm(ks[25], (DEPTH, N_EXPERTS, D, D_EXPERT), D ** -0.5),
        "moe_w_down": nrm(ks[26], (DEPTH, N_EXPERTS, D_EXPERT, D), D_EXPERT ** -0.5),
    }

def second_block(x, c, ctx, c_ctx, w_ada, b_ada, norm_mix, norm_ffn, norm_final, ab_w_in, ab_w_out, mla_q_norm, mla_w_q_up, mla_kv_norm, mla_w_kv_up, gqa_q_norm, gqa_k_norm, na_w_in, na_w_out, na_rpb, moe_w_rg, moe_b_rg, moe_w_re, moe_b_re, moe_w_gate, moe_w_up, moe_w_down):
    bsz, s, d = x.shape
    n_ctx = ctx.shape[1]
    rows_n = s // GRID_W
    wr = min(WIN_R, rows_n)
    t = jnp.arange(s, dtype=jnp.int32)
    r = t // GRID_W
    col = t % GRID_W
    rope_a = axial_rope_table(r.astype(jnp.float32), col.astype(jnp.float32), ROPE_A)
    rope_b = axial_rope_table(r.astype(jnp.float32), col.astype(jnp.float32), HEAD_DIM_2)
    rs = jnp.clip(r - wr // 2, 0, rows_n - wr)
    cs = jnp.clip(col - WIN_C // 2, 0, GRID_W - WIN_C)
    key_r = rs[:, None] + jnp.arange(wr, dtype=jnp.int32)[None]
    key_c = cs[:, None] + jnp.arange(WIN_C, dtype=jnp.int32)[None]
    nbr_idx = (key_r[:, :, None] * GRID_W + key_c[:, None, :]).reshape(s, wr * WIN_C)
    rel_idx = ((key_r - r[:, None] + WIN_R - 1)[:, :, None] * (2 * WIN_C - 1)
               + (key_c - col[:, None] + WIN_C - 1)[:, None, :]).reshape(s, wr * WIN_C)

    x_lat = x
    x_ctx = ctx
    silu_c = jax.nn.silu(c)
    silu_cc = jax.nn.silu(c_ctx)
    for l in range(DEPTH):
        last = l == DEPTH - 1
        mod_l = (silu_c @ w_ada[l] + b_ada[l])[:, None, :]
        mod_c = (silu_cc @ w_ada[l] + b_ada[l])[None, None, :]
        sh1, sc1, g1, sh2, sc2, g2 = jnp.split(mod_l, 6, axis=-1)
        sh1c, sc1c, g1c, sh2c, sc2c, g2c = jnp.split(mod_c, 6, axis=-1)
        h_l = modulate(x_lat, norm_mix[l], sh1, sc1)
        h_c = modulate(x_ctx, norm_mix[l], sh1c, sc1c)
        if l % 2 == 0:
            i = l // 2
            o_c, o_l = mixer_ab(h_c, h_l, rope_a, rope_b, ab_w_in[i], ab_w_out[i], mla_q_norm[i], mla_w_q_up[i],
                                mla_kv_norm[i], mla_w_kv_up[i], gqa_q_norm[i], gqa_k_norm[i], not last)
        else:
            i = l // 2
            o_c, o_l = mixer_na(h_c, h_l, nbr_idx, rel_idx, na_w_in[i], na_w_out[i], na_rpb[i], not last)
        x_lat = x_lat + g1 * o_l
        h_l = modulate(x_lat, norm_ffn[l], sh2, sc2)
        if not last:
            x_ctx = x_ctx + g1c * o_c
            h_c = modulate(x_ctx, norm_ffn[l], sh2c, sc2c)
            tokens = jnp.concatenate([h_c.reshape(-1, d), h_l.reshape(-1, d)], axis=0)
            y = hier_moe(tokens, moe_w_rg[l], moe_b_rg[l], moe_w_re[l], moe_b_re[l], moe_w_gate[l], moe_w_up[l], moe_w_down[l])
            n_c = bsz * n_ctx
            x_ctx = x_ctx + g2c * y[:n_c].reshape(bsz, n_ctx, d)
            x_lat = x_lat + g2 * y[n_c:].reshape(bsz, s, d)
        else:
            y = hier_moe(h_l.reshape(-1, d), moe_w_rg[l], moe_b_rg[l], moe_w_re[l], moe_b_re[l], moe_w_gate[l], moe_w_up[l], moe_w_down[l])
            x_lat = x_lat + g2 * y.reshape(bsz, s, d)
    return rmsnorm(x_lat, norm_final)


def setup_inputs(seed=0):
    out = dict(first_inputs(seed))
    for name, value in second_inputs(seed + 1).items():
        if name != "x":
            out[name + "_2"] = value
    return out


def reference(
    x, norm_mix_w, w_in, ssd_conv_w, ssd_conv_b, ssd_dt_bias, ssd_a_log, ssd_d, ssd_norm_w,
    w_proj_attn, w_proj_ssd, w_out, norm_ffn_w, ffn_w_up, ffn_conv_w, ffn_conv_b, ffn_w_down,
    norm_final_w, c_2, ctx_2, c_ctx_2, w_ada_2, b_ada_2, norm_mix_2, norm_ffn_2, norm_final_2,
    ab_w_in_2, ab_w_out_2, mla_q_norm_2, mla_w_q_up_2, mla_kv_norm_2, mla_w_kv_up_2,
    gqa_q_norm_2, gqa_k_norm_2, na_w_in_2, na_w_out_2, na_rpb_2, moe_w_rg_2, moe_b_rg_2,
    moe_w_re_2, moe_b_re_2, moe_w_gate_2, moe_w_up_2, moe_w_down_2,
):
    x = first_block(
        x, norm_mix_w, w_in, ssd_conv_w, ssd_conv_b, ssd_dt_bias, ssd_a_log, ssd_d, ssd_norm_w,
        w_proj_attn, w_proj_ssd, w_out, norm_ffn_w, ffn_w_up, ffn_conv_w, ffn_conv_b,
        ffn_w_down, norm_final_w,
    )
    return second_block(
        x, c_2, ctx_2, c_ctx_2, w_ada_2, b_ada_2, norm_mix_2, norm_ffn_2, norm_final_2,
        ab_w_in_2, ab_w_out_2, mla_q_norm_2, mla_w_q_up_2, mla_kv_norm_2, mla_w_kv_up_2,
        gqa_q_norm_2, gqa_k_norm_2, na_w_in_2, na_w_out_2, na_rpb_2, moe_w_rg_2, moe_b_rg_2,
        moe_w_re_2, moe_b_re_2, moe_w_gate_2, moe_w_up_2, moe_w_down_2,
    )


_drawn_inputs = setup_inputs


def setup_inputs(seed=0):
    import zlib

    import numpy as np

    out = dict(_drawn_inputs(seed))
    spreads = {}
    factors = {'ffn_conv_b': 2.752,
     'norm_mix_2': 2.781,
     'mla_q_norm_2': 5.552,
     'mla_kv_norm_2': 2.765,
     'gqa_q_norm_2': 8.0,
     'gqa_k_norm_2': 7.544,
     'na_rpb_2': 8.0,
     'moe_b_rg_2': 5.751,
     'moe_b_re_2': 5.723}
    for name, (base, spread) in spreads.items():
        noise = np.random.default_rng([zlib.crc32(name.encode()), seed]).standard_normal(out[name].shape)
        drawn = base * np.exp(spread * noise) if base else spread * noise
        out[name] = __import__('jax').numpy.asarray(drawn.astype(out[name].dtype))
    for name, factor in factors.items():
        out[name] = (out[name] * factor).astype(out[name].dtype)
    return out
```

```python
from contextlib import ExitStack

import numpy as np

import concourse.bass as bass
from concourse import mybir

F32 = mybir.dt.float32
U32 = mybir.dt.uint32
ALU = mybir.AluOpType
ACT = mybir.ActivationFunctionType
AX = mybir.AxisListType

P = 128
D = 1024
KD = D // P
SEQ = 256
TT = SEQ // P
EPS = 1e-6
NEG = -1.0e30
TAKEN = -3.0e38

HEADS, HD, KVH = 8, 128, 2
IH, IDM = 8, 64
TOPK = min(256, SEQ // 4)
INNER, SHD, SHEADS, GROUPS, STATE = 2048, 64, 32, 4, 128
HPG = SHEADS // GROUPS
GW = INNER // GROUPS
CONV = 4
XBC = INNER + 2 * GROUPS * STATE
XCH = XBC // P
FFN, FCONV = 2816, 3
FCH = FFN // P
COL = {}
_o = 0
for _n, _w in (("q", 1024), ("k", 256), ("v", 256), ("qi", 512), ("ki", 64), ("wi", 8), ("z", INNER),
               ("xbc", XBC), ("dt", SHEADS), ("ga", D), ("gs", D)):
    COL[_n] = _o
    _o += _w

HA, NOPE, ROPE, VA, QL, KVL = 8, 64, 32, 64, 384, 256
HB, KVB, HD2 = 8, 2, 64
HC = 16
NT2 = 4
GRID_W, WIN_R, WIN_C = 64, 8, 16
EXPERTS, EG, NGR, DE = 32, 8, 4, 512
CAP = 128

PC = {}
_o = 0
for _n, _w in (("norm_mix", KD), ("conv_w", XCH * CONV), ("conv_b", XCH), ("ssd_norm", INNER // P),
               ("norm_ffn", KD), ("fconv_w", 2 * FCH * FCONV), ("fconv_b", 2 * FCH)):
    PC[_n] = _o
    _o += _w
PCW = _o
PD = {}
_o = 0
for _n, _w in (("c", 2 * KD), ("b_ada", 2 * 48), ("norm_mix", 2 * KD), ("q_norm", QL // P),
               ("kv_norm", KVL // P)):
    PD[_n] = _o
    _o += _w
PDW = _o
PR = {}
_o = 0
for _n, _w in (("dt_bias", 64), ("a_log", 64), ("d", 64), ("gq_norm", 64), ("gk_norm", 64),
               ("b_router", 72)):
    PR[_n] = _o
    _o += _w
PRW = _o


def shape_constants():
    parts = {}
    i = np.arange(P)
    parts["ident"] = np.eye(P, dtype=np.float32)
    parts["upto"] = (i[:, None] <= i[None, :]).astype(np.float32)
    parts["before"] = (i[:, None] < i[None, :]).astype(np.float32)
    parts["ones"] = np.ones((P, P), np.float32)
    parts["segmask"] = np.where(i[:, None] <= i[None, :], 0.0, NEG).astype(np.float32)
    pos = np.arange(SEQ)
    causal = np.where(pos[None, :] <= pos[:, None], 0.0, NEG).astype(np.float32)
    parts["causal"] = causal.reshape(TT, P, SEQ).transpose(1, 0, 2)

    def split(a):
        return a.reshape(TT, P, -1).transpose(1, 0, 2)

    def half_tables(rot):
        inv = np.float32(500000.0) ** (-np.arange(0, rot, 2, dtype=np.float32) / np.float32(rot))
        ang = (pos.astype(np.float32)[:, None] * inv[None, :].astype(np.float32)).astype(np.float32)
        c, s = np.cos(ang), np.sin(ang)
        return split(np.concatenate([c, c], 1)), split(np.concatenate([-s, s], 1))

    parts["cosa"], parts["sina"] = half_tables(HD // 4)
    parts["cosi"], parts["sini"] = half_tables(IDM // 4)

    def axial(rot):
        n = rot // 4
        inv = np.float32(10000.0) ** (-np.arange(n, dtype=np.float32) / np.float32(n))
        r, c = (pos // GRID_W).astype(np.float32), (pos % GRID_W).astype(np.float32)
        ang = np.concatenate([r[:, None] * inv, c[:, None] * inv], 1).astype(np.float32)
        co, si = np.cos(ang), np.sin(ang)
        return (split(np.stack([co, co], -1).reshape(SEQ, rot)),
                split(np.stack([-si, si], -1).reshape(SEQ, rot)))

    parts["cos2a"], parts["sin2a"] = axial(ROPE)
    parts["cos2b"], parts["sin2b"] = axial(HD2)
    rows = SEQ // GRID_W
    cs = np.clip(pos % GRID_W - WIN_C // 2, 0, GRID_W - WIN_C)
    kc = pos % GRID_W
    seen = (kc[None, :] >= cs[:, None]) & (kc[None, :] < cs[:, None] + WIN_C)
    assert rows <= WIN_R
    parts["window"] = split(np.where(seen, 0.0, NEG).astype(np.float32))
    parts["iota"] = np.broadcast_to(np.arange(EXPERTS, dtype=np.float32), (P, EXPERTS))
    token = (np.arange(NT2)[None, :] * P + i[:, None]).astype(np.float32)
    parts["token"] = token
    where, cols, at = {}, [], 0
    for name, a in parts.items():
        w = int(np.prod(a.shape[1:]))
        where[name] = (at, a.shape[1:])
        cols.append(np.ascontiguousarray(a, dtype=np.float32).reshape(P, w))
        at += w
    return np.concatenate(cols, 1), where


CONST, CONST_AT = shape_constants()


class Signal:

    def __init__(self, ctx, nc, name):
        self.sem = ctx.enter_context(nc.semaphore(name))
        self.name = name
        self.count = 0

    def mark(self, ins, by=1):
        self.count += by
        return (self, self.count)


class Buf:

    def __init__(self, t):
        self.t = t
        self.free = []


class Turn:

    def __init__(self, bufs):
        self.bufs = bufs
        self.n = 0

    def next(self):
        b = self.bufs[self.n % len(self.bufs)]
        self.n += 1
        return b


def pipeline(parts, depth):
    parts = list(parts)
    running = []
    while parts or running:
        if parts and len(running) < depth:
            running.append(parts.pop(0))
        for r in list(running):
            try:
                next(r)
            except StopIteration:
                running.remove(r)


RING = 5


class Core:

    def __init__(self, nc, ctx, block, A):
        self.nc, self.ctx, self.block, self.A = nc, ctx, block, A
        self.waited = {}
        self.names = 0
        self.spread = []
        self.pe = Signal(ctx, nc, "tensor_done")
        self.dve = Signal(ctx, nc, "vector_done")
        self.act = Signal(ctx, nc, "scalar_done")
        self.pool = Signal(ctx, nc, "pool_done")
        self.moved = Turn([Signal(ctx, nc, f"moved{i}") for i in range(24)])
        self.landed = [Signal(ctx, nc, f"weights_landed{i}") for i in range(RING)]
        self.slots = [ctx.enter_context(nc.sbuf_tensor(f"wslot{i}", [P, 4096], F32)) for i in range(RING)]
        self.banks = Turn([Buf(ctx.enter_context(nc.psum_tensor(f"bank{i}", [P, 512], F32))) for i in range(8)])
        self.const = self.sb("const", [P, CONST.shape[1]])
        self.eps = self.sb("eps", [P, 1])
        self.ident = self.c("ident")
        self.plan, self.landings, self.taken = [], {}, 0

    def sb(self, name, shape, dt=F32, ctx=None):
        self.names += 1
        return (ctx or self.ctx).enter_context(self.nc.sbuf_tensor(f"{name}_{self.names}", shape, dt))

    def turn(self, ctx, name, n, shape, dt=F32):
        return Turn([Buf(self.sb(f"{name}{i}", shape, dt, ctx)) for i in range(n)])

    def c(self, name):
        at, shape = CONST_AT[name]
        w = int(np.prod(shape))
        ap = self.const[:, at:at + w]
        return ap if len(shape) == 1 else ap.rearrange("p (a b) -> p a b", a=shape[0])

    def due(self, eng, *marks):
        left = []
        for m in marks:
            if m is None:
                continue
            sig, value = m
            key = (str(eng.engine), sig.name)
            if self.waited.get(key, 0) < value:
                self.waited[key] = value
                left.append((sig.sem, value))
        return left

    def move(self, eng, out, in_, *deps):
        sig = self.moved.next()
        for due in self.due(eng, (sig, sig.count) if sig.count else None, *deps):
            eng.wait_ge(*due)
        return sig.mark(eng.dma_start(out, in_).then_inc(sig.sem, 16), 16)

    def settle(self):
        marks = [(s, s.count) for s in [self.pe, self.dve, self.act, self.pool] + self.moved.bufs if s.count]
        self.settled = marks

        @self.block.tensor
        def _(e):
            for due in self.due(e, *marks):
                e.wait_ge(*due)

        @self.block.vector
        def _(e):
            for due in self.due(e, *marks):
                e.wait_ge(*due)

        @self.block.scalar
        def _(e):
            for due in self.due(e, *marks):
                e.wait_ge(*due)

        @self.block.gpsimd
        def _(e):
            for due in self.due(e, *marks):
                e.wait_ge(*due)

    def plan_tile(self, key, w, k0, kc, n0, n):
        self.plan.append((key, [(0, kc, n, 0, n, w[k0:k0 + kc * P, n0:n0 + n])]))

    def plan_expert(self, key, name, l, b, kc, n):
        w = self.A[name]
        if b < EXPERTS:
            self.plan_tile(key, w[l, b], 0, kc, 0, n)
        else:
            self.plan.append((key, [(0, kc, n, 0, n, (w, l, b - EXPERTS))]))

    def issue(self, i, *deps):
        if i >= len(self.plan):
            return
        key, parts = self.plan[i]
        sig = self.landed[i % RING]

        @self.block.sync
        def _(sp):
            for due in self.due(sp, *deps):
                sp.wait_ge(*due)
            for at, kc, n, c0, cn, src in parts:
                if isinstance(src, tuple):
                    wt, l, x = src
                    for due in self.due(sp, self.xid_ready):
                        sp.wait_ge(*due)
                    e = sp.value_load(self.xid[0:1, x:x + 1], min_val=0, max_val=EXPERTS - 1)
                    src = wt[l, bass.ds(e, 1)].rearrange("a k n -> (a k) n")
                dst = self.slots[i % RING][:, at:at + kc * n].rearrange("p (k n) -> p k n", k=kc)[:, :, c0:c0 + cn]
                self.landings[i] = sig.mark(sp.dma_start(dst, src.rearrange("(k p) n -> p k n", p=P)).then_inc(sig.sem, 16), 16)

    def start_weights(self):
        for i in range(RING):
            self.issue(i)

    def take(self, key):
        i = self.taken
        self.taken += 1
        want, parts = self.plan[i]
        assert want == key, (want, key)
        _, kc, n, _, _, _ = parts[0]
        view = self.slots[i % RING][:, 0:kc * n].rearrange("p (k n) -> p k n", k=kc)
        return i, view, self.landings[i]

    def give(self, i, mark):
        self.issue(i + RING, mark)

    def tokens_out(self, tiles, xT, n_tiles, deps, use, cols=None):
        banks = [self.banks.next() for _ in range(n_tiles)]
        done = [None] * n_tiles
        k0 = 0
        for a, key in enumerate(tiles):
            i, w, landed = self.take(key)
            kc, n = w.shape[1], w.shape[2]

            @self.block.tensor
            def _(pe):
                for due in self.due(pe, landed, *deps):
                    pe.wait_ge(*due)
                for t in range(n_tiles):
                    if a == 0:
                        for due in self.due(pe, *banks[t].free):
                            pe.wait_ge(*due)
                    for k in range(kc):
                        ins = pe.matmul(banks[t].t[:, 0:n], xT(k0 + k, t), w[:, k, :],
                                        start=(a == 0 and k == 0), stop=(a == len(tiles) - 1 and k == kc - 1))
                    done[t] = self.pe.mark(ins.then_inc(self.pe.sem, 1))
            self.give(i, done[-1])
            k0 += kc
        for t in range(n_tiles):
            banks[t].free = [use(t, banks[t].t[:, 0:n], done[t])]

    def features_out(self, key, xT, width, deps, use, extra=None):
        i, w, landed = self.take(key)
        kc, n = w.shape[1], w.shape[2]
        mark = None
        for j in range(n // P):
            b = self.banks.next()

            @self.block.tensor
            def _(pe):
                nonlocal mark
                for due in self.due(pe, landed, *deps, *b.free):
                    pe.wait_ge(*due)
                for k in range(kc):
                    ins = pe.matmul(b.t[:, 0:width], w[:, k, j * P:(j + 1) * P], xT(k),
                                    start=(k == 0), stop=(k == kc - 1))
                mark = self.pe.mark(ins.then_inc(self.pe.sem, 1))
            if j == n // P - 1:
                self.give(i, mark)
            b.free = [use(j, b.t[:, 0:width], mark)]

    def inverse_rms(self, ctx_bufs, src, width, *deps):
        junk, st = ctx_bufs
        j, s = junk.next(), st.next()

        @self.block.scalar
        def _(act):
            for due in self.due(act, *deps, *j.free, *s.free):
                act.wait_ge(*due)
            m = self.act.mark(act.activation(j.t[:, 0:width], src, ACT.Square, accum_out=s.t[:, 0:1]).then_inc(self.act.sem, 1))
            j.free = [m]
            for due in self.due(act, m):
                act.wait_ge(*due)
            self.m1 = self.act.mark(act.activation(s.t[:, 1:2], s.t[:, 0:1], ACT.Sqrt, bias=self.eps[:, 0:1],
                                                   scale=1.0 / width).then_inc(self.act.sem, 1))

        @self.block.vector
        def _(v):
            for due in self.due(v, self.m1):
                v.wait_ge(*due)
            self.m2 = self.dve.mark(v.reciprocal(s.t[:, 2:3], s.t[:, 1:2]).then_inc(self.dve.sem, 1))
        return s, s.t[:, 2:3], self.m2

    def norm_rows(self, w, src, dst, width, *deps):
        s, inv, m = self.inverse_rms((w["junk"], w["stat"]), src, width, *deps)

        @self.block.vector
        def _(v):
            for due in self.due(v, m, *deps):
                v.wait_ge(*due)
            self.m3 = self.dve.mark(v.tensor_scalar(dst, src, inv, None, ALU.mult).then_inc(self.dve.sem, 1))
        s.free = [self.m3]
        return self.m3

    def transposed(self, pieces, use, *deps):
        b = self.banks.next()

        @self.block.tensor
        def _(pe):
            for due in self.due(pe, *deps, *b.free):
                pe.wait_ge(*due)
            for n, src in enumerate(pieces):
                w = src.shape[1]
                rows = src.shape[0]
                ins = pe.transpose(b.t[0:w, n * P:n * P + rows], src, self.ident[0:rows, 0:rows])
            self.mt = self.pe.mark(ins.then_inc(self.pe.sem, 1))
        m = self.mt
        b.free = [use(b.t, m)]
        return m, b.free[0]

    def copy(self, i, dst, src, *deps):
        if i % 2:
            @self.block.scalar
            def _(act):
                for due in self.due(act, *deps):
                    act.wait_ge(*due)
                self.mc = self.act.mark(act.activation(dst, src, ACT.Copy).then_inc(self.act.sem, 1))
        else:
            @self.block.vector
            def _(v):
                for due in self.due(v, *deps):
                    v.wait_ge(*due)
                self.mc = self.dve.mark(v.tensor_copy(dst, src).then_inc(self.dve.sem, 1))
        return self.mc

    def rope(self, w, src, dst, cos, sin, interleaved, *deps):
        h, rot = src.shape[1], src.shape[2]
        a, b = w["ropea"].next(), w["ropeb"].next()
        at = a.t[:, 0:h * rot].rearrange("p (h r) -> p h r", h=h)
        bt = b.t[:, 0:h * rot].rearrange("p (h r) -> p h r", h=h)
        cosb = cos.unsqueeze(1).broadcast_to([P, h, rot])
        sinb = sin.unsqueeze(1).broadcast_to([P, h, rot])

        def halves(x):
            if interleaved:
                return x[:, :, 0:rot:2], x[:, :, 1:rot:2]
            return x[:, :, 0:rot // 2], x[:, :, rot // 2:rot]
        (s1, s2), (b1, b2), (n1, n2) = halves(src), halves(bt), halves(sinb)

        @self.block.vector
        def _(v):
            for due in self.due(v, *deps, *a.free, *b.free):
                v.wait_ge(*due)
            self.dve.mark(v.tensor_tensor(at, src, cosb, ALU.mult).then_inc(self.dve.sem, 1))
            self.dve.mark(v.tensor_tensor(b1, s2, n1, ALU.mult).then_inc(self.dve.sem, 1))
            for due in self.due(v, self.dve.mark(v.tensor_tensor(b2, s1, n2, ALU.mult).then_inc(self.dve.sem, 1))):
                v.wait_ge(*due)
            self.mr = self.dve.mark(v.tensor_tensor(dst, at, bt, ALU.add).then_inc(self.dve.sem, 1))
        a.free = b.free = [self.mr]
        return self.mr

    def attend(self, w, q, k, values, nk, scale, bias, out, deps):
        self_ = self
        b = self.banks.next()
        kt = nk // P
        dv = values[0].shape[1]
        po = out.start_partition if not callable(out.start_partition) else out.start_partition()

        @self.block.tensor
        def _(pe):
            for due in self.due(pe, *deps, *b.free):
                pe.wait_ge(*due)
            self.ma = self.pe.mark(pe.matmul(b.t[:, 0:nk], q, k, start=True, stop=True).then_inc(self.pe.sem, 1))
        ready = self.ma
        yield
        s, st = w["prob"].next(), w["stat"].next()
        st.free, stfree = [], st.free

        @self.block.vector
        def _(v):
            for due in self.due(v, ready, *stfree, *s.free, *deps):
                v.wait_ge(*due)
            if bias is not None:
                m = self.dve.mark(v.scalar_tensor_tensor(out=s.t[:, 0:nk], in0=b.t[:, 0:nk], scalar=scale,
                                                         in1=bias, op0=ALU.mult, op1=ALU.add).then_inc(self.dve.sem, 1))
                b.free = [m]
                for due in self.due(v, m):
                    v.wait_ge(*due)
                self.ma = self.dve.mark(v.tensor_reduce(st.t[:, 0:1], s.t[:, 0:nk], AX.X, ALU.max, negate=True).then_inc(self.dve.sem, 1))
            else:
                self.ma = self.dve.mark(v.tensor_reduce(st.t[:, 0:1], b.t[:, 0:nk], AX.X, ALU.max, negate=True).then_inc(self.dve.sem, 1))
                if scale != 1.0:
                    for due in self.due(v, self.ma):
                        v.wait_ge(*due)
                    self.ma = self.dve.mark(v.tensor_scalar(st.t[:, 0:1], st.t[:, 0:1], scale, None, ALU.mult).then_inc(self.dve.sem, 1))
        top = self.ma

        @self.block.scalar
        def _(act):
            for due in self.due(act, top, *s.free):
                act.wait_ge(*due)
            src = s.t[:, 0:nk] if bias is not None else b.t[:, 0:nk]
            self.ma = self.act.mark(act.activation(s.t[:, 0:nk], src, ACT.Exp, bias=st.t[:, 0:1],
                                                   scale=1.0 if bias is not None else scale,
                                                   accum_out=st.t[:, 1:2]).then_inc(self.act.sem, 1))
        if bias is None:
            b.free = [self.ma]
        exps = self.ma
        yield

        @self.block.vector
        def _(v):
            for due in self.due(v, exps):
                v.wait_ge(*due)
            for due in self.due(v, self.dve.mark(v.reciprocal(st.t[:, 2:3], st.t[:, 1:2]).then_inc(self.dve.sem, 1))):
                v.wait_ge(*due)
            self.ma = self.dve.mark(v.tensor_scalar(s.t[:, 0:nk], s.t[:, 0:nk], st.t[:, 2:3], None, ALU.mult).then_inc(self.dve.sem, 1))
        st.free = [self.ma]
        b2 = self.banks.next()
        probs = self.ma

        @self.block.tensor
        def _(pe):
            for due in self.due(pe, probs, *b2.free):
                pe.wait_ge(*due)
            for i in range(kt):
                ins = pe.transpose(b2.t[:, i * P:(i + 1) * P], s.t[:, i * P:(i + 1) * P], self.ident)
            self.ma = self.pe.mark(ins.then_inc(self.pe.sem, 1))
        turned = s.free = [self.ma]
        yield
        pt = w["probT"].next()
        m = self.copy(1, pt.t[:, 0:nk], b2.t[:, 0:nk], *turned, *pt.free)
        b2.free = [m]
        b3 = self.banks.next()

        @self.block.tensor
        def _(pe):
            for due in self.due(pe, m, *b3.free):
                pe.wait_ge(*due)
            for i in range(kt):
                ins = pe.matmul(b3.t[po:po + dv, 0:P], values[i], pt.t[:, i * P:(i + 1) * P],
                                start=(i == 0), stop=(i == kt - 1))
            self.ma = self.pe.mark(ins.then_inc(self.pe.sem, 1))
        pt.free = [self.ma]
        summed = self.ma
        yield
        m = self.copy(0, out, b3.t[po:po + dv, 0:P], summed)
        b3.free = [m]
        w["done"].append(m)


def work_buffers(K, ctx, width=D, rows=2):
    w = {"stat": K.turn(ctx, "stat", 12, [P, 4])}
    if width:
        w["junk"] = K.turn(ctx, "junk", 1, [P, width])
    if rows:
        w["xn"] = K.turn(ctx, "xn", rows, [P, D])
    return w


def plan_first(K, l):
    A = K.A
    win = A["w_in"][l]
    for n in range(2):
        K.plan_tile(("q", l, n), win, 0, KD, COL["q"] + 512 * n, 512)
    K.plan_tile(("kv", l), win, 0, KD, COL["k"], 512)
    K.plan_tile(("qi", l), win, 0, KD, COL["qi"], 512)
    K.plan_tile(("kiwi", l), win, 0, KD, COL["ki"], 72)
    for n in range(2):
        K.plan_tile(("ga", l, n), win, 0, KD, COL["ga"] + 512 * n, 512)
        K.plan_tile(("pa", l, n), A["w_proj_attn"][l], 0, KD, 512 * n, 512)
    K.plan_tile(("dt", l), win, 0, KD, COL["dt"], SHEADS)
    for n in (4, 5, 0, 1, 2, 3):
        K.plan_tile(("xbc", l, n), win, 0, KD, COL["xbc"] + 512 * n, 512)
    for g in range(GROUPS):
        K.plan_tile(("z", l, g), win, 0, KD, COL["z"] + GW * g, GW)
    for n in range(2):
        K.plan_tile(("gs", l, n), win, 0, KD, COL["gs"] + 512 * n, 512)
        for k in range(2):
            K.plan_tile(("ps", l, n, k), A["w_proj_ssd"][l], 1024 * k, KD, 512 * n, 512)
    for n in range(2):
        K.plan_tile(("wo", l, n), A["w_out"][l], 0, KD, 512 * n, 512)
    for j in range(6):
        n = 512 if j < 5 else 256
        K.plan_tile(("fg", l, j), A["ffn_w_up"][l], 0, KD, 512 * j, n)
        K.plan_tile(("fv", l, j), A["ffn_w_up"][l], 0, KD, FFN + 512 * j, n)
    for n in range(2):
        for k, kc in enumerate((8, 8, 6)):
            K.plan_tile(("fd", l, n, k), A["ffn_w_down"][l], 1024 * k, kc, 512 * n, 512)


def rows_to_hT(K, w, x, tiles, hT, scale_cols, shift_cols, deps):
    out = []
    for t in tiles:
        xn = w["xn"].next()
        m = K.norm_rows(w, x(t), xn.t[:, :], D, *deps, *xn.free)
        for h in range(2):
            def use(bank, mk):
                for j in range(4):
                    k = 4 * h + j
                    dst, src = hT[:, k, t * P:(t + 1) * P], bank[:, j * P:(j + 1) * P]

                    @K.block.vector
                    def _(v):
                        for due in K.due(v, mk, *deps):
                            v.wait_ge(*due)
                        if shift_cols is None:
                            K.mh = K.dve.mark(v.tensor_scalar(dst, src, scale_cols(k, t), None, ALU.mult).then_inc(K.dve.sem, 1))
                        else:
                            K.mh = K.dve.mark(v.tensor_scalar(dst, src, scale_cols(k, t), shift_cols(k, t),
                                                              ALU.mult, ALU.add).then_inc(K.dve.sem, 1))
                return K.mh
            mp, md = K.transposed([xn.t[:, (4 * h + j) * P:(4 * h + j + 1) * P] for j in range(4)], use, m)
            xn.free = [mp]
            out.append(md)
    return out


def first_attention(K, l, hT, hdeps, acc):
    block = K.block
    with ExitStack() as ctx:
        w = work_buffers(K, ctx, 0, 0)
        w["ropea"], w["ropeb"] = (K.turn(ctx, n, 2, [P, 256]) for n in ("ropea", "ropeb"))
        w["prob"] = K.turn(ctx, "prob", 3, [P, SEQ])
        w["probT"] = K.turn(ctx, "probT", 3, [P, SEQ])
        tok = K.turn(ctx, "tok", 4, [P, 512])
        qT = K.sb("qT", [P, HEADS, SEQ], ctx=ctx)
        kT = K.sb("kT", [P, KVH, SEQ], ctx=ctx)
        vt = K.sb("vt", [P, TT, KVH * HD], ctx=ctx)
        qiT = K.sb("qiT", [P, IH // 2, SEQ], ctx=ctx)
        kiT = K.sb("kiT", [P, SEQ], ctx=ctx)
        wi = K.sb("wi", [P, TT, IH], ctx=ctx)
        score = K.sb("score", [P, TT, SEQ], ctx=ctx)
        left = K.sb("left", [P, TT, SEQ], ctx=ctx)
        top8 = K.sb("top8", [P, TT, 8], ctx=ctx)
        oT = K.sb("oT", [P, HEADS, SEQ], ctx=ctx)
        gate = K.sb("gate", [P, TT, 512], ctx=ctx)
        relu = K.turn(ctx, "relu", 2, [P, SEQ])
        xT = lambda k, t: hT[:, k, t * P:(t + 1) * P]
        ready = []

        def rotated(heads, cos, sin, rot, width, put, extra=None):
            def use(t, bank, mk):
                b = tok.next()
                c = K.copy(1, b.t[:, 0:bank.shape[1]], bank, mk, *b.free)
                d3 = b.t[:, 0:heads * width].rearrange("p (h d) -> p h d", h=heads)[:, :, 0:rot]
                m = K.rope(w, d3, d3, K.c(cos)[:, t, :], K.c(sin)[:, t, :], False, mk, c)
                b.free = [put(t, b.t, m)]
                return c
            return use

        def put_heads(dst, first):
            def put(t, rows, m):
                def use(bank, mk):
                    mm = K.copy(0, dst[:, first:first + 4, t * P:(t + 1) * P],
                                bank[:, 0:512].rearrange("p (h t) -> p h t", h=4), mk)
                    ready.append(mm)
                    return mm
                return K.transposed([rows[:, h * P:(h + 1) * P] for h in range(4)], use, m)[0]
            return put
        for n in range(2):
            K.tokens_out([("q", l, n)], xT, TT, hdeps, rotated(4, "cosa", "sina", HD // 4, HD, put_heads(qT, 4 * n)))

        def put_kv(t, rows, m):
            mv = K.copy(1, vt[:, t, :], rows[:, 256:512], m)

            def use(bank, mk):
                mm = K.copy(0, kT[:, :, t * P:(t + 1) * P], bank[:, 0:256].rearrange("p (h t) -> p h t", h=2), mk)
                ready.append(mm)
                return mm
            ready.append(mv)
            last = K.transposed([rows[:, h * P:(h + 1) * P] for h in range(2)], use, m)[0]
            put_kv.also = mv
            return last

        def use_kv(t, bank, mk):
            b = tok.next()
            c = K.copy(1, b.t[:, :], bank, mk, *b.free)
            d3 = b.t[:, 0:256].rearrange("p (h d) -> p h d", h=2)[:, :, 0:32]
            m = K.rope(w, d3, d3, K.c("cosa")[:, t, :], K.c("sina")[:, t, :], False, mk, c)
            last = put_kv(t, b.t, m)
            b.free = [last, put_kv.also]
            return c
        K.tokens_out([("kv", l)], xT, TT, hdeps, use_kv)
        K.tokens_out([("qi", l)], xT, TT, hdeps, rotated(8, "cosi", "sini", IDM // 4, IDM, put_heads(qiT, 0)))

        def use_ki(t, bank, mk):
            b = tok.next()
            c = K.copy(1, b.t[:, 0:64], bank[:, 0:64], mk, *b.free)
            c2 = K.copy(1, wi[:, t, :], bank[:, 64:72], mk)
            m = K.rope(w, b.t[:, 0:16].unsqueeze(1), b.t[:, 0:16].unsqueeze(1), K.c("cosi")[:, t, :],
                       K.c("sini")[:, t, :], False, mk, c)
            m2 = K.copy(0, b.t[:, 64:128], b.t[:, 0:64], m, c)

            def use(bk, mk2):
                mm = K.copy(0, kiT[:, t * P:(t + 1) * P], bk[:, 0:P], mk2)
                ready.append(mm)
                return mm
            ready.append(c2)
            b.free = [K.transposed([b.t[:, 0:128]], use, m2)[0]]

            return c2
        K.tokens_out([("kiwi", l)], xT, TT, hdeps, use_ki)

        last = [None, None]
        for t in range(TT):
            for h in range(IH):
                b = K.banks.next()
                r = relu.next()
                p0 = 64 * (h % 2)

                @block.tensor
                def _(pe):
                    for due in K.due(pe, *ready, *b.free):
                        pe.wait_ge(*due)
                    K.mx = K.pe.mark(pe.matmul(b.t[:, 0:SEQ], qiT[p0:p0 + 64, h // 2, t * P:(t + 1) * P],
                                               kiT[p0:p0 + 64, :], start=True, stop=True).then_inc(K.pe.sem, 1))

                @block.scalar
                def _(act):
                    for due in K.due(act, K.mx, *r.free):
                        act.wait_ge(*due)
                    K.my = K.act.mark(act.activation(r.t[:, :], b.t[:, 0:SEQ], ACT.Relu).then_inc(K.act.sem, 1))
                b.free = [K.my]

                @block.vector
                def _(v):
                    for due in K.due(v, K.my, last[t]):
                        v.wait_ge(*due)
                    prev = K.c("causal")[:, t, :] if h == 0 else score[:, t, :]
                    last[t] = K.dve.mark(v.scalar_tensor_tensor(out=score[:, t, :], in0=r.t[:, :],
                                                                scalar=wi[:, t, h:h + 1], in1=prev,
                                                                op0=ALU.mult, op1=ALU.add).then_inc(K.dve.sem, 1))
                r.free = [last[t]]
        for r8 in range(TOPK // 8):
            for t in range(TT):
                src = score if r8 == 0 else left

                @block.vector
                def _(v):
                    for due in K.due(v, last[t]):
                        v.wait_ge(*due)
                    for due in K.due(v, K.dve.mark(v.max(top8[:, t, :], src[:, t, :]).then_inc(K.dve.sem, 1))):
                        v.wait_ge(*due)
                    last[t] = K.dve.mark(v.match_replace(left[:, t, :], top8[:, t, :], src[:, t, :], TAKEN).then_inc(K.dve.sem, 1))
        for t in range(TT):
            @block.vector
            def _(v):
                for due in K.due(v, last[t]):
                    v.wait_ge(*due)
                m = K.dve.mark(v.tensor_scalar(score[:, t, :], left[:, t, :], TAKEN * 0.5, NEG, ALU.is_gt, ALU.mult).then_inc(K.dve.sem, 1))
                for due in K.due(v, m):
                    v.wait_ge(*due)
                last[t] = K.dve.mark(v.tensor_tensor(score[:, t, :], score[:, t, :], K.c("causal")[:, t, :], ALU.add).then_inc(K.dve.sem, 1))

        w["done"] = []
        jobs = []
        for h in range(HEADS):
            g = h // (HEADS // KVH)
            for t in range(TT):
                nk = (t + 1) * P
                jobs.append(K.attend(w, qT[:, h, t * P:(t + 1) * P], kT[:, g, 0:nk],
                                     [vt[:, i, g * HD:(g + 1) * HD] for i in range(t + 1)], nk, HD ** -0.5,
                                     score[:, t, 0:nk], oT[:, h, t * P:(t + 1) * P], [last[t], *ready]))
        pipeline(jobs, 3)
        attended = w["done"][-2:] + [w["done"][-1]]
        attended = list(w["done"])
        gfree = []
        for n in range(2):
            gm = {}

            def use_gate(t, bank, mk):
                @block.scalar
                def _(act):
                    for due in K.due(act, mk, *gfree):
                        act.wait_ge(*due)
                    K.mg = K.act.mark(act.activation(gate[:, t, :], bank, ACT.Sigmoid).then_inc(K.act.sem, 1))
                gm[t] = K.mg
                return K.mg
            K.tokens_out([("ga", l, n)], xT, TT, hdeps, use_gate)

            def use(t, bank, mk):
                @block.vector
                def _(v):
                    for due in K.due(v, mk, gm[t]):
                        v.wait_ge(*due)
                    K.mg = K.dve.mark(v.tensor_tensor(acc[:, t, 512 * n:512 * n + 512], bank,
                                                      gate[:, t, :], ALU.mult).then_inc(K.dve.sem, 1))
                return K.mg
            K.tokens_out([("pa", l, n)], lambda k, t: oT[:, k, t * P:(t + 1) * P], TT, attended, use)
            gfree = [(K.dve, K.dve.count)]
        K.settle()


def first_ssd(K, l, hT, hdeps, acc, cols, rows):
    block = K.block
    with ExitStack() as ctx:
        w = work_buffers(K, ctx, GW, 0)
        xbcT = K.sb("xbcT", [P, XCH, SEQ], ctx=ctx)
        padded = K.turn(ctx, "padded", 3, [P, SEQ + CONV - 1])
        conv = K.turn(ctx, "conv", 3, [P, SEQ])
        bT = K.sb("bT", [P, INNER // P, SEQ], ctx=ctx)
        xs = K.sb("xs", [P, TT, GW], ctx=ctx)
        xdt = K.sb("xdt", [P, TT, GW], ctx=ctx)
        zs = K.sb("zs", [P, TT, GW], ctx=ctx)
        dts = K.sb("dts", [P, TT, 8, SHEADS], ctx=ctx)
        brow = K.sb("brow", [P, STATE], ctx=ctx)
        xdec = K.sb("xdec", [P, GW], ctx=ctx)
        state = K.sb("state", [P, GW], ctx=ctx)
        cbT = K.sb("cbT", [P, TT, P], ctx=ctx)
        decay = K.turn(ctx, "decay", 1, [P, HPG, P])
        yb = K.turn(ctx, "y", 2, [P, GW])
        tmp = K.turn(ctx, "ytmp", 1, [P, GW])
        xT = lambda k, t: hT[:, k, t * P:(t + 1) * P]
        DTV, ADT, CS, NCS, ECS, W1, W2, W3 = range(8)
        small = []

        def use_dt(t, bank, mk):
            d = lambda i: dts[:, t, i, :]

            @block.vector
            def _(v):
                for due in K.due(v, mk):
                    v.wait_ge(*due)
                m = K.dve.mark(v.tensor_tensor(d(W1), bank[:, 0:SHEADS], rows("dt_bias"), ALU.add).then_inc(K.dve.sem, 1))
                for due in K.due(v, m):
                    v.wait_ge(*due)
                m = K.dve.mark(v.tensor_scalar(d(W2), d(W1), -1.0, None, ALU.mult).then_inc(K.dve.sem, 1))
                for due in K.due(v, m):
                    v.wait_ge(*due)
                K.md = K.dve.mark(v.tensor_tensor(d(W2), d(W2), d(W1), ALU.min).then_inc(K.dve.sem, 1))

            @block.scalar
            def _(act):
                for due in K.due(act, K.md):
                    act.wait_ge(*due)
                m = K.act.mark(act.activation(d(W3), d(W2), ACT.Exp).then_inc(K.act.sem, 1))
                K.me = K.act.mark(act.activation(d(NCS), rows("a_log"), ACT.Exp).then_inc(K.act.sem, 1))
                for due in K.due(act, m):
                    act.wait_ge(*due)

            @block.vector
            def _(v):
                for due in K.due(v, K.me):
                    v.wait_ge(*due)
                for due in K.due(v, K.dve.mark(v.tensor_scalar(d(CS), d(W3), 1.0, None, ALU.add).then_inc(K.dve.sem, 1))):
                    v.wait_ge(*due)
                K.mf = K.dve.mark(v.tensor_scalar(d(ECS), d(CS), -1.0, None, ALU.add).then_inc(K.dve.sem, 1))
                for due in K.due(v, K.mf):
                    v.wait_ge(*due)
                for due in K.due(v, K.dve.mark(v.tensor_tensor(d(ECS), d(ECS), d(W3), ALU.subtract).then_inc(K.dve.sem, 1))):
                    v.wait_ge(*due)
                for due in K.due(v, K.dve.mark(v.reciprocal(d(W2), d(CS)).then_inc(K.dve.sem, 1))):
                    v.wait_ge(*due)
                for due in K.due(v, K.dve.mark(v.tensor_tensor(d(ECS), d(ECS), d(W2), ALU.mult).then_inc(K.dve.sem, 1))):
                    v.wait_ge(*due)

            @block.scalar
            def _(act):
                for due in K.due(act, K.mf, (K.dve, K.dve.count)):
                    act.wait_ge(*due)
                K.me = K.act.mark(act.activation(d(W3), d(CS), ACT.Ln).then_inc(K.act.sem, 1))

            @block.vector
            def _(v):
                for due in K.due(v, K.me):
                    v.wait_ge(*due)
                for due in K.due(v, K.dve.mark(v.tensor_tensor(d(W3), d(W3), d(ECS), ALU.subtract).then_inc(K.dve.sem, 1))):
                    v.wait_ge(*due)
                for due in K.due(v, K.dve.mark(v.tensor_scalar(d(W1), d(W1), 0.0, None, ALU.max).then_inc(K.dve.sem, 1))):
                    v.wait_ge(*due)
                for due in K.due(v, K.dve.mark(v.tensor_tensor(d(DTV), d(W1), d(W3), ALU.add).then_inc(K.dve.sem, 1))):
                    v.wait_ge(*due)
                K.md = K.dve.mark(v.scalar_tensor_tensor(out=d(ADT), in0=d(DTV), scalar=-1.0, in1=d(NCS),
                                                         op0=ALU.mult, op1=ALU.mult).then_inc(K.dve.sem, 1))
            b = K.banks.next()

            @block.tensor
            def _(pe):
                for due in K.due(pe, K.md, *b.free):
                    pe.wait_ge(*due)
                pe.matmul(b.t[:, 0:SHEADS], K.c("upto"), d(ADT), start=True, stop=True)
                K.mp = K.pe.mark(pe.matmul(b.t[:, 64:64 + SHEADS], K.c("ones"), d(ADT), start=True, stop=True).then_inc(K.pe.sem, 1))

            @block.vector
            def _(v):
                for due in K.due(v, K.mp):
                    v.wait_ge(*due)
                K.dve.mark(v.tensor_scalar(d(NCS), b.t[:, 0:SHEADS], -1.0, None, ALU.mult).then_inc(K.dve.sem, 1))
                m = K.dve.mark(v.tensor_copy(d(CS), b.t[:, 0:SHEADS]).then_inc(K.dve.sem, 1))
                for due in K.due(v, m):
                    v.wait_ge(*due)
                m = K.dve.mark(v.tensor_tensor(d(W1), b.t[:, 64:64 + SHEADS], d(CS), ALU.subtract).then_inc(K.dve.sem, 1))
                K.mf = m
            b.free = [K.mf]

            @block.scalar
            def _(act):
                for due in K.due(act, K.mf):
                    act.wait_ge(*due)
                K.act.mark(act.activation(d(ECS), d(CS), ACT.Exp).then_inc(K.act.sem, 1))
                K.me = K.act.mark(act.activation(d(W2), d(W1), ACT.Exp).then_inc(K.act.sem, 1))

            @block.vector
            def _(v):
                for due in K.due(v, K.me):
                    v.wait_ge(*due)
                K.md = K.dve.mark(v.tensor_tensor(d(W2), d(W2), d(DTV), ALU.mult).then_inc(K.dve.sem, 1))
            small.extend([K.md, K.me])
            return K.md
        K.tokens_out([("dt", l)], xT, TT, hdeps, use_dt)

        convd = {}
        for n in (4, 5, 0, 1, 2, 3):
            def use(j, bank, mk):
                ch = 4 * n + j
                pd, cv = padded.next(), conv.next()

                @block.vector
                def _(v):
                    for due in K.due(v, *pd.free):
                        v.wait_ge(*due)
                    K.ms = K.dve.mark(v.memset(pd.t[:, 0:CONV - 1], 0.0).then_inc(K.dve.sem, 1))
                m = K.copy(1, pd.t[:, CONV - 1:CONV - 1 + SEQ], bank, mk, *pd.free)

                @block.vector
                def _(v):
                    for due in K.due(v, m, K.ms, *cv.free):
                        v.wait_ge(*due)
                    for i in range(CONV):
                        tap = cols("conv_w", ch * CONV + i)
                        if i == 0:
                            ins = v.tensor_scalar(cv.t[:, :], pd.t[:, 0:SEQ], tap, cols("conv_b", ch),
                                                  ALU.mult, ALU.add)
                        else:
                            ins = v.scalar_tensor_tensor(out=cv.t[:, :], in0=pd.t[:, i:i + SEQ], scalar=tap,
                                                         in1=cv.t[:, :], op0=ALU.mult, op1=ALU.add)
                        K.mv = K.dve.mark(ins.then_inc(K.dve.sem, 1))
                        for due in K.due(v, K.mv):
                            v.wait_ge(*due)
                pd.free = [K.mv]

                @block.scalar
                def _(act):
                    for due in K.due(act, K.mv):
                        act.wait_ge(*due)
                    K.ml = K.act.mark(act.activation(xbcT[:, ch, :], cv.t[:, :], ACT.Silu).then_inc(K.act.sem, 1))
                cv.free = [K.ml]
                convd[ch] = K.ml
                return m
            K.features_out(("xbc", l, n), lambda k: hT[:, k, 0:SEQ], SEQ, hdeps, use)

        prev = []
        normed = []
        for g in range(GROUPS):
            BT, CT = xbcT[:, 16 + g, :], xbcT[:, 20 + g, :]
            chs = [4 * g + j for j in range(4)]
            zm = {}

            def use_z(t, bank, mk):
                @block.scalar
                def _(act):
                    for due in K.due(act, mk, *prev):
                        act.wait_ge(*due)
                    K.mz = K.act.mark(act.activation(zs[:, t, :], bank, ACT.Silu).then_inc(K.act.sem, 1))
                zm[t] = K.mz
                return K.mz
            K.tokens_out([("z", l, g)], xT, TT, hdeps, use_z)
            hv = lambda a: a.rearrange("p (h d) -> p h d", h=HPG)
            per_head = lambda t, i: dts[:, t, i, HPG * g:HPG * (g + 1)].unsqueeze(2).broadcast_to([P, HPG, SHD])
            xm = {}
            for t in range(TT):
                def use(bank, mk):
                    m = K.copy(1, xs[:, t, :], bank[:, :], mk, *prev)

                    @block.vector
                    def _(v):
                        for due in K.due(v, m, mk, *small, *prev):
                            v.wait_ge(*due)
                        K.mv = K.dve.mark(v.tensor_tensor(hv(xdt[:, t, :]), hv(bank[:, :]), per_head(t, DTV), ALU.mult).then_inc(K.dve.sem, 1))
                    xm[t] = [m, K.mv]
                    if t == 0:
                        @block.vector
                        def _(v):
                            K.mv = K.dve.mark(v.tensor_tensor(hv(xdec[:, :]), hv(bank[:, :]), per_head(t, W2), ALU.mult).then_inc(K.dve.sem, 1))
                        xm["dec"] = K.mv
                    return K.mv
                K.transposed([xbcT[:, ch, t * P:(t + 1) * P] for ch in chs], use, *[convd[c] for c in chs], *prev)
                K.banks.bufs[(K.banks.n - 1) % 8].free.append(xm[t][0])
            def use_b(bank, mk):
                K.mb = K.copy(0, brow[:, :], bank[:, 0:P], mk, *prev)
                return K.mb
            K.transposed([BT[:, 0:P]], use_b, convd[16 + g], *prev)
            b = K.banks.next()

            @block.tensor
            def _(pe):
                for due in K.due(pe, K.mb, xm["dec"], *b.free):
                    pe.wait_ge(*due)
                K.mp = K.pe.mark(pe.matmul(b.t[:, :], brow[:, :], xdec[:, :], start=True, stop=True).then_inc(K.pe.sem, 1))
            sm = K.copy(1, state[:, :], b.t[:, :], K.mp, *prev)
            b.free = [sm]
            nprev = []
            for t in range(TT):
                tl = slice(t * P, (t + 1) * P)
                b = K.banks.next()

                @block.tensor
                def _(pe):
                    for due in K.due(pe, convd[16 + g], convd[20 + g], *b.free):
                        pe.wait_ge(*due)
                    K.mp = K.pe.mark(pe.matmul(b.t[:, 0:P], BT[:, tl], CT[:, tl], start=True, stop=True).then_inc(K.pe.sem, 1))
                cm = K.copy(0, cbT[:, t, :], b.t[:, 0:P], K.mp, *prev)
                b.free = [cm]
                dc = decay.next()
                for q in range(HPG // 4):
                    bq = K.banks.next()
                    hs = [HPG * g + 4 * q + i for i in range(4)]

                    @block.tensor
                    def _(pe):
                        for due in K.due(pe, *small, *bq.free):
                            pe.wait_ge(*due)
                        for i, h in enumerate(hs):
                            ins = pe.matmul(bq.t[:, i * P:(i + 1) * P],
                                            dts[:, t, ADT, h:h + 1].broadcast_to([P, P]), K.c("upto"),
                                            start=True, stop=True)
                        K.mp = K.pe.mark(ins.then_inc(K.pe.sem, 1))

                    @block.vector
                    def _(v):
                        for due in K.due(v, K.mp, *dc.free):
                            v.wait_ge(*due)
                        K.mv = K.dve.mark(v.tensor_tensor(
                            dc.t[:, 4 * q:4 * q + 4, :], bq.t[:, :].rearrange("p (h l) -> p h l", h=4),
                            K.c("segmask").unsqueeze(1).broadcast_to([P, 4, P]), ALU.add).then_inc(K.dve.sem, 1))
                    bq.free = [K.mv]

                    @block.scalar
                    def _(act):
                        for due in K.due(act, K.mv):
                            act.wait_ge(*due)
                        for i, h in enumerate(hs):
                            K.ml = K.act.mark(act.activation(dc.t[:, 4 * q + i, :], dc.t[:, 4 * q + i, :], ACT.Exp,
                                                             bias=dts[:, t, NCS, h:h + 1]).then_inc(K.act.sem, 1))

                    @block.vector
                    def _(v):
                        for due in K.due(v, K.ml, cm):
                            v.wait_ge(*due)
                        K.mv = K.dve.mark(v.tensor_tensor(
                            dc.t[:, 4 * q:4 * q + 4, :], dc.t[:, 4 * q:4 * q + 4, :],
                            cbT[:, t, :].unsqueeze(1).broadcast_to([P, 4, P]), ALU.mult).then_inc(K.dve.sem, 1))
                by = K.banks.next()

                @block.tensor
                def _(pe):
                    for due in K.due(pe, K.mv, *xm[t], *by.free):
                        pe.wait_ge(*due)
                    for e in range(HPG):
                        ins = pe.matmul(by.t[:, e * SHD:(e + 1) * SHD], dc.t[:, e, :],
                                        xdt[:, t, e * SHD:(e + 1) * SHD], start=True, stop=True)
                    K.mp = K.pe.mark(ins.then_inc(K.pe.sem, 1))
                dc.free = [K.mp]
                y, tm = yb.next(), tmp.next()
                ymark = K.mp
                if t == 1:
                    bo = K.banks.next()

                    @block.tensor
                    def _(pe):
                        for due in K.due(pe, sm, *bo.free):
                            pe.wait_ge(*due)
                        K.mo = K.pe.mark(pe.matmul(bo.t[:, :], CT[:, tl], state[:, :], start=True, stop=True).then_inc(K.pe.sem, 1))

                @block.vector
                def _(v):
                    for due in K.due(v, *xm[t], *tm.free, *y.free, *small):
                        v.wait_ge(*due)
                    m = K.dve.mark(v.tensor_tensor(hv(tm.t[:, :]), hv(xs[:, t, :]),
                                                   rows("d")[:, HPG * g:HPG * (g + 1)].unsqueeze(2)
                                                   .broadcast_to([P, HPG, SHD]), ALU.mult).then_inc(K.dve.sem, 1))
                    for due in K.due(v, m, ymark):
                        v.wait_ge(*due)
                    m = K.dve.mark(v.tensor_tensor(y.t[:, :], by.t[:, :], tm.t[:, :], ALU.add).then_inc(K.dve.sem, 1))
                    by.free = [m]
                    if t == 1:
                        for due in K.due(v, m, K.mo):
                            v.wait_ge(*due)
                        m = K.dve.mark(v.tensor_tensor(hv(tm.t[:, :]), hv(bo.t[:, :]), per_head(t, ECS), ALU.mult).then_inc(K.dve.sem, 1))
                        bo.free = [m]
                        for due in K.due(v, m):
                            v.wait_ge(*due)
                        m = K.dve.mark(v.tensor_tensor(y.t[:, :], y.t[:, :], tm.t[:, :], ALU.add).then_inc(K.dve.sem, 1))
                    tm.free = [m]
                    for due in K.due(v, m, zm[t]):
                        v.wait_ge(*due)
                    K.mv = K.dve.mark(v.tensor_tensor(y.t[:, :], y.t[:, :], zs[:, t, :], ALU.mult).then_inc(K.dve.sem, 1))
                m = K.norm_rows(w, y.t[:, :], y.t[:, :], GW, K.mv)

                def use(bank, mk):
                    for j in range(4):
                        @block.vector
                        def _(v):
                            for due in K.due(v, mk):
                                v.wait_ge(*due)
                            K.mv = K.dve.mark(v.tensor_scalar(bT[:, 4 * g + j, tl], bank[:, j * P:(j + 1) * P],
                                                              cols("ssd_norm", 4 * g + j), None, ALU.mult).then_inc(K.dve.sem, 1))
                    return K.mv
                mp, md = K.transposed([y.t[:, j * P:(j + 1) * P] for j in range(4)], use, m)
                y.free = [mp]
                nprev += [mp, md]
            normed += nprev
            prev = nprev + [(K.pe, K.pe.count), (K.act, K.act.count), (K.dve, K.dve.count)]
        gm = {}
        for n in range(2):
            def use_gate(t, bank, mk):
                @block.scalar
                def _(act):
                    for due in K.due(act, mk, *prev):
                        act.wait_ge(*due)
                    K.mg = K.act.mark(act.activation(zs[:, t, :], bank, ACT.Sigmoid).then_inc(K.act.sem, 1))
                gm[t] = K.mg
                return K.mg
            K.tokens_out([("gs", l, n)], xT, TT, hdeps, use_gate)

            def use(t, bank, mk):
                part = acc[:, t, 512 * n:512 * n + 512]

                @block.vector
                def _(v):
                    for due in K.due(v, mk, gm[t]):
                        v.wait_ge(*due)
                    m = K.dve.mark(v.tensor_tensor(zs[:, t, :], bank, zs[:, t, :], ALU.mult).then_inc(K.dve.sem, 1))
                    for due in K.due(v, m):
                        v.wait_ge(*due)
                    K.mg = K.dve.mark(v.tensor_tensor(part, part, zs[:, t, :], ALU.add).then_inc(K.dve.sem, 1))
                return K.mg
            K.tokens_out([("ps", l, n, k) for k in range(2)], lambda k, t: bT[:, k, t * P:(t + 1) * P], TT, normed, use)
            prev = [(K.dve, K.dve.count)]
        K.settle()


def project_residual(K, ctx, src, keys, x, use=None):
    sT = K.sb("mergedT", [P, KD, SEQ], ctx=ctx)
    ready = []
    for t in range(TT):
        for h in range(2):
            def put(bank, mk):
                m = K.copy(h, sT[:, 4 * h:4 * h + 4, t * P:(t + 1) * P],
                           bank[:, :].rearrange("p (k t) -> p k t", k=4), mk)
                ready.append(m)
                return m
            K.transposed([src[:, t, (4 * h + j) * P:(4 * h + j + 1) * P] for j in range(4)], put, (K.dve, K.dve.count))
    for n, key in enumerate(keys):
        def add(t, bank, mk):
            part = x[:, t, 512 * n:512 * n + 512]

            @K.block.vector
            def _(v):
                for due in K.due(v, mk):
                    v.wait_ge(*due)
                K.mg = K.dve.mark(v.tensor_tensor(part, part, bank, ALU.add).then_inc(K.dve.sem, 1))
            return K.mg
        K.tokens_out([key], lambda k, t: sT[:, k, t * P:(t + 1) * P], TT, ready, add)


def first_ffn(K, l, x, hT, cols):
    block = K.block
    with ExitStack() as ctx:
        w = work_buffers(K, ctx)
        gv = K.turn(ctx, "fpad", 4, [P, SEQ + FCONV - 1])
        cv = K.turn(ctx, "fconv", 3, [P, SEQ])
        gates = K.sb("gates", [P, 4, SEQ], ctx=ctx)
        actT = K.sb("actT", [P, FCH, SEQ], ctx=ctx)
        hdeps = rows_to_hT(K, w, lambda t: x[:, t, :], range(TT), hT, lambda k, t: cols("norm_ffn", k), None,
                           [(K.dve, K.dve.count)])
        done = []
        gfree = [[] for _ in range(4)]
        gm = {}

        def convolve(ch, bank, mk, dst, dfree):
            pd = gv.next()

            @block.vector
            def _(v):
                for due in K.due(v, *pd.free):
                    v.wait_ge(*due)
                K.ms = K.dve.mark(v.memset(pd.t[:, 0:FCONV - 1], 0.0).then_inc(K.dve.sem, 1))
            m = K.copy(1, pd.t[:, FCONV - 1:FCONV - 1 + SEQ], bank, mk, *pd.free)

            @block.vector
            def _(v):
                for due in K.due(v, m, K.ms, *dfree):
                    v.wait_ge(*due)
                for i in range(FCONV):
                    tap = cols("fconv_w", ch * FCONV + i)
                    if i == 0:
                        ins = v.tensor_scalar(dst, pd.t[:, 0:SEQ], tap, cols("fconv_b", ch), ALU.mult, ALU.add)
                    else:
                        ins = v.scalar_tensor_tensor(out=dst, in0=pd.t[:, i:i + SEQ], scalar=tap, in1=dst,
                                                     op0=ALU.mult, op1=ALU.add)
                    K.mv = K.dve.mark(ins.then_inc(K.dve.sem, 1))
                    for due in K.due(v, K.mv):
                        v.wait_ge(*due)
            pd.free = [K.mv]
            return m, K.mv
        for n in range(6):
            def use_gate(j, bank, mk):
                m, c = convolve(4 * n + j, bank, mk, gates[:, j, :], gfree[j])

                @block.scalar
                def _(act):
                    for due in K.due(act, c):
                        act.wait_ge(*due)
                    gm[j] = K.act.mark(act.activation(gates[:, j, :], gates[:, j, :], ACT.Silu).then_inc(K.act.sem, 1))
                return m

            def use_val(j, bank, mk):
                d = cv.next()
                m, c = convolve(FCH + 4 * n + j, bank, mk, d.t[:, :], d.free)

                @block.vector
                def _(v):
                    for due in K.due(v, c, gm[j]):
                        v.wait_ge(*due)
                    K.mv = K.dve.mark(v.tensor_tensor(actT[:, 4 * n + j, :], gates[:, j, :], d.t[:, :], ALU.mult).then_inc(K.dve.sem, 1))
                d.free = gfree[j] = [K.mv]
                done.append(K.mv)
                return m
            K.features_out(("fg", l, n), lambda k: hT[:, k, 0:SEQ], SEQ, hdeps, use_gate)
            K.features_out(("fv", l, n), lambda k: hT[:, k, 0:SEQ], SEQ, hdeps, use_val)
        for n in range(2):
            def add(t, bank, mk):
                part = x[:, t, 512 * n:512 * n + 512]

                @block.vector
                def _(v):
                    for due in K.due(v, mk):
                        v.wait_ge(*due)
                    K.mg = K.dve.mark(v.tensor_tensor(part, part, bank, ALU.add).then_inc(K.dve.sem, 1))
                return K.mg
            K.tokens_out([("fd", l, n, k) for k in range(3)], lambda k, t: actT[:, k, t * P:(t + 1) * P], TT, done, add)
        K.settle()


def first_block(K, x, hT, xdeps):
    A, block = K.A, K.block
    with ExitStack() as ctx:
        colt = K.sb("cols1", [P, 2 * PCW], ctx=ctx)
        rowt = K.sb("rows1", [P, PRW], ctx=ctx)

        @block.gpsimd
        def _(g):
            K.pm = [K.move(g, colt[:, :], A["cols1"]), K.move(g, rowt[:, :], A["rows"].partition_broadcast(P))]
        deps = list(xdeps) + K.pm
        for l in range(2):
            cols = lambda n, i: colt[:, l * PCW + PC[n] + i:l * PCW + PC[n] + i + 1]
            rows = lambda n: rowt[:, PR[n] + 32 * l:PR[n] + 32 * (l + 1)]
            with ExitStack() as mctx:
                acc = K.sb("acc", [P, TT, D], ctx=mctx)
                with ExitStack() as c2:
                    w = work_buffers(K, c2)
                    hdeps = rows_to_hT(K, w, lambda t: x[:, t, :], range(TT), hT, lambda k, t: cols("norm_mix", k),
                                       None, deps)
                    K.settle()
                first_attention(K, l, hT, hdeps, acc)
                first_ssd(K, l, hT, hdeps, acc, cols, rows)
                project_residual(K, mctx, acc, [("wo", l, 0), ("wo", l, 1)], x)
                K.settle()
            first_ffn(K, l, x, hT, cols)
            deps = [(K.dve, K.dve.count)]


def plan_ada(K, l):
    for j in range(12):
        K.plan_tile(("ada", l, j), K.A["w_ada_2"][l], 0, KD, 512 * j, 512)


def plan_second(K, l):
    A = K.A
    if l == 0:
        win = A["ab_w_in_2"][0]
        K.plan_tile(("cq",), win, 0, KD, 0, QL)
        K.plan_tile(("ckv",), win, 0, KD, QL, KVL + ROPE)
        for n in range(2):
            K.plan_tile(("qup", n), A["mla_w_q_up_2"][0], 0, QL // P, 384 * n, 384)
        for n in range(2):
            K.plan_tile(("kvup", n), A["mla_w_kv_up_2"][0], 0, KVL // P, 512 * n, 512)
        K.plan_tile(("gq",), win, 0, KD, QL + KVL + ROPE, 512)
        K.plan_tile(("gkv",), win, 0, KD, QL + KVL + ROPE + 512, 256)
        for n in range(2):
            K.plan_tile(("abo", n), A["ab_w_out_2"][0], 0, KD, 512 * n, 512)
    else:
        for n in range(6):
            K.plan_tile(("na", n), A["na_w_in_2"][0], 0, KD, 512 * n, 512)
        for n in range(2):
            K.plan_tile(("nao", n), A["na_w_out_2"][0], 0, KD, 512 * n, 512)
    n = blocks_of(l)[1]
    for b in range(n + 1):
        if b < n:
            K.plan_expert(("eg", l, b), "moe_w_gate_2", l, b, KD, DE)
            K.plan_expert(("eu", l, b), "moe_w_up_2", l, b, KD, DE)
        if b > 0:
            K.plan_expert(("ed", l, b - 1), "moe_w_down_2", l, b - 1, DE // P, D)


def blocks_of(l):
    tiles = NT2 if l == 0 else TT
    return tiles, EXPERTS + (2 * tiles * P) // (CAP + 1)


def modulation(K, l, ctx, cols, modrows):
    block = K.block
    mod = K.sb("mod", [P, 48, 2], ctx=ctx)
    gain = K.sb("gain", [P, KD, 2], ctx=ctx)
    with ExitStack() as c2:
        sc = K.sb("silu_c", [P, KD, 2], ctx=c2)
        packed = K.sb("packed", [P, 64], ctx=c2)
        row = K.sb("modrow", [64, P], ctx=c2)

        @block.scalar
        def _(act):
            for due in K.due(act, *K.settled):
                act.wait_ge(*due)
            K.ml = K.act.mark(act.activation(sc[:, :, :], cols("c", 0, 16).rearrange("p (k s) -> p k s", s=2), ACT.Silu).then_inc(K.act.sem, 1))
        b = K.banks.next()
        for j in range(12):
            i, w, landed = K.take(("ada", l, j))

            @block.tensor
            def _(pe):
                for due in K.due(pe, landed, K.ml, *b.free):
                    pe.wait_ge(*due)
                for q in range(4):
                    for k in range(KD):
                        at = 2 * (4 * j + q)
                        ins = pe.matmul(b.t[:, at:at + 2], w[:, k, q * P:(q + 1) * P], sc[:, k, :],
                                        start=(k == 0), stop=(k == KD - 1))
                K.mp = K.pe.mark(ins.then_inc(K.pe.sem, 1))
            K.give(i, K.mp)

        @block.vector
        def _(v):
            for due in K.due(v, K.mp, *K.settled):
                v.wait_ge(*due)
            m = K.dve.mark(v.tensor_tensor(mod[:, :, :], b.t[:, 0:96].rearrange("p (j s) -> p j s", s=2),
                                           cols("b_ada", 48 * l, 48).unsqueeze(2).broadcast_to([P, 48, 2]), ALU.add).then_inc(K.dve.sem, 1))
            b.free = [m]
            for due in K.due(v, m):
                v.wait_ge(*due)
            pk = packed[:, :].rearrange("p (a s k) -> p a s k", a=4, s=2)
            for a in range(4):
                K.mv = K.dve.mark(v.tensor_copy(pk[:, a, :, :],
                                                mod[:, 8 * (a + 2):8 * (a + 3), :].rearrange("p k s -> p s k")).then_inc(K.dve.sem, 1))
            m = K.dve.mark(v.tensor_scalar(gain[:, :, :], mod[:, 8:16, :], 1.0, None, ALU.add).then_inc(K.dve.sem, 1))
            for due in K.due(v, m):
                v.wait_ge(*due)
            K.mg = K.dve.mark(v.tensor_tensor(gain[:, :, :], gain[:, :, :],
                                              cols("norm_mix", 8 * l, 8).unsqueeze(2).broadcast_to([P, KD, 2]), ALU.mult).then_inc(K.dve.sem, 1))

        def use(bank, mk):
            K.mr = K.copy(0, row[:, :], bank[0:64, 0:P], mk)
            return K.mr
        K.transposed([packed[:, :]], use, K.mv)

        @block.gpsimd
        def _(g):
            K.ms = K.move(g, modrows[l], row[:, :], K.mr)
        K.settle()
    return mod, gain, K.ms


MG1, MSH2, MSC2, MG2 = range(4)


def add_gated(K, ctx, x_of, keys, xT, tiles, rows, deps):
    tmp = K.turn(ctx, "gated", 2, [P, 512])
    for n, key in enumerate(keys):
        def use(i, bank, mk):
            t = tiles[i]
            tm = tmp.next()
            part = x_of(t)[:, 512 * n:512 * n + 512]

            @K.block.vector
            def _(v):
                for due in K.due(v, mk, *tm.free, *deps):
                    v.wait_ge(*due)
                m = K.dve.mark(v.tensor_tensor(tm.t[:, :], bank, rows(t)[:, 512 * n:512 * n + 512], ALU.mult).then_inc(K.dve.sem, 1))
                for due in K.due(v, m):
                    v.wait_ge(*due)
                K.mg = K.dve.mark(v.tensor_tensor(part, part, tm.t[:, :], ALU.add).then_inc(K.dve.sem, 1))
            tm.free = [K.mg]
            return K.mg
        K.tokens_out([key], lambda k, i: xT(k, tiles[i]), len(tiles), deps, use)


def latent_attention(K, ctx0, hT, hdeps, oT, cols):
    block = K.block
    with ExitStack() as ctx:
        w = work_buffers(K, ctx, 384, 0)
        w["ropea"], w["ropeb"] = (K.turn(ctx, n, 1, [P, 128]) for n in ("ropea", "ropeb"))
        w["prob"] = K.turn(ctx, "prob", 3, [P, 512])
        w["probT"] = K.turn(ctx, "probT", 2, [P, 512])
        tok = K.turn(ctx, "tok", 3, [P, 384])
        cqT = K.sb("cqT", [P, QL // P, NT2 * P], ctx=ctx)
        ckvT = K.sb("ckvT", [P, KVL // P, NT2 * P], ctx=ctx)
        kr = K.sb("kr", [P, NT2, ROPE], ctx=ctx)
        qT = K.sb("qaT", [NOPE + ROPE, HA, NT2 * P], ctx=ctx)
        kT = K.sb("kaT", [NOPE + ROPE, HA, NT2 * P], ctx=ctx)
        va = K.sb("va", [P, NT2, HA, VA], ctx=ctx)
        xT = lambda k, t: hT[:, k, t * P:(t + 1) * P]
        ready, low = [], []

        def use_low(width, norm, dst):
            def use(t, bank, mk):
                b = tok.next()
                c = K.copy(1, b.t[:, 0:bank.shape[1]], bank, mk, *b.free)
                extra = []
                if bank.shape[1] > width:
                    if t >= 2:
                        src = b.t[:, width:width + ROPE].unsqueeze(1)
                        m = K.rope(w, src, kr[:, t:t + 1, :], K.c("cos2a")[:, t - 2, :], K.c("sin2a")[:, t - 2, :],
                                   True, c)
                    else:
                        m = K.copy(0, kr[:, t, :], b.t[:, width:width + ROPE], c)
                    extra.append(m)
                    low.append(m)
                m = K.norm_rows(w, b.t[:, 0:width], b.t[:, 0:width], width, c)

                def put(bk, mk2):
                    for j in range(width // P):
                        @block.vector
                        def _(v):
                            for due in K.due(v, mk2):
                                v.wait_ge(*due)
                            K.mv = K.dve.mark(v.tensor_scalar(dst[:, j, t * P:(t + 1) * P], bk[:, j * P:(j + 1) * P],
                                                              cols(norm, j, 1), None, ALU.mult).then_inc(K.dve.sem, 1))
                    low.append(K.mv)
                    return K.mv
                b.free = [K.transposed([b.t[:, j * P:(j + 1) * P] for j in range(width // P)], put, m)[0], *extra]
                return c
            return use
        K.tokens_out([("cq",)], xT, NT2, hdeps, use_low(QL, "q_norm", cqT))
        K.tokens_out([("ckv",)], xT, NT2, hdeps, use_low(KVL, "kv_norm", ckvT))

        def put_heads(dst, n, t, rows, *ms):
            def put(bank, mk):
                mm = K.copy(1, dst[:, 4 * n:4 * n + 4, t * P:(t + 1) * P],
                            bank[0:96, :].rearrange("p (h t) -> p h t", h=4), mk)
                ready.append(mm)
                return mm
            return K.transposed([rows[:, 96 * h:96 * h + 96] for h in range(4)], put, *ms)[0]
        for n in range(2):
            def use_q(t, bank, mk):
                b = tok.next()
                m = c = K.copy(1, b.t[:, :], bank, mk, *b.free)
                if t >= 2:
                    part = b.t[:, :].rearrange("p (h d) -> p h d", h=4)[:, :, NOPE:96]
                    m = K.rope(w, part, part, K.c("cos2a")[:, t - 2, :], K.c("sin2a")[:, t - 2, :], True, c)
                b.free = [put_heads(qT, n, t, b.t, m)]
                return c
            K.tokens_out([("qup", n)], lambda k, t: cqT[:, k, t * P:(t + 1) * P], NT2, low, use_q)
        for n in range(2):
            def use_kv(t, bank, mk):
                b = tok.next()
                rows = b.t[:, :].rearrange("p (h d) -> p h d", h=4)
                src = bank.rearrange("p (h d) -> p h d", h=4)
                c = K.copy(1, rows[:, :, 0:NOPE], src[:, :, 0:NOPE], mk, *b.free)
                mv = K.copy(1, va[:, t, 4 * n:4 * n + 4, :], src[:, :, NOPE:P], mk)
                m = K.copy(0, rows[:, :, NOPE:96], kr[:, t:t + 1, :].broadcast_to([P, 4, ROPE]), *low, *b.free)
                ready.append(mv)
                b.free = [put_heads(kT, n, t, b.t, m, c)]
                return mv
            K.tokens_out([("kvup", n)], lambda k, t: ckvT[:, k, t * P:(t + 1) * P], NT2, low, use_kv)
        w["done"] = []
        jobs = []
        for h in range(HA):
            for t in range(NT2):
                nk = 256 if t < 2 else 512
                p0 = 64 * (h % 2)
                jobs.append(K.attend(w, qT[:, h, t * P:(t + 1) * P], kT[:, h, 0:nk],
                                     [va[:, i, h, :] for i in range(nk // P)], nk, (NOPE + ROPE) ** -0.5, None,
                                     oT[p0:p0 + 64, h // 2, t * P:(t + 1) * P], ready))
        pipeline(jobs, 3)
        K.settle()


def grouped_attention(K, hT, hdeps, oT, rowt):
    block = K.block
    with ExitStack() as ctx:
        w = work_buffers(K, ctx, 0, 0)
        w["ropea"], w["ropeb"] = (K.turn(ctx, n, 1, [P, 512]) for n in ("ropea", "ropeb"))
        w["prob"] = K.turn(ctx, "prob", 3, [P, 512])
        w["probT"] = K.turn(ctx, "probT", 2, [P, 512])
        sq = K.sb("sq", [P, 512], ctx=ctx)
        sm = K.sb("sm", [P, 16], ctx=ctx)
        tok = K.turn(ctx, "tok", 3, [P, 512])
        kk = K.turn(ctx, "kk", 2, [P, 2, 2, HD2])
        qT = K.sb("qbT", [P, HB // 2, NT2 * P], ctx=ctx)
        kT = K.sb("kbT", [P, KVB, NT2 * P], ctx=ctx)
        vb = K.sb("vb", [P, NT2, KVB, HD2], ctx=ctx)
        xT = lambda k, t: hT[:, k, t * P:(t + 1) * P]
        ready = []
        state = {"free": []}

        def head_norm(rows, heads, norm, t, *deps):
            n = heads * HD2
            s3 = sq[:, 0:n].rearrange("p (h d) -> p h d", h=heads)

            @block.vector
            def _(v):
                for due in K.due(v, *deps, *state["free"]):
                    v.wait_ge(*due)
                m = K.dve.mark(v.tensor_tensor(s3, rows, rows, ALU.mult).then_inc(K.dve.sem, 1))
                for due in K.due(v, m):
                    v.wait_ge(*due)
                K.mv = K.dve.mark(v.tensor_reduce(sm[:, 0:heads], s3, AX.X, ALU.add).then_inc(K.dve.sem, 1))

            @block.scalar
            def _(act):
                for due in K.due(act, K.mv):
                    act.wait_ge(*due)
                K.ml = K.act.mark(act.activation(sm[:, 8:8 + heads], sm[:, 0:heads], ACT.Sqrt, bias=K.eps[:, 0:1],
                                                 scale=1.0 / HD2).then_inc(K.act.sem, 1))

            @block.vector
            def _(v):
                for due in K.due(v, K.ml):
                    v.wait_ge(*due)
                m = K.dve.mark(v.reciprocal(sm[:, 0:heads], sm[:, 8:8 + heads]).then_inc(K.dve.sem, 1))
                for due in K.due(v, m):
                    v.wait_ge(*due)
                m = K.dve.mark(v.tensor_tensor(rows, rows, sm[:, 0:heads].unsqueeze(2).broadcast_to([P, heads, HD2]),
                                               ALU.mult).then_inc(K.dve.sem, 1))
                for due in K.due(v, m):
                    v.wait_ge(*due)
                K.mv = K.dve.mark(v.tensor_tensor(
                    rows, rows, rowt[:, PR[norm]:PR[norm] + HD2].unsqueeze(1).broadcast_to([P, heads, HD2]), ALU.mult).then_inc(K.dve.sem, 1))
            state["free"] = [K.mv]
            m = K.mv
            if t >= 2:
                m = K.rope(w, rows, rows, K.c("cos2b")[:, t - 2, :], K.c("sin2b")[:, t - 2, :], True, m)
            return m

        def use_q(t, bank, mk):
            b = tok.next()
            c = K.copy(1, b.t[:, :], bank, mk, *b.free)
            m = head_norm(b.t[:, :].rearrange("p (h d) -> p h d", h=HB), HB, "gq_norm", t, c)

            def put(bk, mk2):
                mm = K.copy(0, qT[:, :, t * P:(t + 1) * P], bk[:, :].rearrange("p (h t) -> p h t", h=4), mk2)
                ready.append(mm)
                return mm
            b.free = [K.transposed([b.t[:, j * P:(j + 1) * P] for j in range(4)], put, m)[0]]
            return c
        K.tokens_out([("gq",)], xT, NT2, hdeps, use_q)

        def use_kv(t, bank, mk):
            b, kd = tok.next(), kk.next()
            c = K.copy(1, b.t[:, 0:256], bank, mk, *b.free)
            mv = K.copy(1, vb[:, t, :, :], b.t[:, P:2 * P].rearrange("p (g d) -> p g d", g=2), c)
            m = head_norm(b.t[:, 0:P].rearrange("p (h d) -> p h d", h=KVB), KVB, "gk_norm", t, c)
            m2 = K.copy(0, kd.t[:, :, :, :],
                        b.t[:, 0:P].rearrange("p (g d) -> p g d", g=2).unsqueeze(2).broadcast_to([P, 2, 2, HD2]),
                        m, *kd.free)

            def put(bk, mk2):
                mm = K.copy(0, kT[:, :, t * P:(t + 1) * P], bk[:, 0:256].rearrange("p (h t) -> p h t", h=2), mk2)
                ready.append(mm)
                return mm
            ready.append(mv)
            b.free = [m2, mv]
            kd.free = [K.transposed([kd.t[:, g, :, :].rearrange("p a d -> p (a d)") for g in range(2)], put, m2)[0]]
            return c
        K.tokens_out([("gkv",)], xT, NT2, hdeps, use_kv)
        w["done"] = []
        jobs = []
        for h in range(HB):
            for t in range(NT2):
                nk = 256 if t < 2 else 512
                p0, g = 64 * (h % 2), h // (HB // KVB)
                jobs.append(K.attend(w, qT[p0:p0 + 64, h // 2, t * P:(t + 1) * P], kT[p0:p0 + 64, g, 0:nk],
                                     [vb[:, i, g, :] for i in range(nk // P)], nk, HD2 ** -0.5, None,
                                     oT[p0:p0 + 64, 4 + h // 2, t * P:(t + 1) * P], ready))
        pipeline(jobs, 3)
        K.settle()


SPAN_R = 2 * (SEQ // GRID_W) - 1


def spread_bias(K):
    rows_n = SEQ // GRID_W
    span_c = 2 * WIN_C - 1
    K.windows = K.nc.dram_tensor("bias_windows", [GRID_W, HC, SPAN_R, GRID_W], F32).ap()

    @K.block.gpsimd
    def _(g):
        K.spread = []
        for c in range(GRID_W):
            src = bass.AP(K.A["rpb_2"].tensor, (WIN_R - rows_n) * span_c + WIN_C - 1 - c,
                          [[(2 * WIN_R - 1) * span_c, HC], [span_c, SPAN_R], [1, GRID_W]])
            K.spread.append(K.move(g, K.windows[c], src))


def neighbourhood_attention(K, hT, hdeps, oT):
    block = K.block
    rows_n = SEQ // GRID_W
    with ExitStack() as ctx:
        w = work_buffers(K, ctx, 0, 0)
        w["prob"] = K.turn(ctx, "prob", 3, [P, 512])
        w["probT"] = K.turn(ctx, "probT", 2, [P, 512])
        tok = K.turn(ctx, "tok", 3, [P, 512])
        bias = K.turn(ctx, "bias", 3, [P, TT, 512])
        qT = K.sb("qnT", [P, HC // 2, SEQ], ctx=ctx)
        kT = K.sb("knT", [P, HC // 2, NT2 * P], ctx=ctx)
        vn = K.sb("vn", [P, NT2, HC * HD2], ctx=ctx)
        ready = []
        for b in bias.bufs:
            @block.vector
            def _(v):
                b.free = [K.dve.mark(v.memset(b.t[:, :, 0:SEQ], 0.0).then_inc(K.dve.sem, 1))]

        def turned(dst, n):
            def use(i, bank, mk):
                b = tok.next()
                c = K.copy(1, b.t[:, :], bank, mk, *b.free)

                def put(bk, mk2):
                    mm = K.copy(0, dst[:, 4 * n:4 * n + 4, i * P:(i + 1) * P],
                                bk[:, :].rearrange("p (h t) -> p h t", h=4), mk2)
                    ready.append(mm)
                    return mm
                b.free = [K.transposed([b.t[:, j * P:(j + 1) * P] for j in range(4)], put, c)[0]]
                return c
            return use
        for n in range(2):
            K.tokens_out([("na", n)], lambda k, t: hT[:, k, (t + 2) * P:(t + 3) * P], TT, hdeps, turned(qT, n))
        for n in range(2):
            K.tokens_out([("na", 2 + n)], lambda k, t: hT[:, k, t * P:(t + 1) * P], NT2, hdeps, turned(kT, n))
        for n in range(2):
            def use_v(t, bank, mk):
                m = K.copy(1, vn[:, t, 512 * n:512 * n + 512], bank, mk)
                ready.append(m)
                return m
            K.tokens_out([("na", 4 + n)], lambda k, t: hT[:, k, t * P:(t + 1) * P], NT2, hdeps, use_v)
        w["done"] = []

        def head(h):
            b = bias.next()
            marks = []

            @block.gpsimd
            def _(g):
                for r in range(rows_n):
                    src = K.windows[:, h, rows_n - 1 - r:2 * rows_n - 1 - r, :]
                    q0 = GRID_W * (r % 2)
                    dst = b.t[q0:q0 + GRID_W, r // 2, SEQ:2 * SEQ].rearrange("p (a b) -> p a b", a=rows_n)
                    marks.append(K.move(g, dst, src, *b.free, *K.spread))

            @block.vector
            def _(v):
                for due in K.due(v, *marks):
                    v.wait_ge(*due)
                K.mv = K.dve.mark(v.tensor_tensor(b.t[:, :, SEQ:2 * SEQ], b.t[:, :, SEQ:2 * SEQ], K.c("window"), ALU.add).then_inc(K.dve.sem, 1))
            m = K.mv
            p0 = 64 * (h % 2)
            jobs = [K.attend(w, qT[p0:p0 + 64, h // 2, t * P:(t + 1) * P], kT[p0:p0 + 64, h // 2, :],
                             [vn[:, i, h * HD2:(h + 1) * HD2] for i in range(NT2)], 512, HD2 ** -0.5, b.t[:, t, :],
                             oT[p0:p0 + 64, h // 2, t * P:(t + 1) * P], [*ready, m]) for t in range(TT)]
            while jobs:
                for j in list(jobs):
                    try:
                        next(j)
                    except StopIteration:
                        jobs.remove(j)
                yield
            b.free = [(K.dve, K.dve.count)]
        pipeline([head(h) for h in range(HC)], 2)
        K.settle()


def moe(K, l, streams, hT, modrows, rowt, dram):
    block, A = K.block, K.A
    tiles, nb = blocks_of(l)
    nx = nb - EXPERTS
    deep = tiles * P // CAP
    ids_dram, h_dram, y_dram = dram
    row_of = {}
    x_of = lambda t: streams[t // 2][0][:, t % 2, :] if len(streams) == 2 else streams[0][0][:, t, :]
    s_of = lambda t: streams[t // 2][1] if len(streams) == 2 else streams[0][1]

    def broadcast_row(g, dst, a, s, *deps):
        src = modrows[l].rearrange("(a s k) p -> a s (k p)", a=4, s=2)[a, s]
        return K.move(g, dst, src.partition_broadcast(P), *deps)

    with ExitStack() as octx:
        wts = K.sb("wts", [P, NT2, 2], ctx=octx)
        yrow = K.sb("yrow", [P, NT2, 2], U32, ctx=octx)
        xid = K.sb("xid", [P, max(nx, 1)], U32, ctx=octx)
        tokidx = K.sb("tokidx", [CAP, nb], U32, ctx=octx)
        with ExitStack() as ctx:
            w = work_buffers(K, ctx, D, 2)
            gain = K.sb("gain2", [P, 2, D], ctx=ctx)
            shift = K.sb("shift2", [P, 2, D], ctx=ctx)
            nrow = K.sb("nrow", [P, D], ctx=ctx)
            router = K.sb("router", [P, KD, 36], ctx=ctx)
            lg = K.turn(ctx, "lg", 2, [P, 36])
            sm = K.turn(ctx, "rsm", 2, [P, 8, 8])
            ix = K.turn(ctx, "rix", 2, [P, 2, 8], U32)
            oh = K.sb("onehot", [P, NT2, 2, EXPERTS], ctx=ctx)
            both = K.sb("both", [P, NT2, EXPERTS], ctx=ctx)
            ek = K.sb("ek", [P, NT2, 2], ctx=ctx)
            cnt = K.sb("cnt", [P, 6, EXPERTS], ctx=ctx)
            cmp = K.sb("cmp", [P, max(nx, 1), EXPERTS], ctx=ctx)
            pos = K.turn(ctx, "pos", 2, [P, 12])
            scr = K.sb("scr", [P, 2, EXPERTS], ctx=ctx)
            tokpos = K.sb("tokpos", [P, NT2, 2], U32, ctx=ctx)
            tokid = K.sb("tokid", [P, NT2], U32, ctx=ctx)
            zero = K.sb("zero", [P, nb * CAP // P], U32, ctx=ctx)
            xidf = K.sb("xidf", [P, max(nx, 1)], ctx=ctx)

            @block.vector
            def _(v):
                for due in K.due(v, *K.settled):
                    v.wait_ge(*due)
                K.dve.mark(v.memset(zero[:, :], 0).then_inc(K.dve.sem, 1))
                K.mv = K.dve.mark(v.tensor_copy(tokid[:, :], K.c("token")).then_inc(K.dve.sem, 1))
            early = K.mv
            lm = []

            @block.gpsimd
            def _(g):
                for _, s in streams:
                    lm.append(broadcast_row(g, gain[:, s, :], MSC2, s, *K.settled))
                    lm.append(broadcast_row(g, shift[:, s, :], MSH2, s))
                lm.append(K.move(g, nrow[:, :], A["norm_ffn_2"][l].partition_broadcast(P)))
                lm.append(K.move(g, router[:, :, :], A["router_2"][l].rearrange("(k p) n -> p k n", p=P)))
                K.mz = K.move(g, ids_dram.rearrange("(p n) a -> p (n a)", p=P), zero[:, :], early)

            @block.vector
            def _(v):
                for due in K.due(v, *lm):
                    v.wait_ge(*due)
                for _, s in streams:
                    K.mv = K.dve.mark(v.scalar_tensor_tensor(out=gain[:, s, :], in0=gain[:, s, :], scalar=1.0,
                                                             in1=nrow[:, :], op0=ALU.add, op1=ALU.mult).then_inc(K.dve.sem, 1))
            gm = K.mv
            hstored = []
            onehots = []
            for t in range(tiles):
                s = s_of(t)
                xn = w["xn"].next()
                m = K.norm_rows(w, x_of(t), xn.t[:, :], D, *K.settled, *xn.free)

                @block.vector
                def _(v):
                    for due in K.due(v, m, gm):
                        v.wait_ge(*due)
                    m2 = K.dve.mark(v.tensor_tensor(xn.t[:, :], xn.t[:, :], gain[:, s, :], ALU.mult).then_inc(K.dve.sem, 1))
                    for due in K.due(v, m2):
                        v.wait_ge(*due)
                    K.mv = K.dve.mark(v.tensor_tensor(xn.t[:, :], xn.t[:, :], shift[:, s, :], ALU.add).then_inc(K.dve.sem, 1))
                m = K.mv

                @block.gpsimd
                def _(g):
                    hstored.append(K.move(g, h_dram[t * P:(t + 1) * P, :], xn.t[:, :], m))
                hm = []
                for hh in range(2):
                    def put(bank, mk):
                        mm = K.copy(1, hT[:, 4 * hh:4 * hh + 4, t * P:(t + 1) * P],
                                    bank[:, :].rearrange("p (k t) -> p k t", k=4), mk, *K.settled)
                        hm.append(mm)
                        return mm
                    mp, _ = K.transposed([xn.t[:, (4 * hh + j) * P:(4 * hh + j + 1) * P] for j in range(4)], put, m)
                xn.free = [mp, hstored[-1]]
                b, L, S, I = K.banks.next(), lg.next(), sm.next(), ix.next()

                @block.tensor
                def _(pe):
                    for due in K.due(pe, *hm, *lm, *b.free):
                        pe.wait_ge(*due)
                    for k in range(KD):
                        ins = pe.matmul(b.t[:, 0:36], hT[:, k, t * P:(t + 1) * P], router[:, k, :],
                                        start=(k == 0), stop=(k == KD - 1))
                    K.mp = K.pe.mark(ins.then_inc(K.pe.sem, 1))
                G8, M8, SEL, V8, E4, OHG, F = (S.t[:, i, :] for i in range(7))

                @block.vector
                def _(v):
                    for due in K.due(v, K.mp, *L.free, *S.free, *I.free):
                        v.wait_ge(*due)
                    K.dve.mark(v.memset(G8, NEG).then_inc(K.dve.sem, 1))
                    m = K.dve.mark(v.tensor_tensor(L.t[:, :], b.t[:, 0:36],
                                                   rowt[:, PR["b_router"] + 36 * l:PR["b_router"] + 36 * l + 36], ALU.add).then_inc(K.dve.sem, 1))
                    b.free = [m]
                    for due in K.due(v, m):
                        v.wait_ge(*due)
                    for due in K.due(v, K.dve.mark(v.tensor_copy(G8[:, 0:NGR], L.t[:, 0:NGR]).then_inc(K.dve.sem, 1))):
                        v.wait_ge(*due)
                    for due in K.due(v, K.dve.mark(v.max(M8, G8).then_inc(K.dve.sem, 1))):
                        v.wait_ge(*due)
                    for due in K.due(v, K.dve.mark(v.max_index(I.t[:, 0, :], M8, G8).then_inc(K.dve.sem, 1))):
                        v.wait_ge(*due)
                    K.dve.mark(v.tensor_scalar(F[:, 0:1], M8[:, 0:1], -1.0, None, ALU.mult).then_inc(K.dve.sem, 1))
                    for due in K.due(v, K.dve.mark(v.tensor_copy(F[:, 1:2], I.t[:, 0, 0:1]).then_inc(K.dve.sem, 1))):
                        v.wait_ge(*due)
                    for due in K.due(v, K.dve.mark(v.tensor_scalar(OHG[:, 0:NGR], K.c("iota")[:, 0:NGR], F[:, 1:2], None,
                                                         ALU.is_equal).then_inc(K.dve.sem, 1))):
                        v.wait_ge(*due)
                    m = K.dve.mark(v.tensor_scalar(SEL, L.t[:, 4:12], OHG[:, 0:1], None, ALU.mult).then_inc(K.dve.sem, 1))
                    for j in range(1, NGR):
                        for due in K.due(v, m):
                            v.wait_ge(*due)
                        m = K.dve.mark(v.scalar_tensor_tensor(out=SEL, in0=L.t[:, 4 + 8 * j:12 + 8 * j],
                                                              scalar=OHG[:, j:j + 1], in1=SEL, op0=ALU.mult,
                                                              op1=ALU.add).then_inc(K.dve.sem, 1))
                    for due in K.due(v, m):
                        v.wait_ge(*due)
                    for due in K.due(v, K.dve.mark(v.max(V8, SEL).then_inc(K.dve.sem, 1))):
                        v.wait_ge(*due)
                    for due in K.due(v, K.dve.mark(v.max_index(I.t[:, 1, :], V8, SEL).then_inc(K.dve.sem, 1))):
                        v.wait_ge(*due)
                    K.dve.mark(v.tensor_tensor(F[:, 2:3], V8[:, 1:2], V8[:, 0:1], ALU.subtract).then_inc(K.dve.sem, 1))
                    for due in K.due(v, K.dve.mark(v.tensor_copy(ek[:, t, :], I.t[:, 1, 0:2]).then_inc(K.dve.sem, 1))):
                        v.wait_ge(*due)
                    m = K.dve.mark(v.scalar_tensor_tensor(out=ek[:, t, :], in0=F[:, 1:2].broadcast_to([P, 2]),
                                                          scalar=float(EG), in1=ek[:, t, :], op0=ALU.mult, op1=ALU.add).then_inc(K.dve.sem, 1))
                    for due in K.due(v, m):
                        v.wait_ge(*due)
                    for k in range(2):
                        m = K.dve.mark(v.tensor_scalar(oh[:, t, k, :], K.c("iota"), ek[:, t, k:k + 1], None,
                                                       ALU.is_equal).then_inc(K.dve.sem, 1))
                    for due in K.due(v, m):
                        v.wait_ge(*due)
                    K.mv = K.dve.mark(v.tensor_tensor(both[:, t, :], oh[:, t, 0, :], oh[:, t, 1, :], ALU.add).then_inc(K.dve.sem, 1))
                onehots.append(K.mv)

                @block.scalar
                def _(act):
                    for due in K.due(act, K.mv):
                        act.wait_ge(*due)
                    K.act.mark(act.activation(E4[:, 0:NGR], L.t[:, 0:NGR], ACT.Exp, bias=F[:, 0:1],
                                              accum_out=F[:, 3:4]).then_inc(K.act.sem, 1))
                    K.ml = K.act.mark(act.activation(F[:, 4:5], F[:, 2:3], ACT.Exp).then_inc(K.act.sem, 1))

                @block.vector
                def _(v):
                    for due in K.due(v, K.ml):
                        v.wait_ge(*due)
                    for due in K.due(v, K.dve.mark(v.scalar_tensor_tensor(out=F[:, 5:6], in0=F[:, 4:5], scalar=1.0,
                                                                in1=F[:, 3:4], op0=ALU.add, op1=ALU.mult).then_inc(K.dve.sem, 1))):
                        v.wait_ge(*due)
                    for due in K.due(v, K.dve.mark(v.reciprocal(wts[:, t, 0:1], F[:, 5:6]).then_inc(K.dve.sem, 1))):
                        v.wait_ge(*due)
                    K.mw = K.dve.mark(v.tensor_tensor(wts[:, t, 1:2], wts[:, t, 0:1], F[:, 4:5], ALU.mult).then_inc(K.dve.sem, 1))
                L.free = S.free = I.free = [K.mw, K.ml]
            b = K.banks.next()

            @block.tensor
            def _(pe):
                for due in K.due(pe, *onehots, *b.free):
                    pe.wait_ge(*due)
                for t in range(tiles):
                    ins = pe.matmul(b.t[:, 0:EXPERTS], K.c("ones"), both[:, t, :], start=(t == 0), stop=(t == tiles - 1))
                K.mp = K.pe.mark(ins.then_inc(K.pe.sem, 1))
            MORE, INCL, EXCL, ZERO, CNT = (cnt[:, i, :] for i in range(5))

            @block.vector
            def _(v):
                for due in K.due(v, K.mp):
                    v.wait_ge(*due)
                m = K.dve.mark(v.tensor_copy(CNT, b.t[:, 0:EXPERTS]).then_inc(K.dve.sem, 1))
                b.free = [m]
                for due in K.due(v, m):
                    v.wait_ge(*due)
                K.dve.mark(v.memset(ZERO, 0.0).then_inc(K.dve.sem, 1))
                m = K.dve.mark(v.tensor_scalar(MORE, CNT, float(CAP), None, ALU.is_gt).then_inc(K.dve.sem, 1))
                for j in range(2, deep):
                    for due in K.due(v, m):
                        v.wait_ge(*due)
                    m = K.dve.mark(v.scalar_tensor_tensor(out=MORE, in0=CNT, scalar=float(j * CAP), in1=MORE,
                                                          op0=ALU.is_gt, op1=ALU.add).then_inc(K.dve.sem, 1))
                for due in K.due(v, m):
                    v.wait_ge(*due)
                for due in K.due(v, K.dve.mark(v.tensor_tensor_scan(INCL, MORE, ZERO, 0.0, ALU.add, ALU.add).then_inc(K.dve.sem, 1))):
                    v.wait_ge(*due)
                m = K.dve.mark(v.tensor_tensor(EXCL, INCL, MORE, ALU.subtract).then_inc(K.dve.sem, 1))
                K.base = m
                m = K.dve.mark(v.tensor_tensor(cmp[:, :, :], INCL.unsqueeze(1).broadcast_to([P, nx, EXPERTS]),
                                               K.c("iota")[:, 0:nx].unsqueeze(2).broadcast_to([P, nx, EXPERTS]),
                                               ALU.is_le).then_inc(K.dve.sem, 1))
                for due in K.due(v, m):
                    v.wait_ge(*due)
                for due in K.due(v, K.dve.mark(v.tensor_reduce(xidf[:, :], cmp[:, :, :], AX.X, ALU.add).then_inc(K.dve.sem, 1))):
                    v.wait_ge(*due)
                for due in K.due(v, K.dve.mark(v.tensor_scalar(xidf[:, :], xidf[:, :], float(EXPERTS - 1), None, ALU.min).then_inc(K.dve.sem, 1))):
                    v.wait_ge(*due)
                K.mx = K.dve.mark(v.tensor_copy(xid[:, :], xidf[:, :]).then_inc(K.dve.sem, 1))
            K.xid_ready, K.xid = K.mx, xid
            scattered = []
            prev = K.mx
            for t in range(tiles):
                b = K.banks.next()

                @block.tensor
                def _(pe):
                    for due in K.due(pe, *b.free):
                        pe.wait_ge(*due)
                    for u in range(t + 1):
                        ins = pe.matmul(b.t[:, 0:EXPERTS], K.c("before") if u == t else K.c("ones"), both[:, u, :],
                                        start=(u == 0), stop=(u == t))
                    K.mp = K.pe.mark(ins.then_inc(K.pe.sem, 1))
                for k in range(2):
                    q = pos.next()
                    R, XB, Q, REM, BLK, A1, A2, POS, TP = (q.t[:, i:i + 1] for i in range(9))

                    @block.vector
                    def _(v):
                        for due in K.due(v, K.mp, *q.free, prev):
                            v.wait_ge(*due)
                        K.dve.mark(v.scalar_tensor_tensor(out=scr[:, 0, :], in0=oh[:, t, k, :], scalar=1.0,
                                                          in1=b.t[:, 0:EXPERTS], op0=ALU.mult, op1=ALU.mult,
                                                          accum_out=R).then_inc(K.dve.sem, 1))
                        m = K.dve.mark(v.scalar_tensor_tensor(out=scr[:, 1, :], in0=oh[:, t, k, :], scalar=1.0, in1=EXCL,
                                                              op0=ALU.mult, op1=ALU.mult, accum_out=XB).then_inc(K.dve.sem, 1))
                        b.free = [m]
                        for due in K.due(v, m):
                            v.wait_ge(*due)
                        m = K.dve.mark(v.tensor_scalar(Q, R, float(CAP), None, ALU.is_ge).then_inc(K.dve.sem, 1))
                        for j in range(2, deep):
                            for due in K.due(v, m):
                                v.wait_ge(*due)
                            m = K.dve.mark(v.scalar_tensor_tensor(out=Q, in0=R, scalar=float(j * CAP), in1=Q,
                                                                  op0=ALU.is_ge, op1=ALU.add).then_inc(K.dve.sem, 1))
                        for due in K.due(v, m):
                            v.wait_ge(*due)
                        K.dve.mark(v.scalar_tensor_tensor(out=REM, in0=Q, scalar=-float(CAP), in1=R, op0=ALU.mult,
                                                          op1=ALU.add).then_inc(K.dve.sem, 1))
                        m = K.dve.mark(v.scalar_tensor_tensor(out=A1, in0=Q, scalar=float(EXPERTS - 1), in1=XB,
                                                              op0=ALU.add, op1=ALU.add).then_inc(K.dve.sem, 1))
                        for due in K.due(v, m):
                            v.wait_ge(*due)
                        m = K.dve.mark(v.tensor_tensor(A1, A1, ek[:, t, k:k + 1], ALU.subtract).then_inc(K.dve.sem, 1))
                        for due in K.due(v, m):
                            v.wait_ge(*due)
                        m = K.dve.mark(v.scalar_tensor_tensor(out=A2, in0=Q, scalar=0.5, in1=A1, op0=ALU.is_gt,
                                                              op1=ALU.mult).then_inc(K.dve.sem, 1))
                        for due in K.due(v, m):
                            v.wait_ge(*due)
                        m = K.dve.mark(v.tensor_tensor(BLK, A2, ek[:, t, k:k + 1], ALU.add).then_inc(K.dve.sem, 1))
                        for due in K.due(v, m):
                            v.wait_ge(*due)
                        K.dve.mark(v.scalar_tensor_tensor(out=POS, in0=BLK, scalar=float(CAP), in1=REM, op0=ALU.mult,
                                                          op1=ALU.add).then_inc(K.dve.sem, 1))
                        m = K.dve.mark(v.scalar_tensor_tensor(out=TP, in0=REM, scalar=float(nb), in1=BLK, op0=ALU.mult,
                                                              op1=ALU.add).then_inc(K.dve.sem, 1))
                        for due in K.due(v, m):
                            v.wait_ge(*due)
                        K.dve.mark(v.tensor_copy(yrow[:, t, k:k + 1], POS).then_inc(K.dve.sem, 1))
                        K.mv = K.dve.mark(v.tensor_copy(tokpos[:, t, k:k + 1], TP).then_inc(K.dve.sem, 1))
                    q.free = [K.mv]
                    prev = K.mv

                    @block.gpsimd
                    def _(g):
                        sig = K.moved.next()
                        for due in K.due(g, (sig, sig.count) if sig.count else None, K.mv, K.mz, early):
                            g.wait_ge(*due)
                        scattered.append(sig.mark(g.indirect_dma_start(
                            ids_dram, bass.IndirectOffsetOnAxis(ap=tokpos[:, t, k:k + 1], axis=0),
                            tokid[:, t:t + 1], None).then_inc(sig.sem, 16), 16))

            @block.gpsimd
            def _(g):
                K.mt = K.move(g, tokidx[:, :], ids_dram.rearrange("(p n) a -> p (n a)", n=nb), *scattered)
            routed = [K.mt, *hstored]
            K.settle()
        with ExitStack() as ctx:
            xg = K.turn(ctx, "xg", 3, [CAP, D])
            xgT = K.turn(ctx, "xgT", 2, [P, KD, CAP])
            gs = K.turn(ctx, "gs", 2, [P, DE // P, CAP])
            aT = K.turn(ctx, "aT", 2, [P, DE // P, CAP])
            yo = K.turn(ctx, "yo", 2, [CAP, D])
            got, stored = {}, []

            def gather(b):
                x = xg.next()

                @block.gpsimd
                def _(g):
                    sig = K.moved.next()
                    for due in K.due(g, (sig, sig.count) if sig.count else None, *routed, *x.free):
                        g.wait_ge(*due)
                    got[b] = (x, sig.mark(g.indirect_dma_start(
                        x.t[:, :], None, h_dram, bass.IndirectOffsetOnAxis(ap=tokidx[:, b:b + 1], axis=0)).then_inc(sig.sem, 16), 16))
            hidden = {}

            def widen(b):
                x, mk = got[b]
                xt = xgT.next()
                per = 512 // CAP
                ready = []
                for c in range(KD // per):
                    bk = K.banks.next()

                    @block.tensor
                    def _(pe):
                        for due in K.due(pe, mk, *bk.free):
                            pe.wait_ge(*due)
                        for j in range(per):
                            kk = c * per + j
                            ins = pe.transpose(bk.t[:, j * CAP:(j + 1) * CAP], x.t[:, kk * P:(kk + 1) * P],
                                               K.ident[0:CAP, 0:CAP])
                        K.mp = K.pe.mark(ins.then_inc(K.pe.sem, 1))
                    m = K.copy(c, xt.t[:, c * per:(c + 1) * per, :],
                               bk.t[:, :].rearrange("p (k t) -> p k t", k=per), K.mp, *xt.free)
                    bk.free = [m]
                    ready.append(m)
                x.free = [K.mp]
                outs = []
                for key in ("eg", "eu"):
                    i, wv, landed = K.take((key, l, b))
                    bk = K.banks.next()

                    @block.tensor
                    def _(pe):
                        for due in K.due(pe, landed, *ready, *bk.free):
                            pe.wait_ge(*due)
                        for j in range(DE // P):
                            for k in range(KD):
                                ins = pe.matmul(bk.t[:, j * CAP:(j + 1) * CAP], wv[:, k, j * P:(j + 1) * P],
                                                xt.t[:, k, :], start=(k == 0), stop=(k == KD - 1))
                        K.mp = K.pe.mark(ins.then_inc(K.pe.sem, 1))
                    K.give(i, K.mp)
                    outs.append((bk, K.mp))
                xt.free = [K.mp]
                (bg, mg), (bu, mu) = outs
                g_, a_ = gs.next(), aT.next()
                n = DE // P * CAP
                flat = lambda z: z.t[:, :, :].rearrange("p k t -> p (k t)")

                @block.scalar
                def _(act):
                    for due in K.due(act, mg, *g_.free):
                        act.wait_ge(*due)
                    K.ml = K.act.mark(act.activation(flat(g_), bg.t[:, 0:n], ACT.Silu).then_inc(K.act.sem, 1))
                bg.free = [K.ml]

                @block.vector
                def _(v):
                    for due in K.due(v, K.ml, mu, *a_.free):
                        v.wait_ge(*due)
                    K.mv = K.dve.mark(v.tensor_tensor(flat(a_), flat(g_), bu.t[:, 0:n], ALU.mult).then_inc(K.dve.sem, 1))
                bu.free = g_.free = [K.mv]
                hidden[b] = (a_, K.mv)

            def narrow(b):
                a_, m = hidden[b]
                i, wv, landed = K.take(("ed", l, b))
                y = yo.next()
                ms = []
                for n in range(2):
                    bk = K.banks.next()

                    @block.tensor
                    def _(pe):
                        for due in K.due(pe, landed, m, *bk.free):
                            pe.wait_ge(*due)
                        for k in range(DE // P):
                            ins = pe.matmul(bk.t[0:CAP, :], a_.t[:, k, :], wv[:, k, 512 * n:512 * n + 512],
                                            start=(k == 0), stop=(k == DE // P - 1))
                        K.mp = K.pe.mark(ins.then_inc(K.pe.sem, 1))
                    mm = K.copy(n, y.t[:, 512 * n:512 * n + 512], bk.t[0:CAP, :], K.mp, *y.free)
                    bk.free = [mm]
                    ms.append(mm)
                K.give(i, K.mp)
                a_.free = [K.mp]

                @block.gpsimd
                def _(g):
                    y.free = [K.move(g, y_dram[b * CAP:(b + 1) * CAP, :], y.t[:, :], *ms)]
                stored.append(y.free[0])
            gather(0)
            gather(1)
            for b in range(nb + 1):
                if b + 2 < nb:
                    gather(b + 2)
                if b < nb:
                    widen(b)
                if b > 0:
                    narrow(b - 1)
            K.settle()
        with ExitStack() as ctx:
            yg = K.turn(ctx, "yg", 4, [P, D])
            gate = K.sb("gate2", [P, 2, D], ctx=ctx)
            gm = []

            @block.gpsimd
            def _(g):
                for _, s in streams:
                    gm.append(broadcast_row(g, gate[:, s, :], MG2, s, *K.settled))
            for t in range(tiles):
                ys = []
                for k in range(2):
                    y = yg.next()

                    @block.gpsimd
                    def _(g):
                        sig = K.moved.next()
                        for due in K.due(g, (sig, sig.count) if sig.count else None, *y.free):
                            g.wait_ge(*due)
                        ys.append((y, sig.mark(g.indirect_dma_start(
                            y.t[:, :], None, y_dram[0:nb * CAP, :],
                            bass.IndirectOffsetOnAxis(ap=yrow[:, t, k:k + 1], axis=0)).then_inc(sig.sem, 16), 16)))

                @block.vector
                def _(v):
                    (y0, m0), (y1, m1) = ys
                    for due in K.due(v, m0, m1, *gm):
                        v.wait_ge(*due)
                    for due in K.due(v, K.dve.mark(v.tensor_scalar(y0.t[:, :], y0.t[:, :], wts[:, t, 0:1], None, ALU.mult).then_inc(K.dve.sem, 1))):
                        v.wait_ge(*due)
                    for due in K.due(v, K.dve.mark(v.scalar_tensor_tensor(out=y0.t[:, :], in0=y1.t[:, :], scalar=wts[:, t, 1:2],
                                                                in1=y0.t[:, :], op0=ALU.mult, op1=ALU.add).then_inc(K.dve.sem, 1))):
                        v.wait_ge(*due)
                    for due in K.due(v, K.dve.mark(v.tensor_tensor(y0.t[:, :], y0.t[:, :], gate[:, s_of(t), :], ALU.mult).then_inc(K.dve.sem, 1))):
                        v.wait_ge(*due)
                    K.mv = K.dve.mark(v.tensor_tensor(x_of(t), x_of(t), y0.t[:, :], ALU.add).then_inc(K.dve.sem, 1))
                    y0.free = y1.free = [K.mv]
            K.settle()


def scaled_norm(K, x, row_src, dst):
    with ExitStack() as ctx:
        w = work_buffers(K, ctx, D, 2)
        row = K.sb("row", [P, D], ctx=ctx)

        @K.block.gpsimd
        def _(g):
            K.ms = K.move(g, row[:, :], row_src.partition_broadcast(P), *K.settled)
        rm = K.ms
        for t in range(TT):
            xn = w["xn"].next()
            m = K.norm_rows(w, x[:, t, :], xn.t[:, :], D, *K.settled, *xn.free)

            @K.block.vector
            def _(v):
                for due in K.due(v, m, rm):
                    v.wait_ge(*due)
                K.mv = K.dve.mark(v.tensor_tensor(dst[:, t, :], xn.t[:, :], row[:, :], ALU.mult).then_inc(K.dve.sem, 1))
            xn.free = [K.mv]
        K.settle()


def second_block(K, x, hT, out):
    A, block, nc = K.A, K.block, K.nc
    modrows = nc.dram_tensor("mod_rows", [2, 64, P], F32).ap()
    with ExitStack() as ctx:
        colt = K.sb("cols2", [P, PDW], ctx=ctx)
        rowt = K.sb("rows2", [P, PRW], ctx=ctx)
        xc = K.sb("xc", [P, TT, D], ctx=ctx)

        @block.gpsimd
        def _(g):
            K.pm = [K.move(g, colt[:, :], A["cols2"]), K.move(g, rowt[:, :], A["rows"].partition_broadcast(P)),
                    K.move(g, xc[:, :, :], A["ctx_2"].rearrange("(t p) d -> p t d", p=P))]
        if not K.spread:
            spread_bias(K)
        K.settle()
        cols = lambda n, i, c: colt[:, PD[n] + i:PD[n] + i + c]
        mods = [modulation(K, l, ctx, cols, modrows) for l in range(2)]
        scaled_norm(K, x, A["norm_final_w"], x)
        for l in range(2):
            mod, gain, _ = mods[l]
            x_of = lambda t: xc[:, t, :] if t < 2 else x[:, t - 2, :]
            s_of = lambda t: 1 if t < 2 else 0
            with ExitStack() as c2:
                w = work_buffers(K, c2)
                hdeps = rows_to_hT(K, w, x_of, range(NT2), hT, lambda k, t: gain[:, k, s_of(t):s_of(t) + 1],
                                   lambda k, t: mod[:, k, s_of(t):s_of(t) + 1], K.settled)
                K.settle()
            with ExitStack() as c2:
                oT = K.sb("oT2", [P, KD, NT2 * P if l == 0 else SEQ], ctx=c2)
                if l == 0:
                    latent_attention(K, c2, hT, hdeps, oT, cols)
                    grouped_attention(K, hT, hdeps, oT, rowt)
                else:
                    neighbourhood_attention(K, hT, hdeps, oT)
                g1 = K.sb("g1", [P, 2, D], ctx=c2)
                gm = []

                @block.gpsimd
                def _(g):
                    for s in range(2 - l):
                        src = modrows[l].rearrange("(a s k) p -> a s (k p)", a=4, s=2)[MG1, s]
                        gm.append(K.move(g, g1[:, s, :], src.partition_broadcast(P), *K.settled))
                if l == 0:
                    add_gated(K, c2, x_of, [("abo", 0), ("abo", 1)], lambda k, t: oT[:, k, t * P:(t + 1) * P],
                              [0, 1, 2, 3], lambda t: g1[:, s_of(t), :], gm)
                else:
                    add_gated(K, c2, x_of, [("nao", 0), ("nao", 1)], lambda k, t: oT[:, k, (t - 2) * P:(t - 1) * P],
                              [2, 3], lambda t: g1[:, 0, :], gm)
                K.settle()
            nb = blocks_of(l)[1]
            dram = (nc.dram_tensor(f"slot_tokens{l}", [nb * CAP, 1], U32).ap(),
                    nc.dram_tensor(f"h_rows{l}", [blocks_of(l)[0] * P, D], F32).ap(),
                    nc.dram_tensor(f"y_rows{l}", [nb * CAP, D], F32).ap())
            moe(K, l, [(xc, 1), (x, 0)] if l == 0 else [(x, 0)], hT, modrows, rowt, dram)
        scaled_norm(K, x, A["norm_final_2"], x)

        @block.gpsimd
        def _(g):
            for due in K.due(g, K.move(g, out.rearrange("(t p) d -> p t d", p=P), x[:, :, :], *K.settled)):
                g.wait_ge(*due)


def laid_out(i):
    f = lambda a: np.ascontiguousarray(np.asarray(a))
    col = lambda a: f(a).reshape(-1, P).T
    cols1 = []
    for l in range(2):
        taps = lambda w: f(w).reshape(w.shape[0], -1, P).transpose(2, 1, 0).reshape(P, -1)
        cols1 += [col(i["norm_mix_w"][l]), taps(i["ssd_conv_w"][l]), col(i["ssd_conv_b"][l]),
                  col(i["ssd_norm_w"][l]), col(i["norm_ffn_w"][l]), taps(i["ffn_conv_w"][l]),
                  col(i["ffn_conv_b"][l])]
    both = f(np.stack([f(i["c_2"])[0], f(i["c_ctx_2"])])).reshape(2, KD, P).transpose(2, 1, 0).reshape(P, -1)
    cols2 = [both] + [col(i["b_ada_2"][l]) for l in range(2)] + [col(i["norm_mix_2"][l]) for l in range(2)]
    cols2 += [col(i["mla_q_norm_2"][0]), col(i["mla_kv_norm_2"][0])]
    rows = [f(i[n]).reshape(-1) for n in ("ssd_dt_bias", "ssd_a_log", "ssd_d", "gqa_q_norm_2", "gqa_k_norm_2")]
    for l in range(2):
        rows += [f(i["moe_b_rg_2"][l]), f(i["moe_b_re_2"][l])]
    out = {"cols1": np.concatenate(cols1, 1), "cols2": np.concatenate(cols2, 1), "rows": np.concatenate(rows),
           "constants": CONST}
    for n in ("w_in", "w_proj_attn", "w_proj_ssd", "w_out", "ffn_w_up", "ffn_w_down", "norm_final_w", "w_ada_2",
              "norm_ffn_2", "norm_final_2", "mla_w_q_up_2", "mla_w_kv_up_2", "ab_w_in_2", "ab_w_out_2",
              "na_w_in_2", "na_w_out_2", "moe_w_gate_2", "moe_w_up_2", "moe_w_down_2"):
        out[n] = f(i[n])
    out["router_2"] = np.concatenate([f(i["moe_w_rg_2"]), f(i["moe_w_re_2"])], 2)
    out["x"] = f(i["x"])[0]
    out["ctx_2"] = f(i["ctx_2"])[0]
    out["rpb_2"] = f(i["na_rpb_2"])[0]
    return {k: np.ascontiguousarray(v) for k, v in out.items()}


def build_program(nc, A, out):
    with ExitStack() as ctx:
        block = ctx.enter_context(nc.Block())
        K = Core(nc, ctx, block, A)
        x = K.sb("x", [P, TT, D])
        hT = K.sb("hT", [P, KD, NT2 * P])
        for l in range(2):
            plan_first(K, l)
        for l in range(2):
            plan_ada(K, l)
        for l in range(2):
            plan_second(K, l)
        K.start_weights()

        @block.gpsimd
        def _(g):
            K.pm = [K.move(g, K.const[:, :], A["constants"]),
                    K.move(g, x[:, :, :], A["x"].rearrange("(t p) d -> p t d", p=P))]

        @block.vector
        def _(v):
            K.pm.append(K.dve.mark(v.memset(K.eps[:, :], EPS).then_inc(K.dve.sem, 1)))
        K.settle()
        spread_bias(K)
        first_block(K, x, hT, K.settled)
        second_block(K, x, hT, out)
        assert K.taken == len(K.plan)


INPUTS = ["constants", "cols1", "cols2", "rows", "x", "ctx_2", "rpb_2", "router_2", "w_in", "w_proj_attn",
          "w_proj_ssd", "w_out", "ffn_w_up", "ffn_w_down", "norm_final_w", "w_ada_2", "norm_ffn_2",
          "norm_final_2", "mla_w_q_up_2", "mla_w_kv_up_2", "ab_w_in_2", "ab_w_out_2", "na_w_in_2", "na_w_out_2",
          "moe_w_gate_2", "moe_w_up_2", "moe_w_down_2"]


def kernel(**inputs):
    import concourse.bacc as bacc
    from concourse.bass_utils import run_bass_kernel_spmd

    nc = bacc.Bacc("TRN2", target_bir_lowering=False, num_devices=1)
    data = laid_out(inputs)
    arrays, A = {}, {}
    for name in INPUTS:
        a = data[name]
        arrays[f"in_{name}"] = a
        A[name] = nc.dram_tensor(f"in_{name}", a.shape, mybir.dt.from_np(a.dtype), kind="ExternalInput").ap()
    out = nc.dram_tensor("out_rows", (SEQ, D), F32, kind="ExternalOutput").ap()
    build_program(nc, A, out)
    r = run_bass_kernel_spmd(nc, [arrays], core_ids=[0])
    return r.results[0]["out_rows"].reshape(1, SEQ, D)
```

```python
from contextlib import ExitStack

import numpy as np

import concourse.bass as bass
from concourse import mybir

F32 = mybir.dt.float32
U32 = mybir.dt.uint32
ALU = mybir.AluOpType
ACT = mybir.ActivationFunctionType
AX = mybir.AxisListType

P = 128
D = 1024
KD = D // P
SEQ = 256
TT = SEQ // P
EPS = 1e-6
NEG = -1.0e30
TAKEN = -3.0e38

HEADS, HD, KVH = 8, 128, 2
IH, IDM = 8, 64
TOPK = min(256, SEQ // 4)
INNER, SHD, SHEADS, GROUPS, STATE = 2048, 64, 32, 4, 128
HPG = SHEADS // GROUPS
GW = INNER // GROUPS
CONV = 4
XBC = INNER + 2 * GROUPS * STATE
XCH = XBC // P
FFN, FCONV = 2816, 3
FCH = FFN // P
COL = {}
_o = 0
for _n, _w in (("q", 1024), ("k", 256), ("v", 256), ("qi", 512), ("ki", 64), ("wi", 8), ("z", INNER),
               ("xbc", XBC), ("dt", SHEADS), ("ga", D), ("gs", D)):
    COL[_n] = _o
    _o += _w

HA, NOPE, ROPE, VA, QL, KVL = 8, 64, 32, 64, 384, 256
HB, KVB, HD2 = 8, 2, 64
HC = 16
NT2 = 4
GRID_W, WIN_R, WIN_C = 64, 8, 16
EXPERTS, EG, NGR, DE = 32, 8, 4, 512
CAP = 128

PC = {}
_o = 0
for _n, _w in (("norm_mix", KD), ("conv_w", XCH * CONV), ("conv_b", XCH), ("ssd_norm", INNER // P),
               ("norm_ffn", KD), ("fconv_w", 2 * FCH * FCONV), ("fconv_b", 2 * FCH)):
    PC[_n] = _o
    _o += _w
PCW = _o
PD = {}
_o = 0
for _n, _w in (("c", 2 * KD), ("b_ada", 2 * 48), ("norm_mix", 2 * KD), ("q_norm", QL // P),
               ("kv_norm", KVL // P)):
    PD[_n] = _o
    _o += _w
PDW = _o
PR = {}
_o = 0
for _n, _w in (("dt_bias", 64), ("a_log", 64), ("d", 64), ("gq_norm", 64), ("gk_norm", 64),
               ("b_router", 72)):
    PR[_n] = _o
    _o += _w
PRW = _o


def shape_constants():
    parts = {}
    i = np.arange(P)
    parts["ident"] = np.eye(P, dtype=np.float32)
    parts["upto"] = (i[:, None] <= i[None, :]).astype(np.float32)
    parts["before"] = (i[:, None] < i[None, :]).astype(np.float32)
    parts["ones"] = np.ones((P, P), np.float32)
    parts["segmask"] = np.where(i[:, None] <= i[None, :], 0.0, NEG).astype(np.float32)
    pos = np.arange(SEQ)
    causal = np.where(pos[None, :] <= pos[:, None], 0.0, NEG).astype(np.float32)
    parts["causal"] = causal.reshape(TT, P, SEQ).transpose(1, 0, 2)

    def split(a):
        return a.reshape(TT, P, -1).transpose(1, 0, 2)

    def half_tables(rot):
        inv = np.float32(500000.0) ** (-np.arange(0, rot, 2, dtype=np.float32) / np.float32(rot))
        ang = (pos.astype(np.float32)[:, None] * inv[None, :].astype(np.float32)).astype(np.float32)
        c, s = np.cos(ang), np.sin(ang)
        return split(np.concatenate([c, c], 1)), split(np.concatenate([-s, s], 1))

    parts["cosa"], parts["sina"] = half_tables(HD // 4)
    parts["cosi"], parts["sini"] = half_tables(IDM // 4)

    def axial(rot):
        n = rot // 4
        inv = np.float32(10000.0) ** (-np.arange(n, dtype=np.float32) / np.float32(n))
        r, c = (pos // GRID_W).astype(np.float32), (pos % GRID_W).astype(np.float32)
        ang = np.concatenate([r[:, None] * inv, c[:, None] * inv], 1).astype(np.float32)
        co, si = np.cos(ang), np.sin(ang)
        return (split(np.stack([co, co], -1).reshape(SEQ, rot)),
                split(np.stack([-si, si], -1).reshape(SEQ, rot)))

    parts["cos2a"], parts["sin2a"] = axial(ROPE)
    parts["cos2b"], parts["sin2b"] = axial(HD2)
    rows = SEQ // GRID_W
    cs = np.clip(pos % GRID_W - WIN_C // 2, 0, GRID_W - WIN_C)
    kc = pos % GRID_W
    seen = (kc[None, :] >= cs[:, None]) & (kc[None, :] < cs[:, None] + WIN_C)
    assert rows <= WIN_R
    parts["window"] = split(np.where(seen, 0.0, NEG).astype(np.float32))
    parts["iota"] = np.broadcast_to(np.arange(EXPERTS, dtype=np.float32), (P, EXPERTS))
    token = (np.arange(NT2)[None, :] * P + i[:, None]).astype(np.float32)
    parts["token"] = token
    where, cols, at = {}, [], 0
    for name, a in parts.items():
        w = int(np.prod(a.shape[1:]))
        where[name] = (at, a.shape[1:])
        cols.append(np.ascontiguousarray(a, dtype=np.float32).reshape(P, w))
        at += w
    return np.concatenate(cols, 1), where


CONST, CONST_AT = shape_constants()


class Signal:

    def __init__(self, ctx, nc, name):
        self.sem = ctx.enter_context(nc.semaphore(name))
        self.name = name
        self.count = 0

    def mark(self, ins, by=1):
        self.count += by
        return (self, self.count)


class Buf:

    def __init__(self, t):
        self.t = t
        self.free = []


class Turn:

    def __init__(self, bufs):
        self.bufs = bufs
        self.n = 0

    def next(self):
        b = self.bufs[self.n % len(self.bufs)]
        self.n += 1
        return b


def together(parts):
    running = list(parts)
    while running:
        for r in list(running):
            try:
                next(r)
            except StopIteration:
                running.remove(r)
        yield


def pipeline(parts, depth, aside=(), every=1):
    parts = list(parts)
    running, aside, rounds = [], iter(aside), 0
    while parts or running:
        rounds += 1
        if rounds % every == 0:
            next(aside, None)
        if parts and len(running) < depth:
            running.append(parts.pop(0))
        for r in list(running):
            try:
                next(r)
            except StopIteration:
                running.remove(r)
    for _ in aside:
        pass


RING = 5


class Core:

    def __init__(self, nc, ctx, A, name="", like=None, slots=None):
        self.nc, self.ctx, self.A = nc, ctx, A
        self.pe = Signal(ctx, nc, f"{name}tensor_done")
        self.dve = Signal(ctx, nc, f"{name}vector_done")
        self.act = Signal(ctx, nc, f"{name}scalar_done")
        self.pool = Signal(ctx, nc, f"{name}pool_done")
        self.moved = Turn([Signal(ctx, nc, f"{name}moved{i}") for i in range(8 if like else 24)])
        self.plan, self.landings, self.taken, self.spread = [], {}, 0, []
        self.rest = []
        if like is None:
            self.waited, self.names = {}, [0]
            self.begin()
            self.slots = [ctx.enter_context(nc.sbuf_tensor(f"wslot{i}", [P, 4096], F32)) for i in range(RING)]
            self.banks = Turn([Buf(ctx.enter_context(nc.psum_tensor(f"bank{i}", [P, 512], F32))) for i in range(8)])
            self.const = self.sb("const", [P, CONST.shape[1]])
            self.eps = self.sb("eps", [P, 1])
        else:
            self.waited, self.names, self.slots = dict(like.waited), like.names, slots
            self.banks, self.const, self.eps = like.banks, like.const, like.eps
        self.landed = [Signal(ctx, nc, f"{name}weights_landed{i}") for i in range(len(self.slots))]
        self.ident = self.c("ident")

    def sb(self, name, shape, dt=F32, ctx=None):
        self.names[0] += 1
        return (ctx or self.ctx).enter_context(self.nc.sbuf_tensor(f"{name}_{self.names[0]}", shape, dt))

    def turn(self, ctx, name, n, shape, dt=F32):
        return Turn([Buf(self.sb(f"{name}{i}", shape, dt, ctx)) for i in range(n)])

    def begin(self):
        self.stretch = self.nc.Block()
        self.block = self.stretch.__enter__()

    def end(self):
        self.stretch.__exit__(None, None, None)

    def apart(self, ctx, name, ring):
        slots = [self.sb(f"{name}_wslot{i}", [P, 4096], ctx=ctx) for i in range(ring)]
        part = Core(self.nc, self.ctx, self.A, f"{name}_", self, slots)
        part.xid, part.xid_ready = self.xid, self.xid_ready
        return part

    def c(self, name):
        at, shape = CONST_AT[name]
        w = int(np.prod(shape))
        ap = self.const[:, at:at + w]
        return ap if len(shape) == 1 else ap.rearrange("p (a b) -> p a b", a=shape[0])

    def due(self, eng, *marks):
        left = []
        for m in marks:
            if m is None:
                continue
            sig, value = m
            key = (str(eng.engine), sig.name)
            if self.waited.get(key, 0) < value:
                self.waited[key] = value
                left.append((sig.sem, value))
        return left

    def move(self, eng, out, in_, *deps):
        sig = self.moved.next()
        for due in self.due(eng, (sig, sig.count) if sig.count else None, *deps):
            eng.wait_ge(*due)
        return sig.mark(eng.dma_start(out, in_).then_inc(sig.sem, 16), 16)

    def flush(self, most=None):
        for _ in range(len(self.rest) if most is None else min(most, len(self.rest))):
            self.rest.pop(0)()
        while most is None and self.rest:
            self.rest.pop(0)()

    def settle(self):
        self.flush()
        marks = [(s, s.count) for s in [self.pe, self.dve, self.act, self.pool] + self.moved.bufs if s.count]
        self.settled = marks

        @self.block.tensor
        def _(e):
            for due in self.due(e, *marks):
                e.wait_ge(*due)

        @self.block.vector
        def _(e):
            for due in self.due(e, *marks):
                e.wait_ge(*due)

        @self.block.scalar
        def _(e):
            for due in self.due(e, *marks):
                e.wait_ge(*due)

        @self.block.gpsimd
        def _(e):
            for due in self.due(e, *marks):
                e.wait_ge(*due)

    def plan_tile(self, key, w, k0, kc, n0, n):
        self.plan.append((key, [(0, kc, n, 0, n, w[k0:k0 + kc * P, n0:n0 + n])]))

    def plan_expert(self, key, name, l, b, kc, n):
        w = self.A[name]
        if b < EXPERTS:
            self.plan_tile(key, w[l, b], 0, kc, 0, n)
        else:
            self.plan.append((key, [(0, kc, n, 0, n, (w, l, b - EXPERTS))]))

    def plan_experts(self, l, blocks):
        for b in [*blocks, None]:
            if b is not None:
                self.plan_expert(("eg", l, b), "moe_w_gate_2", l, b, KD, DE)
                self.plan_expert(("eu", l, b), "moe_w_up_2", l, b, KD, DE)
            if b != blocks[0]:
                before = blocks[-1] if b is None else b - 1
                self.plan_expert(("ed", l, before), "moe_w_down_2", l, before, DE // P, D)

    def issue(self, i, *deps):
        if i >= len(self.plan):
            return
        key, parts = self.plan[i]
        slot = i % len(self.slots)
        sig = self.landed[slot]

        @self.block.sync
        def _(sp):
            for due in self.due(sp, *deps):
                sp.wait_ge(*due)
            for at, kc, n, c0, cn, src in parts:
                if isinstance(src, tuple):
                    wt, l, x = src
                    for due in self.due(sp, self.xid_ready):
                        sp.wait_ge(*due)
                    e = sp.value_load(self.xid[0:1, x:x + 1], min_val=0, max_val=EXPERTS - 1)
                    src = wt[l, bass.ds(e, 1)].rearrange("a k n -> (a k) n")
                dst = self.slots[slot][:, at:at + kc * n].rearrange("p (k n) -> p k n", k=kc)[:, :, c0:c0 + cn]
                self.landings[i] = sig.mark(sp.dma_start(dst, src.rearrange("(k p) n -> p k n", p=P)).then_inc(sig.sem, 16), 16)

    def start_weights(self):
        for i in range(len(self.slots)):
            self.issue(i)

    def take(self, key):
        i = self.taken
        self.taken += 1
        want, parts = self.plan[i]
        assert want == key, (want, key)
        _, kc, n, _, _, _ = parts[0]
        view = self.slots[i % len(self.slots)][:, 0:kc * n].rearrange("p (k n) -> p k n", k=kc)
        return i, view, self.landings[i]

    def give(self, i, mark):
        self.issue(i + len(self.slots), mark)

    def tokens_later(self, key, xT, n_tiles, deps, use):
        i, w, landed = self.take(key)
        kc, n = w.shape[1], w.shape[2]

        def put(t, bank, mark):
            bank.free = [use(t, bank.t[:, 0:n], mark)]
        for t in range(n_tiles):
            bank = self.banks.next()

            @self.block.tensor
            def _(pe):
                for due in self.due(pe, landed, *deps, *bank.free):
                    pe.wait_ge(*due)
                for k in range(kc):
                    ins = pe.matmul(bank.t[:, 0:n], xT(k, t), w[:, k, :], start=(k == 0), stop=(k == kc - 1))
                self.mt = self.pe.mark(ins.then_inc(self.pe.sem, 1))
            bank.free = None
            self.flush(1)
            self.rest.append(lambda t=t, bank=bank, mark=self.mt: put(t, bank, mark))
        self.give(i, self.mt)

    def tokens_steps(self, key, xT, n_tiles, deps, use):
        i, w, landed = self.take(key)
        kc, n = w.shape[1], w.shape[2]
        for t in range(n_tiles):
            bank = self.banks.next()

            @self.block.tensor
            def _(pe):
                for due in self.due(pe, landed, *deps, *bank.free):
                    pe.wait_ge(*due)
                for k in range(kc):
                    ins = pe.matmul(bank.t[:, 0:n], xT(k, t), w[:, k, :], start=(k == 0), stop=(k == kc - 1))
                self.mt = self.pe.mark(ins.then_inc(self.pe.sem, 1))
            if t == n_tiles - 1:
                self.give(i, self.mt)
            bank.free = [use(t, bank.t[:, 0:n], self.mt)]
            yield

    def tokens_out(self, tiles, xT, n_tiles, deps, use, cols=None):
        banks = [self.banks.next() for _ in range(n_tiles)]
        done = [None] * n_tiles
        k0 = 0
        for a, key in enumerate(tiles):
            i, w, landed = self.take(key)
            kc, n = w.shape[1], w.shape[2]

            @self.block.tensor
            def _(pe):
                for due in self.due(pe, landed, *deps):
                    pe.wait_ge(*due)
                for t in range(n_tiles):
                    if a == 0:
                        for due in self.due(pe, *banks[t].free):
                            pe.wait_ge(*due)
                    for k in range(kc):
                        ins = pe.matmul(banks[t].t[:, 0:n], xT(k0 + k, t), w[:, k, :],
                                        start=(a == 0 and k == 0), stop=(a == len(tiles) - 1 and k == kc - 1))
                    done[t] = self.pe.mark(ins.then_inc(self.pe.sem, 1))
            self.give(i, done[-1])
            k0 += kc
        self.flush()
        for t in range(n_tiles):
            banks[t].free = [use(t, banks[t].t[:, 0:n], done[t])]

    def features_out(self, key, xT, width, deps, use, extra=None):
        i, w, landed = self.take(key)
        kc, n = w.shape[1], w.shape[2]
        mark = None
        for j in range(n // P):
            b = self.banks.next()

            @self.block.tensor
            def _(pe):
                nonlocal mark
                for due in self.due(pe, landed, *deps, *b.free):
                    pe.wait_ge(*due)
                for k in range(kc):
                    ins = pe.matmul(b.t[:, 0:width], w[:, k, j * P:(j + 1) * P], xT(k),
                                    start=(k == 0), stop=(k == kc - 1))
                mark = self.pe.mark(ins.then_inc(self.pe.sem, 1))
            if j == n // P - 1:
                self.give(i, mark)
            self.flush(1)
            b.free = [use(j, b.t[:, 0:width], mark)]

    def inverse_rms(self, ctx_bufs, src, width, *deps):
        junk, st = ctx_bufs
        j, s = junk.next(), st.next()

        @self.block.scalar
        def _(act):
            for due in self.due(act, *deps, *j.free, *s.free):
                act.wait_ge(*due)
            m = self.act.mark(act.activation(j.t[:, 0:width], src, ACT.Square, accum_out=s.t[:, 0:1]).then_inc(self.act.sem, 1))
            j.free = [m]
            for due in self.due(act, m):
                act.wait_ge(*due)
            self.m1 = self.act.mark(act.activation(s.t[:, 1:2], s.t[:, 0:1], ACT.Sqrt, bias=self.eps[:, 0:1],
                                                   scale=1.0 / width).then_inc(self.act.sem, 1))

        @self.block.vector
        def _(v):
            for due in self.due(v, self.m1):
                v.wait_ge(*due)
            self.m2 = self.dve.mark(v.reciprocal(s.t[:, 2:3], s.t[:, 1:2]).then_inc(self.dve.sem, 1))
        return s, s.t[:, 2:3], self.m2

    def norm_rows(self, w, src, dst, width, *deps):
        s, inv, m = self.inverse_rms((w["junk"], w["stat"]), src, width, *deps)

        @self.block.vector
        def _(v):
            for due in self.due(v, m, *deps):
                v.wait_ge(*due)
            self.m3 = self.dve.mark(v.tensor_scalar(dst, src, inv, None, ALU.mult).then_inc(self.dve.sem, 1))
        s.free = [self.m3]
        return self.m3

    def transposed(self, pieces, use, *deps):
        b = self.banks.next()

        @self.block.tensor
        def _(pe):
            for due in self.due(pe, *deps, *b.free):
                pe.wait_ge(*due)
            for n, src in enumerate(pieces):
                w = src.shape[1]
                rows = src.shape[0]
                ins = pe.transpose(b.t[0:w, n * P:n * P + rows], src, self.ident[0:rows, 0:rows])
            self.mt = self.pe.mark(ins.then_inc(self.pe.sem, 1))
        m = self.mt
        b.free = [use(b.t, m)]
        return m, b.free[0]

    def copy(self, i, dst, src, *deps):
        if i % 2:
            @self.block.scalar
            def _(act):
                for due in self.due(act, *deps):
                    act.wait_ge(*due)
                self.mc = self.act.mark(act.activation(dst, src, ACT.Copy).then_inc(self.act.sem, 1))
        else:
            @self.block.vector
            def _(v):
                for due in self.due(v, *deps):
                    v.wait_ge(*due)
                self.mc = self.dve.mark(v.tensor_copy(dst, src).then_inc(self.dve.sem, 1))
        return self.mc

    def rope(self, w, src, dst, cos, sin, interleaved, *deps):
        h, rot = src.shape[1], src.shape[2]
        a, b = w["ropea"].next(), w["ropeb"].next()
        at = a.t[:, 0:h * rot].rearrange("p (h r) -> p h r", h=h)
        bt = b.t[:, 0:h * rot].rearrange("p (h r) -> p h r", h=h)
        cosb = cos.unsqueeze(1).broadcast_to([P, h, rot])
        sinb = sin.unsqueeze(1).broadcast_to([P, h, rot])

        def halves(x):
            if interleaved:
                return x[:, :, 0:rot:2], x[:, :, 1:rot:2]
            return x[:, :, 0:rot // 2], x[:, :, rot // 2:rot]
        (s1, s2), (b1, b2), (n1, n2) = halves(src), halves(bt), halves(sinb)

        @self.block.vector
        def _(v):
            for due in self.due(v, *deps, *a.free, *b.free):
                v.wait_ge(*due)
            self.dve.mark(v.tensor_tensor(at, src, cosb, ALU.mult).then_inc(self.dve.sem, 1))
            self.dve.mark(v.tensor_tensor(b1, s2, n1, ALU.mult).then_inc(self.dve.sem, 1))
            for due in self.due(v, self.dve.mark(v.tensor_tensor(b2, s1, n2, ALU.mult).then_inc(self.dve.sem, 1))):
                v.wait_ge(*due)
            self.mr = self.dve.mark(v.tensor_tensor(dst, at, bt, ALU.add).then_inc(self.dve.sem, 1))
        a.free = b.free = [self.mr]
        return self.mr

    def attend(self, w, q, k, values, nk, scale, bias, out, deps):
        self_ = self
        b = self.banks.next()
        kt = nk // P
        dv = values[0].shape[1]
        po = out.start_partition if not callable(out.start_partition) else out.start_partition()

        @self.block.tensor
        def _(pe):
            for due in self.due(pe, *deps, *b.free):
                pe.wait_ge(*due)
            self.ma = self.pe.mark(pe.matmul(b.t[:, 0:nk], q, k, start=True, stop=True).then_inc(self.pe.sem, 1))
        ready = self.ma
        b.free = None
        yield
        s, st = w["prob"].next(), w["stat"].next()
        st.free, stfree = [], st.free

        @self.block.vector
        def _(v):
            for due in self.due(v, ready, *stfree, *s.free, *deps):
                v.wait_ge(*due)
            if bias is not None:
                m = self.dve.mark(v.scalar_tensor_tensor(out=s.t[:, 0:nk], in0=b.t[:, 0:nk], scalar=scale,
                                                         in1=bias, op0=ALU.mult, op1=ALU.add).then_inc(self.dve.sem, 1))
                b.free = [m]
                for due in self.due(v, m):
                    v.wait_ge(*due)
                self.ma = self.dve.mark(v.tensor_reduce(st.t[:, 0:1], s.t[:, 0:nk], AX.X, ALU.max, negate=True).then_inc(self.dve.sem, 1))
            else:
                self.ma = self.dve.mark(v.tensor_reduce(st.t[:, 0:1], b.t[:, 0:nk], AX.X, ALU.max, negate=True).then_inc(self.dve.sem, 1))
                if scale != 1.0:
                    for due in self.due(v, self.ma):
                        v.wait_ge(*due)
                    self.ma = self.dve.mark(v.tensor_scalar(st.t[:, 0:1], st.t[:, 0:1], scale, None, ALU.mult).then_inc(self.dve.sem, 1))
        top = self.ma

        @self.block.scalar
        def _(act):
            for due in self.due(act, top, *s.free):
                act.wait_ge(*due)
            src = s.t[:, 0:nk] if bias is not None else b.t[:, 0:nk]
            self.ma = self.act.mark(act.activation(s.t[:, 0:nk], src, ACT.Exp, bias=st.t[:, 0:1],
                                                   scale=1.0 if bias is not None else scale,
                                                   accum_out=st.t[:, 1:2]).then_inc(self.act.sem, 1))
        if bias is None:
            b.free = [self.ma]
        exps = self.ma
        yield

        @self.block.vector
        def _(v):
            for due in self.due(v, exps):
                v.wait_ge(*due)
            for due in self.due(v, self.dve.mark(v.reciprocal(st.t[:, 2:3], st.t[:, 1:2]).then_inc(self.dve.sem, 1))):
                v.wait_ge(*due)
            self.ma = self.dve.mark(v.tensor_scalar(s.t[:, 0:nk], s.t[:, 0:nk], st.t[:, 2:3], None, ALU.mult).then_inc(self.dve.sem, 1))
        st.free = [self.ma]
        b2 = self.banks.next()
        probs = self.ma

        @self.block.tensor
        def _(pe):
            for due in self.due(pe, probs, *b2.free):
                pe.wait_ge(*due)
            for i in range(kt):
                ins = pe.transpose(b2.t[:, i * P:(i + 1) * P], s.t[:, i * P:(i + 1) * P], self.ident)
            self.ma = self.pe.mark(ins.then_inc(self.pe.sem, 1))
        turned = s.free = [self.ma]
        b2.free = None
        yield
        pt = w["probT"].next()
        m = self.copy(1, pt.t[:, 0:nk], b2.t[:, 0:nk], *turned, *pt.free)
        b2.free = [m]
        b3 = self.banks.next()

        @self.block.tensor
        def _(pe):
            for due in self.due(pe, m, *b3.free):
                pe.wait_ge(*due)
            for i in range(kt):
                ins = pe.matmul(b3.t[po:po + dv, 0:P], values[i], pt.t[:, i * P:(i + 1) * P],
                                start=(i == 0), stop=(i == kt - 1))
            self.ma = self.pe.mark(ins.then_inc(self.pe.sem, 1))
        pt.free = [self.ma]
        summed = self.ma
        b3.free = None
        yield
        m = self.copy(0, out, b3.t[po:po + dv, 0:P], summed)
        b3.free = [m]
        w["done"].append(m)


def work_buffers(K, ctx, width=D, rows=2):
    w = {"stat": K.turn(ctx, "stat", 12, [P, 4])}
    if width:
        w["junk"] = K.turn(ctx, "junk", 1, [P, width])
    if rows:
        w["xn"] = K.turn(ctx, "xn", rows, [P, D])
    return w


SSD_ORDER = (("gs", 0), ("z", 0), ("z", 1), ("ada", 4), ("gs", 1), ("z", 2),
             ("ada", 5), ("z", 3), ("ada", 6), ("ada", 7))


def plan_first(K, l):
    A = K.A
    win = A["w_in"][l]

    def ada(j):
        K.plan_tile(("ada", l, j), A["w_ada_2"][l], 0, KD, 512 * j, 512)
    K.plan_tile(("qi", l), win, 0, KD, COL["qi"], 512)
    K.plan_tile(("kiwi", l), win, 0, KD, COL["ki"], 72)
    for n in range(2):
        K.plan_tile(("q", l, n), win, 0, KD, COL["q"] + 512 * n, 512)
    K.plan_tile(("kv", l), win, 0, KD, COL["k"], 512)
    for n in range(2):
        K.plan_tile(("ga", l, n), win, 0, KD, COL["ga"] + 512 * n, 512)
    for n in range(2):
        K.plan_tile(("pa", l, n), A["w_proj_attn"][l], 0, KD, 512 * n, 512)
    K.plan_tile(("dt", l), win, 0, KD, COL["dt"], SHEADS)
    for n in (4, 5, 0, 1, 2, 3):
        K.plan_tile(("xbc", l, n), win, 0, KD, COL["xbc"] + 512 * n, 512)
        if n < 4:
            ada(n)
    for name, i in SSD_ORDER:
        if name == "ada":
            ada(i)
        else:
            K.plan_tile((name, l, i), win, 0, KD, COL[name] + 512 * i, 512)
    for n in range(2):
        for k in range(2):
            K.plan_tile(("ps", l, n, k), A["w_proj_ssd"][l], 1024 * k, KD, 512 * n, 512)
    for n in range(2):
        K.plan_tile(("wo", l, n), A["w_out"][l], 0, KD, 512 * n, 512)
    for j in range(6):
        n = 512 if j < 5 else 256
        K.plan_tile(("fg", l, j), A["ffn_w_up"][l], 0, KD, 512 * j, n)
        K.plan_tile(("fv", l, j), A["ffn_w_up"][l], 0, KD, FFN + 512 * j, n)
        if j < 4:
            ada(8 + j)
    for n in range(2):
        for k, kc in enumerate((8, 8, 6)):
            K.plan_tile(("fd", l, n, k), A["ffn_w_down"][l], 1024 * k, kc, 512 * n, 512)


def rows_to_hT(K, w, x, tiles, hT, scale_cols, shift_cols, deps):
    out = []
    for t in tiles:
        xn = w["xn"].next()
        m = K.norm_rows(w, x(t), xn.t[:, :], D, *deps, *xn.free)
        for h in range(2):
            def use(bank, mk):
                for j in range(4):
                    k = 4 * h + j
                    dst, src = hT[:, k, t * P:(t + 1) * P], bank[:, j * P:(j + 1) * P]

                    @K.block.vector
                    def _(v):
                        for due in K.due(v, mk, *deps):
                            v.wait_ge(*due)
                        if shift_cols is None:
                            K.mh = K.dve.mark(v.tensor_scalar(dst, src, scale_cols(k, t), None, ALU.mult).then_inc(K.dve.sem, 1))
                        else:
                            K.mh = K.dve.mark(v.tensor_scalar(dst, src, scale_cols(k, t), shift_cols(k, t),
                                                              ALU.mult, ALU.add).then_inc(K.dve.sem, 1))
                return K.mh
            mp, md = K.transposed([xn.t[:, (4 * h + j) * P:(4 * h + j + 1) * P] for j in range(4)], use, m)
            xn.free = [mp]
            out.append(md)
    return out


def first_attention(K, l, hT, hdeps, acc):
    block = K.block
    with ExitStack() as ctx:
        w = work_buffers(K, ctx, 0, 0)
        w["ropea"], w["ropeb"] = (K.turn(ctx, n, 2, [P, 256]) for n in ("ropea", "ropeb"))
        w["prob"] = K.turn(ctx, "prob", 6, [P, SEQ])
        w["probT"] = K.turn(ctx, "probT", 5, [P, SEQ])
        tok = K.turn(ctx, "tok", 4, [P, 512])
        qT = K.sb("qT", [P, HEADS, SEQ], ctx=ctx)
        kT = K.sb("kT", [P, KVH, SEQ], ctx=ctx)
        vt = K.sb("vt", [P, TT, KVH * HD], ctx=ctx)
        qiT = K.sb("qiT", [P, IH // 2, SEQ], ctx=ctx)
        kiT = K.sb("kiT", [P, SEQ], ctx=ctx)
        wi = K.sb("wi", [P, TT, IH], ctx=ctx)
        score = K.sb("score", [P, TT, SEQ], ctx=ctx)
        left = K.sb("left", [P, TT, SEQ], ctx=ctx)
        top8 = K.sb("top8", [P, TT, 8], ctx=ctx)
        oT = K.sb("oT", [P, HEADS, SEQ], ctx=ctx)
        gate = K.sb("gate", [P, TT, D], ctx=ctx)
        relu = K.turn(ctx, "relu", 2, [P, SEQ])
        xT = lambda k, t: hT[:, k, t * P:(t + 1) * P]
        ready = []

        def rotated(heads, cos, sin, rot, width, put, extra=None):
            def use(t, bank, mk):
                b = tok.next()
                c = K.copy(1, b.t[:, 0:bank.shape[1]], bank, mk, *b.free)
                d3 = b.t[:, 0:heads * width].rearrange("p (h d) -> p h d", h=heads)[:, :, 0:rot]
                m = K.rope(w, d3, d3, K.c(cos)[:, t, :], K.c(sin)[:, t, :], False, mk, c)
                b.free = [put(t, b.t, m)]
                return c
            return use

        scored = []

        def put_heads(dst, first, ready=ready):
            def put(t, rows, m):
                def use(bank, mk):
                    mm = K.copy(0, dst[:, first:first + 4, t * P:(t + 1) * P],
                                bank[:, 0:512].rearrange("p (h t) -> p h t", h=4), mk)
                    ready.append(mm)
                    return mm
                return K.transposed([rows[:, h * P:(h + 1) * P] for h in range(4)], use, m)[0]
            return put
        def put_kv(t, rows, m):
            mv = K.copy(1, vt[:, t, :], rows[:, 256:512], m)

            def use(bank, mk):
                mm = K.copy(0, kT[:, :, t * P:(t + 1) * P], bank[:, 0:256].rearrange("p (h t) -> p h t", h=2), mk)
                ready.append(mm)
                return mm
            ready.append(mv)
            last = K.transposed([rows[:, h * P:(h + 1) * P] for h in range(2)], use, m)[0]
            put_kv.also = mv
            return last

        def use_kv(t, bank, mk):
            b = tok.next()
            c = K.copy(1, b.t[:, :], bank, mk, *b.free)
            d3 = b.t[:, 0:256].rearrange("p (h d) -> p h d", h=2)[:, :, 0:32]
            m = K.rope(w, d3, d3, K.c("cosa")[:, t, :], K.c("sina")[:, t, :], False, mk, c)
            last = put_kv(t, b.t, m)
            b.free = [last, put_kv.also]
            return c
        K.tokens_later(("qi", l), xT, TT, hdeps, rotated(8, "cosi", "sini", IDM // 4, IDM, put_heads(qiT, 0, scored)))

        def use_ki(t, bank, mk):
            b = tok.next()
            c = K.copy(1, b.t[:, 0:64], bank[:, 0:64], mk, *b.free)
            c2 = K.copy(1, wi[:, t, :], bank[:, 64:72], mk)
            m = K.rope(w, b.t[:, 0:16].unsqueeze(1), b.t[:, 0:16].unsqueeze(1), K.c("cosi")[:, t, :],
                       K.c("sini")[:, t, :], False, mk, c)
            m2 = K.copy(0, b.t[:, 64:128], b.t[:, 0:64], m, c)

            def use(bk, mk2):
                mm = K.copy(0, kiT[:, t * P:(t + 1) * P], bk[:, 0:P], mk2)
                scored.append(mm)
                return mm
            scored.append(c2)
            b.free = [K.transposed([b.t[:, 0:128]], use, m2)[0]]

            return c2
        K.tokens_later(("kiwi", l), xT, TT, hdeps, use_ki)
        qs = rotated(4, "cosa", "sina", HD // 4, HD, put_heads(qT, 0)), rotated(4, "cosa", "sina", HD // 4, HD,
                                                                               put_heads(qT, 4))
        K.tokens_later(("q", l, 0), xT, TT, hdeps, qs[0])

        K.flush()
        last = [None, None]
        for t in range(TT):
            for h in range(IH):
                b = K.banks.next()
                r = relu.next()
                p0 = 64 * (h % 2)

                @block.tensor
                def _(pe):
                    for due in K.due(pe, *scored, *b.free):
                        pe.wait_ge(*due)
                    K.mx = K.pe.mark(pe.matmul(b.t[:, 0:SEQ], qiT[p0:p0 + 64, h // 2, t * P:(t + 1) * P],
                                               kiT[p0:p0 + 64, :], start=True, stop=True).then_inc(K.pe.sem, 1))

                @block.scalar
                def _(act):
                    for due in K.due(act, K.mx, *r.free):
                        act.wait_ge(*due)
                    K.my = K.act.mark(act.activation(r.t[:, :], b.t[:, 0:SEQ], ACT.Relu).then_inc(K.act.sem, 1))
                b.free = [K.my]

                @block.vector
                def _(v):
                    for due in K.due(v, K.my, last[t], *scored):
                        v.wait_ge(*due)
                    prev = K.c("causal")[:, t, :] if h == 0 else score[:, t, :]
                    last[t] = K.dve.mark(v.scalar_tensor_tensor(out=score[:, t, :], in0=r.t[:, :],
                                                                scalar=wi[:, t, h:h + 1], in1=prev,
                                                                op0=ALU.mult, op1=ALU.add).then_inc(K.dve.sem, 1))
                r.free = [last[t]]
        K.tokens_later(("q", l, 1), xT, TT, hdeps, qs[1])
        K.tokens_later(("kv", l), xT, TT, hdeps, use_kv)
        gm = {}

        def use_gate(n):
            def use(t, bank, mk):
                @block.scalar
                def _(act):
                    for due in K.due(act, mk):
                        act.wait_ge(*due)
                    K.mg = K.act.mark(act.activation(gate[:, t, 512 * n:512 * n + 512], bank, ACT.Sigmoid).then_inc(K.act.sem, 1))
                gm[n, t] = K.mg
                return K.mg
            return use
        K.tokens_out([("ga", l, 0)], xT, TT, hdeps, use_gate(0))
        for r8 in range(TOPK // 8):
            for t in range(TT):
                src = score if r8 == 0 else left

                @block.vector
                def _(v):
                    for due in K.due(v, last[t]):
                        v.wait_ge(*due)
                    for due in K.due(v, K.dve.mark(v.max(top8[:, t, :], src[:, t, :]).then_inc(K.dve.sem, 1))):
                        v.wait_ge(*due)
                    last[t] = K.dve.mark(v.match_replace(left[:, t, :], top8[:, t, :], src[:, t, :], TAKEN).then_inc(K.dve.sem, 1))
        for t in range(TT):
            @block.vector
            def _(v):
                for due in K.due(v, last[t]):
                    v.wait_ge(*due)
                m = K.dve.mark(v.tensor_scalar(score[:, t, :], left[:, t, :], TAKEN * 0.5, NEG, ALU.is_gt, ALU.mult).then_inc(K.dve.sem, 1))
                for due in K.due(v, m):
                    v.wait_ge(*due)
                last[t] = K.dve.mark(v.tensor_tensor(score[:, t, :], score[:, t, :], K.c("causal")[:, t, :], ALU.add).then_inc(K.dve.sem, 1))

        w["done"] = []
        jobs = []
        for h in range(HEADS):
            g = h // (HEADS // KVH)
            for t in range(TT):
                nk = (t + 1) * P
                jobs.append(K.attend(w, qT[:, h, t * P:(t + 1) * P], kT[:, g, 0:nk],
                                     [vt[:, i, g * HD:(g + 1) * HD] for i in range(t + 1)], nk, HD ** -0.5,
                                     score[:, t, 0:nk], oT[:, h, t * P:(t + 1) * P], [last[t], *ready]))
        pipeline(jobs, 6, K.tokens_steps(("ga", l, 1), xT, TT, hdeps, use_gate(1)), 3)
        attended = list(w["done"])
        for n in range(2):
            def use(t, bank, mk):
                @block.vector
                def _(v):
                    for due in K.due(v, mk, gm[n, t]):
                        v.wait_ge(*due)
                    K.mg = K.dve.mark(v.tensor_tensor(acc[:, t, 512 * n:512 * n + 512], bank,
                                                      gate[:, t, 512 * n:512 * n + 512], ALU.mult).then_inc(K.dve.sem, 1))
                return K.mg
            K.tokens_out([("pa", l, n)], lambda k, t: oT[:, k, t * P:(t + 1) * P], TT, attended, use)
        K.settle()


def first_ssd(K, l, hT, hdeps, acc, cols, rows, silu_c, modrows):
    block = K.block
    with ExitStack() as ctx:
        w = work_buffers(K, ctx, GW, 0)
        xbcT = K.sb("xbcT", [P, XCH, SEQ], ctx=ctx)
        bT = xbcT
        dts = K.sb("dts", [P, TT, 8, SHEADS], ctx=ctx)
        decay = K.turn(ctx, "decay", 4, [P, HPG, P])
        gate = K.sb("gate", [P, TT, D], ctx=ctx)
        xT = lambda k, t: hT[:, k, t * P:(t + 1) * P]
        DTV, ADT, CS, NCS, ECS, W1, W2, W3 = range(8)
        small = []

        def use_dt(t, bank, mk):
            d = lambda i: dts[:, t, i, :]

            @block.vector
            def _(v):
                for due in K.due(v, mk):
                    v.wait_ge(*due)
                m = K.dve.mark(v.tensor_tensor(d(W1), bank[:, 0:SHEADS], rows("dt_bias"), ALU.add).then_inc(K.dve.sem, 1))
                for due in K.due(v, m):
                    v.wait_ge(*due)
                m = K.dve.mark(v.tensor_scalar(d(W2), d(W1), -1.0, None, ALU.mult).then_inc(K.dve.sem, 1))
                for due in K.due(v, m):
                    v.wait_ge(*due)
                K.md = K.dve.mark(v.tensor_tensor(d(W2), d(W2), d(W1), ALU.min).then_inc(K.dve.sem, 1))

            @block.scalar
            def _(act):
                for due in K.due(act, K.md):
                    act.wait_ge(*due)
                m = K.act.mark(act.activation(d(W3), d(W2), ACT.Exp).then_inc(K.act.sem, 1))
                K.me = K.act.mark(act.activation(d(NCS), rows("a_log"), ACT.Exp).then_inc(K.act.sem, 1))
                for due in K.due(act, m):
                    act.wait_ge(*due)

            @block.vector
            def _(v):
                for due in K.due(v, K.me):
                    v.wait_ge(*due)
                for due in K.due(v, K.dve.mark(v.tensor_scalar(d(CS), d(W3), 1.0, None, ALU.add).then_inc(K.dve.sem, 1))):
                    v.wait_ge(*due)
                K.mf = K.dve.mark(v.tensor_scalar(d(ECS), d(CS), -1.0, None, ALU.add).then_inc(K.dve.sem, 1))
                for due in K.due(v, K.mf):
                    v.wait_ge(*due)
                for due in K.due(v, K.dve.mark(v.tensor_tensor(d(ECS), d(ECS), d(W3), ALU.subtract).then_inc(K.dve.sem, 1))):
                    v.wait_ge(*due)
                for due in K.due(v, K.dve.mark(v.reciprocal(d(W2), d(CS)).then_inc(K.dve.sem, 1))):
                    v.wait_ge(*due)
                for due in K.due(v, K.dve.mark(v.tensor_tensor(d(ECS), d(ECS), d(W2), ALU.mult).then_inc(K.dve.sem, 1))):
                    v.wait_ge(*due)

            @block.scalar
            def _(act):
                for due in K.due(act, K.mf, (K.dve, K.dve.count)):
                    act.wait_ge(*due)
                K.me = K.act.mark(act.activation(d(W3), d(CS), ACT.Ln).then_inc(K.act.sem, 1))

            @block.vector
            def _(v):
                for due in K.due(v, K.me):
                    v.wait_ge(*due)
                for due in K.due(v, K.dve.mark(v.tensor_tensor(d(W3), d(W3), d(ECS), ALU.subtract).then_inc(K.dve.sem, 1))):
                    v.wait_ge(*due)
                for due in K.due(v, K.dve.mark(v.tensor_scalar(d(W1), d(W1), 0.0, None, ALU.max).then_inc(K.dve.sem, 1))):
                    v.wait_ge(*due)
                for due in K.due(v, K.dve.mark(v.tensor_tensor(d(DTV), d(W1), d(W3), ALU.add).then_inc(K.dve.sem, 1))):
                    v.wait_ge(*due)
                K.md = K.dve.mark(v.scalar_tensor_tensor(out=d(ADT), in0=d(DTV), scalar=-1.0, in1=d(NCS),
                                                         op0=ALU.mult, op1=ALU.mult).then_inc(K.dve.sem, 1))
            K.rest.append(lambda m=K.md: sums(t, d, m))
            return K.md

        def sums(t, d, mark):
            b = K.banks.next()

            @block.tensor
            def _(pe):
                for due in K.due(pe, mark, *b.free):
                    pe.wait_ge(*due)
                pe.matmul(b.t[:, 0:SHEADS], K.c("upto"), d(ADT), start=True, stop=True)
                K.mp = K.pe.mark(pe.matmul(b.t[:, 64:64 + SHEADS], K.c("ones"), d(ADT), start=True, stop=True).then_inc(K.pe.sem, 1))

            @block.vector
            def _(v):
                for due in K.due(v, K.mp):
                    v.wait_ge(*due)
                K.dve.mark(v.tensor_scalar(d(NCS), b.t[:, 0:SHEADS], -1.0, None, ALU.mult).then_inc(K.dve.sem, 1))
                m = K.dve.mark(v.tensor_copy(d(CS), b.t[:, 0:SHEADS]).then_inc(K.dve.sem, 1))
                for due in K.due(v, m):
                    v.wait_ge(*due)
                m = K.dve.mark(v.tensor_tensor(d(W1), b.t[:, 64:64 + SHEADS], d(CS), ALU.subtract).then_inc(K.dve.sem, 1))
                K.mf = m
            b.free = [K.mf]

            @block.scalar
            def _(act):
                for due in K.due(act, K.mf):
                    act.wait_ge(*due)
                K.act.mark(act.activation(d(ECS), d(CS), ACT.Exp).then_inc(K.act.sem, 1))
                K.me = K.act.mark(act.activation(d(W2), d(W1), ACT.Exp).then_inc(K.act.sem, 1))

            @block.vector
            def _(v):
                for due in K.due(v, K.me):
                    v.wait_ge(*due)
                K.md = K.dve.mark(v.tensor_tensor(d(W2), d(W2), d(DTV), ALU.mult).then_inc(K.dve.sem, 1))
            small.extend([K.md, K.me])
        K.tokens_out([("dt", l)], xT, TT, hdeps, use_dt)

        convd = {}
        ada = Modulation(K, l, ctx, silu_c, modrows)
        scope = ExitStack()
        padded = K.turn(scope, "padded", 3, [P, SEQ + CONV - 1])
        conv = K.turn(scope, "conv", 3, [P, SEQ])
        pending = []
        for n in (4, 5, 0, 1, 2, 3):
            def use(j, bank, mk):
                ch = 4 * n + j
                pd, cv = padded.next(), conv.next()

                @block.vector
                def _(v):
                    for due in K.due(v, *pd.free):
                        v.wait_ge(*due)
                    K.ms = K.dve.mark(v.memset(pd.t[:, 0:CONV - 1], 0.0).then_inc(K.dve.sem, 1))
                m = K.copy(1, pd.t[:, CONV - 1:CONV - 1 + SEQ], bank, mk, *pd.free)

                @block.vector
                def _(v):
                    for due in K.due(v, m, K.ms, *cv.free):
                        v.wait_ge(*due)
                    for i in range(CONV):
                        tap = cols("conv_w", ch * CONV + i)
                        if i == 0:
                            ins = v.tensor_scalar(cv.t[:, :], pd.t[:, 0:SEQ], tap, cols("conv_b", ch),
                                                  ALU.mult, ALU.add)
                        else:
                            ins = v.scalar_tensor_tensor(out=cv.t[:, :], in0=pd.t[:, i:i + SEQ], scalar=tap,
                                                         in1=cv.t[:, :], op0=ALU.mult, op1=ALU.add)
                        K.mv = K.dve.mark(ins.then_inc(K.dve.sem, 1))
                        for due in K.due(v, K.mv):
                            v.wait_ge(*due)
                pd.free = [K.mv]

                @block.scalar
                def _(act):
                    for due in K.due(act, K.mv):
                        act.wait_ge(*due)
                    K.ml = K.act.mark(act.activation(xbcT[:, ch, :], cv.t[:, :], ACT.Silu).then_inc(K.act.sem, 1))
                cv.free = [K.ml]
                convd[ch] = K.ml
                return m
            K.features_out(("xbc", l, n), lambda k: hT[:, k, 0:SEQ], SEQ, hdeps, use)
            pending = ada.sum_up(pending)
            if n < 4:
                pending = ada.weigh(n)
        pending = ada.sum_up(pending)
        scope.close()
        sets = Turn([Buf({n: K.sb(f"{n}{i}", shape, ctx=ctx) for n, shape in (
            ("xs", [P, TT, GW]), ("xdt", [P, TT, GW]), ("zs", [P, TT, GW]), ("brow", [P, STATE]), ("xdec", [P, GW]),
            ("cbT", [P, TT, P]))}) for i in range(2)])
        for each in sets.bufs:
            each.free = [(K.act, K.act.count), (K.dve, K.dve.count)]

        normed = []

        def group(g):
            mine = sets.next()
            prev = mine.free
            xs, xdt, zs, brow, xdec, cbT = (mine.t[n] for n in ("xs", "xdt", "zs", "brow", "xdec", "cbT"))
            state = xdec
            BT, CT = xbcT[:, 16 + g, :], xbcT[:, 20 + g, :]
            chs = [4 * g + j for j in range(4)]
            zm = {}

            def use_z(t, bank, mk):
                @block.scalar
                def _(act):
                    for due in K.due(act, mk, *prev):
                        act.wait_ge(*due)
                    K.mz = K.act.mark(act.activation(zs[:, t, :], bank, ACT.Silu).then_inc(K.act.sem, 1))
                zm[t] = K.mz
                return K.mz
            K.tokens_out([("z", l, g)], xT, TT, hdeps, use_z)
            hv = lambda a: a.rearrange("p (h d) -> p h d", h=HPG)
            per_head = lambda t, i: dts[:, t, i, HPG * g:HPG * (g + 1)].unsqueeze(2).broadcast_to([P, HPG, SHD])
            xm = {}
            for t in range(TT):
                def use(bank, mk):
                    @block.vector
                    def _(v):
                        for due in K.due(v, mk, *small, *prev):
                            v.wait_ge(*due)
                        m = K.dve.mark(v.tensor_tensor(hv(xs[:, t, :]), hv(bank[:, :]),
                                                       rows("d")[:, HPG * g:HPG * (g + 1)].unsqueeze(2)
                                                       .broadcast_to([P, HPG, SHD]), ALU.mult).then_inc(K.dve.sem, 1))
                        K.mv = K.dve.mark(v.tensor_tensor(hv(xdt[:, t, :]), hv(bank[:, :]), per_head(t, DTV), ALU.mult).then_inc(K.dve.sem, 1))
                    xm[t] = [K.mv]
                    if t == 0:
                        @block.vector
                        def _(v):
                            K.mv = K.dve.mark(v.tensor_tensor(hv(xdec[:, :]), hv(bank[:, :]), per_head(t, W2), ALU.mult).then_inc(K.dve.sem, 1))
                        xm["dec"] = K.mv
                    return K.mv
                K.transposed([xbcT[:, ch, t * P:(t + 1) * P] for ch in chs], use, *[convd[c] for c in chs], *prev)
            yield
            def use_b(bank, mk):
                K.mb = K.copy(0, brow[:, :], bank[:, 0:P], mk, *prev)
                return K.mb
            K.transposed([BT[:, 0:P]], use_b, convd[16 + g], *prev)
            b = K.banks.next()

            @block.tensor
            def _(pe):
                for due in K.due(pe, K.mb, xm["dec"], *b.free):
                    pe.wait_ge(*due)
                K.mp = K.pe.mark(pe.matmul(b.t[:, :], brow[:, :], xdec[:, :], start=True, stop=True).then_inc(K.pe.sem, 1))
            sm = K.copy(1, state[:, :], b.t[:, :], K.mp, *prev)
            b.free = [sm]
            yield
            nprev = []

            def chunk(t):
                tl = slice(t * P, (t + 1) * P)
                b = K.banks.next()

                @block.tensor
                def _(pe):
                    for due in K.due(pe, convd[16 + g], convd[20 + g], *b.free):
                        pe.wait_ge(*due)
                    K.mp = K.pe.mark(pe.matmul(b.t[:, 0:P], BT[:, tl], CT[:, tl], start=True, stop=True).then_inc(K.pe.sem, 1))
                cm = K.copy(0, cbT[:, t, :], b.t[:, 0:P], K.mp, *prev)
                b.free = [cm]
                dc = decay.next()
                heads = [[HPG * g + 4 * q + i for i in range(4)] for q in range(HPG // 4)]
                exps = []
                for q, hs in enumerate(heads):
                    bq = K.banks.next()

                    @block.tensor
                    def _(pe):
                        for due in K.due(pe, *small, *bq.free):
                            pe.wait_ge(*due)
                        for i, h in enumerate(hs):
                            ins = pe.matmul(bq.t[:, i * P:(i + 1) * P],
                                            dts[:, t, ADT, h:h + 1].broadcast_to([P, P]), K.c("upto"),
                                            start=True, stop=True)
                        K.mp = K.pe.mark(ins.then_inc(K.pe.sem, 1))

                    @block.vector
                    def _(v):
                        for due in K.due(v, K.mp, *dc.free):
                            v.wait_ge(*due)
                        K.mv = K.dve.mark(v.tensor_tensor(
                            dc.t[:, 4 * q:4 * q + 4, :], bq.t[:, :].rearrange("p (h l) -> p h l", h=4),
                            K.c("segmask").unsqueeze(1).broadcast_to([P, 4, P]), ALU.add).then_inc(K.dve.sem, 1))
                    bq.free = [K.mv]

                    @block.scalar
                    def _(act):
                        for due in K.due(act, K.mv):
                            act.wait_ge(*due)
                        for i, h in enumerate(hs):
                            K.ml = K.act.mark(act.activation(dc.t[:, 4 * q + i, :], dc.t[:, 4 * q + i, :], ACT.Exp,
                                                             bias=dts[:, t, NCS, h:h + 1]).then_inc(K.act.sem, 1))
                    exps.append(K.ml)
                yield
                for q, hs in enumerate(heads):
                    @block.vector
                    def _(v):
                        for due in K.due(v, exps[q], cm):
                            v.wait_ge(*due)
                        K.mv = K.dve.mark(v.tensor_tensor(
                            dc.t[:, 4 * q:4 * q + 4, :], dc.t[:, 4 * q:4 * q + 4, :],
                            cbT[:, t, :].unsqueeze(1).broadcast_to([P, 4, P]), ALU.mult).then_inc(K.dve.sem, 1))
                masked = K.mv
                yield
                by = K.banks.next()

                @block.tensor
                def _(pe):
                    for due in K.due(pe, masked, *xm[t], *by.free):
                        pe.wait_ge(*due)
                    for e in range(HPG):
                        ins = pe.matmul(by.t[:, e * SHD:(e + 1) * SHD], dc.t[:, e, :],
                                        xdt[:, t, e * SHD:(e + 1) * SHD], start=True, stop=True)
                    K.mp = K.pe.mark(ins.then_inc(K.pe.sem, 1))
                dc.free = [K.mp]
                y, tm = xs[:, t, :], xdt[:, t, :]
                ymark = K.mp
                if t == 1:
                    bo = K.banks.next()

                    @block.tensor
                    def _(pe):
                        for due in K.due(pe, sm, *bo.free):
                            pe.wait_ge(*due)
                        K.mo = K.pe.mark(pe.matmul(bo.t[:, :], CT[:, tl], state[:, :], start=True, stop=True).then_inc(K.pe.sem, 1))

                @block.vector
                def _(v):
                    for due in K.due(v, *xm[t], ymark, *small):
                        v.wait_ge(*due)
                    m = K.dve.mark(v.tensor_tensor(y, by.t[:, :], y, ALU.add).then_inc(K.dve.sem, 1))
                    by.free = [m]
                    if t == 1:
                        for due in K.due(v, m, K.mo):
                            v.wait_ge(*due)
                        m = K.dve.mark(v.tensor_tensor(hv(tm), hv(bo.t[:, :]), per_head(t, ECS), ALU.mult).then_inc(K.dve.sem, 1))
                        bo.free = [m]
                        for due in K.due(v, m):
                            v.wait_ge(*due)
                        m = K.dve.mark(v.tensor_tensor(y, y, tm, ALU.add).then_inc(K.dve.sem, 1))
                    for due in K.due(v, m, zm[t]):
                        v.wait_ge(*due)
                    K.mv = K.dve.mark(v.tensor_tensor(y, y, zs[:, t, :], ALU.mult).then_inc(K.dve.sem, 1))
                gated = K.mv
                yield
                m = K.norm_rows(w, y, y, GW, gated)
                yield

                def use(bank, mk):
                    for j in range(4):
                        @block.vector
                        def _(v):
                            for due in K.due(v, mk):
                                v.wait_ge(*due)
                            K.mv = K.dve.mark(v.tensor_scalar(bT[:, 4 * g + j, tl], bank[:, j * P:(j + 1) * P],
                                                              cols("ssd_norm", 4 * g + j), None, ALU.mult).then_inc(K.dve.sem, 1))
                    return K.mv
                mp, md = K.transposed([y[:, j * P:(j + 1) * P] for j in range(4)], use, m)
                nprev.extend([mp, md])
            yield from together([chunk(t) for t in range(TT)])
            normed.extend(nprev)
            mine.free = nprev + [(K.pe, K.pe.count), (K.act, K.act.count), (K.dve, K.dve.count)]
        gm = {}

        def beside():
            for n in range(2):
                def use_gate(t, bank, mk):
                    @block.scalar
                    def _(act):
                        for due in K.due(act, mk):
                            act.wait_ge(*due)
                        K.mg = K.act.mark(act.activation(gate[:, t, 512 * n:512 * n + 512], bank, ACT.Sigmoid)
                                          .then_inc(K.act.sem, 1))
                    gm[n, t] = K.mg
                    return K.mg
                yield from K.tokens_steps(("gs", l, n), xT, TT, hdeps, use_gate)
                yield from ada.steps(4 + n)
            for j in (6, 7):
                yield from ada.steps(j)
        pipeline([group(g) for g in range(GROUPS)], 2, beside())
        for n in range(2):
            def use(t, bank, mk):
                part = acc[:, t, 512 * n:512 * n + 512]
                gated = gate[:, t, 512 * n:512 * n + 512]

                @block.vector
                def _(v):
                    for due in K.due(v, mk, gm[n, t]):
                        v.wait_ge(*due)
                    m = K.dve.mark(v.tensor_tensor(gated, bank, gated, ALU.mult).then_inc(K.dve.sem, 1))
                    for due in K.due(v, m):
                        v.wait_ge(*due)
                    K.mg = K.dve.mark(v.tensor_tensor(part, part, gated, ALU.add).then_inc(K.dve.sem, 1))
                return K.mg
            K.tokens_out([("ps", l, n, k) for k in range(2)], lambda k, t: bT[:, k, t * P:(t + 1) * P], TT, normed, use)
        K.settle()


def project_residual(K, ctx, src, keys, x, use=None):
    sT = K.sb("mergedT", [P, KD, SEQ], ctx=ctx)
    ready = []
    for t in range(TT):
        for h in range(2):
            def put(bank, mk):
                m = K.copy(h, sT[:, 4 * h:4 * h + 4, t * P:(t + 1) * P],
                           bank[:, :].rearrange("p (k t) -> p k t", k=4), mk)
                ready.append(m)
                return m
            K.transposed([src[:, t, (4 * h + j) * P:(4 * h + j + 1) * P] for j in range(4)], put, (K.dve, K.dve.count))
    for n, key in enumerate(keys):
        def add(t, bank, mk):
            part = x[:, t, 512 * n:512 * n + 512]

            @K.block.vector
            def _(v):
                for due in K.due(v, mk):
                    v.wait_ge(*due)
                K.mg = K.dve.mark(v.tensor_tensor(part, part, bank, ALU.add).then_inc(K.dve.sem, 1))
            return K.mg
        K.tokens_out([key], lambda k, t: sT[:, k, t * P:(t + 1) * P], TT, ready, add)


class Modulation:

    def __init__(self, K, l, ctx, silu_c, modrows):
        self.K, self.l, self.silu_c, self.modrows = K, l, silu_c, modrows
        self.acc = K.turn(ctx, "ada", 2, [P, 512])
        self.row = K.turn(ctx, "adarow", 1, [1, 512])

    def weigh(self, j):
        pending = []
        for _ in self.weighing(j, pending):
            pass
        return pending

    def steps(self, j):
        pending = []
        yield from self.weighing(j, pending)
        yield
        self.sum_up(pending)

    def weighing(self, j, out):
        K = self.K
        i, w, landed = K.take(("ada", self.l, j))
        for s in range(2):
            if s == 1 and self.l == 1 and j >= 4:
                yield
                yield
                continue
            a = self.acc.next()
            for k in range(KD):
                c = self.silu_c[0][:, 2 * k + s:2 * k + s + 1]

                @K.block.vector
                def _(v):
                    if k == 0:
                        for due in K.due(v, landed, self.silu_c[1], *a.free):
                            v.wait_ge(*due)
                        K.mv = K.dve.mark(v.tensor_scalar(a.t[:, :], w[:, k, :], c, None, ALU.mult).then_inc(K.dve.sem, 1))
                    else:
                        for due in K.due(v, mark):
                            v.wait_ge(*due)
                        K.mv = K.dve.mark(v.scalar_tensor_tensor(out=a.t[:, :], in0=w[:, k, :], scalar=c, in1=a.t[:, :],
                                                                 op0=ALU.mult, op1=ALU.add).then_inc(K.dve.sem, 1))
                mark = K.mv
                if k == KD - 1:
                    out.append((j, s, a, mark))
                if k % 4 == 3:
                    yield
        K.give(i, mark)

    def sum_up(self, pending):
        K = self.K
        for j, s, a, m in pending:
            b, r = K.banks.next(), self.row.next()

            @K.block.tensor
            def _(pe):
                for due in K.due(pe, m, *b.free):
                    pe.wait_ge(*due)
                K.mp = K.pe.mark(pe.matmul(b.t[0:1, :], K.c("ones")[:, 0:1], a.t[:, :], start=True, stop=True)
                                 .then_inc(K.pe.sem, 1))
            a.free = [K.mp]

            @K.block.gpsimd
            def _(g):
                src = K.A["b_ada_2"][self.l, 512 * j:512 * j + 512]
                K.mb = K.move(g, r.t[:, :], src.partition_broadcast(1), *r.free)

            @K.block.vector
            def _(v):
                for due in K.due(v, K.mp, K.mb):
                    v.wait_ge(*due)
                K.mv = K.dve.mark(v.tensor_tensor(r.t[:, :], b.t[0:1, :], r.t[:, :], ALU.add).then_inc(K.dve.sem, 1))
            b.free = [K.mv]

            @K.block.gpsimd
            def _(g):
                dst = self.modrows[self.l, j // 2, s:s + 1, 512 * (j % 2):512 * (j % 2) + 512]
                K.ms = K.move(g, dst, r.t[:, :], K.mv)
            r.free = [K.ms]
        return []


def first_ffn(K, l, x, hT, cols, silu_c, modrows):
    block = K.block
    with ExitStack() as ctx:
        w = work_buffers(K, ctx)
        gv = K.turn(ctx, "fpad", 4, [P, SEQ + FCONV - 1])
        cv = K.turn(ctx, "fconv", 3, [P, SEQ])
        gates = K.sb("gates", [P, 4, SEQ], ctx=ctx)
        actT = K.sb("actT", [P, FCH, SEQ], ctx=ctx)
        hdeps = rows_to_hT(K, w, lambda t: x[:, t, :], range(TT), hT, lambda k, t: cols("norm_ffn", k), None,
                           [(K.dve, K.dve.count)])
        done = []
        gfree = [[] for _ in range(4)]
        gm = {}

        def convolve(ch, bank, mk, dst, dfree):
            pd = gv.next()

            @block.vector
            def _(v):
                for due in K.due(v, *pd.free):
                    v.wait_ge(*due)
                K.ms = K.dve.mark(v.memset(pd.t[:, 0:FCONV - 1], 0.0).then_inc(K.dve.sem, 1))
            m = K.copy(1, pd.t[:, FCONV - 1:FCONV - 1 + SEQ], bank, mk, *pd.free)

            @block.vector
            def _(v):
                for due in K.due(v, m, K.ms, *dfree):
                    v.wait_ge(*due)
                for i in range(FCONV):
                    tap = cols("fconv_w", ch * FCONV + i)
                    if i == 0:
                        ins = v.tensor_scalar(dst, pd.t[:, 0:SEQ], tap, cols("fconv_b", ch), ALU.mult, ALU.add)
                    else:
                        ins = v.scalar_tensor_tensor(out=dst, in0=pd.t[:, i:i + SEQ], scalar=tap, in1=dst,
                                                     op0=ALU.mult, op1=ALU.add)
                    K.mv = K.dve.mark(ins.then_inc(K.dve.sem, 1))
                    for due in K.due(v, K.mv):
                        v.wait_ge(*due)
            pd.free = [K.mv]
            return m, K.mv
        ada = Modulation(K, l, ctx, silu_c, modrows)
        pending = []
        for n in range(6):
            def use_gate(j, bank, mk):
                m, c = convolve(4 * n + j, bank, mk, gates[:, j, :], gfree[j])

                @block.scalar
                def _(act):
                    for due in K.due(act, c):
                        act.wait_ge(*due)
                    gm[j] = K.act.mark(act.activation(gates[:, j, :], gates[:, j, :], ACT.Silu).then_inc(K.act.sem, 1))
                return m

            def use_val(j, bank, mk):
                d = cv.next()
                m, c = convolve(FCH + 4 * n + j, bank, mk, d.t[:, :], d.free)

                @block.vector
                def _(v):
                    for due in K.due(v, c, gm[j]):
                        v.wait_ge(*due)
                    K.mv = K.dve.mark(v.tensor_tensor(actT[:, 4 * n + j, :], gates[:, j, :], d.t[:, :], ALU.mult).then_inc(K.dve.sem, 1))
                d.free = gfree[j] = [K.mv]
                done.append(K.mv)
                return m
            K.features_out(("fg", l, n), lambda k: hT[:, k, 0:SEQ], SEQ, hdeps, use_gate)
            K.features_out(("fv", l, n), lambda k: hT[:, k, 0:SEQ], SEQ, hdeps, use_val)
            pending = ada.sum_up(pending)
            if n < 4:
                pending = ada.weigh(8 + n)
        for n in range(2):
            def add(t, bank, mk):
                part = x[:, t, 512 * n:512 * n + 512]

                @block.vector
                def _(v):
                    for due in K.due(v, mk):
                        v.wait_ge(*due)
                    K.mg = K.dve.mark(v.tensor_tensor(part, part, bank, ALU.add).then_inc(K.dve.sem, 1))
                return K.mg
            K.tokens_out([("fd", l, n, k) for k in range(3)], lambda k, t: actT[:, k, t * P:(t + 1) * P], TT, done, add)
        K.settle()


def first_block(K, x, xdeps, modrows):
    A, block = K.A, K.block
    with ExitStack() as ctx:
        hT = K.sb("h1T", [P, KD, SEQ], ctx=ctx)
        silu = K.sb("silu_c", [P, 2 * KD], ctx=ctx)
        colt = K.sb("cols1", [P, 2 * PCW], ctx=ctx)
        rowt = K.sb("rows1", [P, PRW], ctx=ctx)

        @block.gpsimd
        def _(g):
            K.pm = [K.move(g, colt[:, :], A["cols1"]), K.move(g, rowt[:, :], A["rows"].partition_broadcast(P))]
            K.pc = K.move(g, silu[:, :], A["cols2"][:, PD["c"]:PD["c"] + 2 * KD])

        @block.scalar
        def _(act):
            for due in K.due(act, K.pc):
                act.wait_ge(*due)
            K.ml = K.act.mark(act.activation(silu[:, :], silu[:, :], ACT.Silu).then_inc(K.act.sem, 1))
        silu_c = (silu, K.ml)
        deps = list(xdeps) + K.pm
        for l in range(2):
            cols = lambda n, i: colt[:, l * PCW + PC[n] + i:l * PCW + PC[n] + i + 1]
            rows = lambda n: rowt[:, PR[n] + 32 * l:PR[n] + 32 * (l + 1)]
            with ExitStack() as mctx:
                acc = K.sb("acc", [P, TT, D], ctx=mctx)
                with ExitStack() as c2:
                    w = work_buffers(K, c2)
                    hdeps = rows_to_hT(K, w, lambda t: x[:, t, :], range(TT), hT, lambda k, t: cols("norm_mix", k),
                                       None, deps)
                    K.settle()
                first_attention(K, l, hT, hdeps, acc)
                first_ssd(K, l, hT, hdeps, acc, cols, rows, silu_c, modrows)
                project_residual(K, mctx, acc, [("wo", l, 0), ("wo", l, 1)], x)
                K.settle()
            if l == 0:
                spread_bias(K)
            first_ffn(K, l, x, hT, cols, silu_c, modrows)
            deps = [(K.dve, K.dve.count)]


def plan_second(K, l):
    A = K.A
    if l == 0:
        win = A["ab_w_in_2"][0]
        K.plan_tile(("cq",), win, 0, KD, 0, QL)
        K.plan_tile(("ckv",), win, 0, KD, QL, KVL + ROPE)
        for n in range(2):
            K.plan_tile(("qup", n), A["mla_w_q_up_2"][0], 0, QL // P, 384 * n, 384)
        for n in range(2):
            K.plan_tile(("kvup", n), A["mla_w_kv_up_2"][0], 0, KVL // P, 512 * n, 512)
        K.plan_tile(("gq",), win, 0, KD, QL + KVL + ROPE, 512)
        K.plan_tile(("gkv",), win, 0, KD, QL + KVL + ROPE + 512, 256)
        for n in range(2):
            K.plan_tile(("abo", n), A["ab_w_out_2"][0], 0, KD, 512 * n, 512)
    else:
        for n in range(6):
            K.plan_tile(("na", n), A["na_w_in_2"][0], 0, KD, 512 * n, 512)
        for n in range(2):
            K.plan_tile(("nao", n), A["na_w_out_2"][0], 0, KD, 512 * n, 512)
    K.plan_experts(l, range(EXPERTS))


def blocks_of(l):
    tiles = NT2 if l == 0 else TT
    return tiles, EXPERTS + (2 * tiles * P) // (CAP + 1)


def modulation_columns(K, l, tmp, both, cols, modrows):
    block = K.block
    rows = K.sb("modr", [2 * 2 * KD, P], ctx=tmp)
    shift, gain = both[:, 0], both[:, 1]

    @block.gpsimd
    def _(g):
        src = modrows[l, MSH1:MSC1 + 1].rearrange("j s (k p) -> (j s k) p", p=P)
        K.pm = K.move(g, rows[:, :], src, *K.settled)

    def use(bank, mk):
        @block.vector
        def _(v):
            for due in K.due(v, mk):
                v.wait_ge(*due)
            K.mg = K.dve.mark(v.tensor_copy(both[:, :, :, :].rearrange("p j s k -> p (j s k)"), bank[:, 0:4 * KD])
                              .then_inc(K.dve.sem, 1))
            for due in K.due(v, K.mg):
                v.wait_ge(*due)
            for s in range(2):
                K.mg = K.dve.mark(v.scalar_tensor_tensor(out=gain[:, s, :], in0=gain[:, s, :], scalar=1.0,
                                                         in1=cols("norm_mix", 8 * l, 8), op0=ALU.add, op1=ALU.mult)
                                  .then_inc(K.dve.sem, 1))
        return K.mg
    K.transposed([rows[:, :]], use, K.pm)
    return shift, gain, [K.mg]


MSH1, MSC1, MG1, MSH2, MSC2, MG2 = range(6)


def add_gated(K, ctx, x_of, keys, xT, tiles, rows, deps):
    tmp = K.turn(ctx, "gated", 2, [P, 512])
    for n, key in enumerate(keys):
        def use(i, bank, mk):
            t = tiles[i]
            tm = tmp.next()
            part = x_of(t)[:, 512 * n:512 * n + 512]

            @K.block.vector
            def _(v):
                for due in K.due(v, mk, *tm.free, *deps):
                    v.wait_ge(*due)
                m = K.dve.mark(v.tensor_tensor(tm.t[:, :], bank, rows(t)[:, 512 * n:512 * n + 512], ALU.mult).then_inc(K.dve.sem, 1))
                for due in K.due(v, m):
                    v.wait_ge(*due)
                K.mg = K.dve.mark(v.tensor_tensor(part, part, tm.t[:, :], ALU.add).then_inc(K.dve.sem, 1))
            tm.free = [K.mg]
            return K.mg
        K.tokens_out([key], lambda k, i: xT(k, tiles[i]), len(tiles), deps, use)


def latent_attention(K, ctx0, hT, hdeps, oT, cols):
    block = K.block
    with ExitStack() as ctx:
        w = work_buffers(K, ctx, 384, 0)
        w["ropea"], w["ropeb"] = (K.turn(ctx, n, 1, [P, 128]) for n in ("ropea", "ropeb"))
        w["prob"] = K.turn(ctx, "prob", 3, [P, 512])
        w["probT"] = K.turn(ctx, "probT", 2, [P, 512])
        tok = K.turn(ctx, "tok", 3, [P, 384])
        cqT = K.sb("cqT", [P, QL // P, NT2 * P], ctx=ctx)
        ckvT = K.sb("ckvT", [P, KVL // P, NT2 * P], ctx=ctx)
        kr = K.sb("kr", [P, NT2, ROPE], ctx=ctx)
        qT = K.sb("qaT", [NOPE + ROPE, HA, NT2 * P], ctx=ctx)
        kT = K.sb("kaT", [NOPE + ROPE, HA, NT2 * P], ctx=ctx)
        va = K.sb("va", [P, NT2, HA, VA], ctx=ctx)
        xT = lambda k, t: hT[:, k, t * P:(t + 1) * P]
        ready, low = [], []

        def use_low(width, norm, dst):
            def use(t, bank, mk):
                b = tok.next()
                c = K.copy(1, b.t[:, 0:bank.shape[1]], bank, mk, *b.free)
                extra = []
                if bank.shape[1] > width:
                    if t >= 2:
                        src = b.t[:, width:width + ROPE].unsqueeze(1)
                        m = K.rope(w, src, kr[:, t:t + 1, :], K.c("cos2a")[:, t - 2, :], K.c("sin2a")[:, t - 2, :],
                                   True, c)
                    else:
                        m = K.copy(0, kr[:, t, :], b.t[:, width:width + ROPE], c)
                    extra.append(m)
                    low.append(m)
                m = K.norm_rows(w, b.t[:, 0:width], b.t[:, 0:width], width, c)

                def put(bk, mk2):
                    for j in range(width // P):
                        @block.vector
                        def _(v):
                            for due in K.due(v, mk2):
                                v.wait_ge(*due)
                            K.mv = K.dve.mark(v.tensor_scalar(dst[:, j, t * P:(t + 1) * P], bk[:, j * P:(j + 1) * P],
                                                              cols(norm, j, 1), None, ALU.mult).then_inc(K.dve.sem, 1))
                    low.append(K.mv)
                    return K.mv
                b.free = [K.transposed([b.t[:, j * P:(j + 1) * P] for j in range(width // P)], put, m)[0], *extra]
                return c
            return use
        K.tokens_out([("cq",)], xT, NT2, hdeps, use_low(QL, "q_norm", cqT))
        K.tokens_out([("ckv",)], xT, NT2, hdeps, use_low(KVL, "kv_norm", ckvT))

        def put_heads(dst, n, t, rows, *ms):
            def put(bank, mk):
                mm = K.copy(1, dst[:, 4 * n:4 * n + 4, t * P:(t + 1) * P],
                            bank[0:96, :].rearrange("p (h t) -> p h t", h=4), mk)
                ready.append(mm)
                return mm
            return K.transposed([rows[:, 96 * h:96 * h + 96] for h in range(4)], put, *ms)[0]
        for n in range(2):
            def use_q(t, bank, mk):
                b = tok.next()
                m = c = K.copy(1, b.t[:, :], bank, mk, *b.free)
                if t >= 2:
                    part = b.t[:, :].rearrange("p (h d) -> p h d", h=4)[:, :, NOPE:96]
                    m = K.rope(w, part, part, K.c("cos2a")[:, t - 2, :], K.c("sin2a")[:, t - 2, :], True, c)
                b.free = [put_heads(qT, n, t, b.t, m)]
                return c
            K.tokens_out([("qup", n)], lambda k, t: cqT[:, k, t * P:(t + 1) * P], NT2, low, use_q)
        for n in range(2):
            def use_kv(t, bank, mk):
                b = tok.next()
                rows = b.t[:, :].rearrange("p (h d) -> p h d", h=4)
                src = bank.rearrange("p (h d) -> p h d", h=4)
                c = K.copy(1, rows[:, :, 0:NOPE], src[:, :, 0:NOPE], mk, *b.free)
                mv = K.copy(1, va[:, t, 4 * n:4 * n + 4, :], src[:, :, NOPE:P], mk)
                m = K.copy(0, rows[:, :, NOPE:96], kr[:, t:t + 1, :].broadcast_to([P, 4, ROPE]), *low, *b.free)
                ready.append(mv)
                b.free = [put_heads(kT, n, t, b.t, m, c)]
                return mv
            K.tokens_out([("kvup", n)], lambda k, t: ckvT[:, k, t * P:(t + 1) * P], NT2, low, use_kv)
        w["done"] = []
        jobs = []
        for h in range(HA):
            for t in range(NT2):
                nk = 256 if t < 2 else 512
                p0 = 64 * (h % 2)
                jobs.append(K.attend(w, qT[:, h, t * P:(t + 1) * P], kT[:, h, 0:nk],
                                     [va[:, i, h, :] for i in range(nk // P)], nk, (NOPE + ROPE) ** -0.5, None,
                                     oT[p0:p0 + 64, h // 2, t * P:(t + 1) * P], ready))
        pipeline(jobs, 3)
        K.settle()


def grouped_attention(K, hT, hdeps, oT, rowt):
    block = K.block
    with ExitStack() as ctx:
        w = work_buffers(K, ctx, 0, 0)
        w["ropea"], w["ropeb"] = (K.turn(ctx, n, 1, [P, 512]) for n in ("ropea", "ropeb"))
        w["prob"] = K.turn(ctx, "prob", 3, [P, 512])
        w["probT"] = K.turn(ctx, "probT", 2, [P, 512])
        sq = K.sb("sq", [P, 512], ctx=ctx)
        sm = K.sb("sm", [P, 16], ctx=ctx)
        tok = K.turn(ctx, "tok", 3, [P, 512])
        kk = K.turn(ctx, "kk", 2, [P, 2, 2, HD2])
        qT = K.sb("qbT", [P, HB // 2, NT2 * P], ctx=ctx)
        kT = K.sb("kbT", [P, KVB, NT2 * P], ctx=ctx)
        vb = K.sb("vb", [P, NT2, KVB, HD2], ctx=ctx)
        xT = lambda k, t: hT[:, k, t * P:(t + 1) * P]
        ready = []
        state = {"free": []}

        def head_norm(rows, heads, norm, t, *deps):
            n = heads * HD2
            s3 = sq[:, 0:n].rearrange("p (h d) -> p h d", h=heads)

            @block.vector
            def _(v):
                for due in K.due(v, *deps, *state["free"]):
                    v.wait_ge(*due)
                m = K.dve.mark(v.tensor_tensor(s3, rows, rows, ALU.mult).then_inc(K.dve.sem, 1))
                for due in K.due(v, m):
                    v.wait_ge(*due)
                K.mv = K.dve.mark(v.tensor_reduce(sm[:, 0:heads], s3, AX.X, ALU.add).then_inc(K.dve.sem, 1))

            @block.scalar
            def _(act):
                for due in K.due(act, K.mv):
                    act.wait_ge(*due)
                K.ml = K.act.mark(act.activation(sm[:, 8:8 + heads], sm[:, 0:heads], ACT.Sqrt, bias=K.eps[:, 0:1],
                                                 scale=1.0 / HD2).then_inc(K.act.sem, 1))

            @block.vector
            def _(v):
                for due in K.due(v, K.ml):
                    v.wait_ge(*due)
                m = K.dve.mark(v.reciprocal(sm[:, 0:heads], sm[:, 8:8 + heads]).then_inc(K.dve.sem, 1))
                for due in K.due(v, m):
                    v.wait_ge(*due)
                m = K.dve.mark(v.tensor_tensor(rows, rows, sm[:, 0:heads].unsqueeze(2).broadcast_to([P, heads, HD2]),
                                               ALU.mult).then_inc(K.dve.sem, 1))
                for due in K.due(v, m):
                    v.wait_ge(*due)
                K.mv = K.dve.mark(v.tensor_tensor(
                    rows, rows, rowt[:, PR[norm]:PR[norm] + HD2].unsqueeze(1).broadcast_to([P, heads, HD2]), ALU.mult).then_inc(K.dve.sem, 1))
            state["free"] = [K.mv]
            m = K.mv
            if t >= 2:
                m = K.rope(w, rows, rows, K.c("cos2b")[:, t - 2, :], K.c("sin2b")[:, t - 2, :], True, m)
            return m

        def use_q(t, bank, mk):
            b = tok.next()
            c = K.copy(1, b.t[:, :], bank, mk, *b.free)
            m = head_norm(b.t[:, :].rearrange("p (h d) -> p h d", h=HB), HB, "gq_norm", t, c)

            def put(bk, mk2):
                mm = K.copy(0, qT[:, :, t * P:(t + 1) * P], bk[:, :].rearrange("p (h t) -> p h t", h=4), mk2)
                ready.append(mm)
                return mm
            b.free = [K.transposed([b.t[:, j * P:(j + 1) * P] for j in range(4)], put, m)[0]]
            return c
        K.tokens_out([("gq",)], xT, NT2, hdeps, use_q)

        def use_kv(t, bank, mk):
            b, kd = tok.next(), kk.next()
            c = K.copy(1, b.t[:, 0:256], bank, mk, *b.free)
            mv = K.copy(1, vb[:, t, :, :], b.t[:, P:2 * P].rearrange("p (g d) -> p g d", g=2), c)
            m = head_norm(b.t[:, 0:P].rearrange("p (h d) -> p h d", h=KVB), KVB, "gk_norm", t, c)
            m2 = K.copy(0, kd.t[:, :, :, :],
                        b.t[:, 0:P].rearrange("p (g d) -> p g d", g=2).unsqueeze(2).broadcast_to([P, 2, 2, HD2]),
                        m, *kd.free)

            def put(bk, mk2):
                mm = K.copy(0, kT[:, :, t * P:(t + 1) * P], bk[:, 0:256].rearrange("p (h t) -> p h t", h=2), mk2)
                ready.append(mm)
                return mm
            ready.append(mv)
            b.free = [m2, mv]
            kd.free = [K.transposed([kd.t[:, g, :, :].rearrange("p a d -> p (a d)") for g in range(2)], put, m2)[0]]
            return c
        K.tokens_out([("gkv",)], xT, NT2, hdeps, use_kv)
        w["done"] = []
        jobs = []
        for h in range(HB):
            for t in range(NT2):
                nk = 256 if t < 2 else 512
                p0, g = 64 * (h % 2), h // (HB // KVB)
                jobs.append(K.attend(w, qT[p0:p0 + 64, h // 2, t * P:(t + 1) * P], kT[p0:p0 + 64, g, 0:nk],
                                     [vb[:, i, g, :] for i in range(nk // P)], nk, HD2 ** -0.5, None,
                                     oT[p0:p0 + 64, 4 + h // 2, t * P:(t + 1) * P], ready))
        pipeline(jobs, 3)
        K.settle()


SPAN_R = 2 * (SEQ // GRID_W) - 1


def spread_bias(K):
    rows_n = SEQ // GRID_W
    span_c = 2 * WIN_C - 1
    K.windows = K.nc.dram_tensor("bias_windows", [GRID_W, HC, SPAN_R, GRID_W], F32).ap()

    @K.block.gpsimd
    def _(g):
        K.spread = []
        for c in range(GRID_W):
            src = bass.AP(K.A["rpb_2"].tensor, (WIN_R - rows_n) * span_c + WIN_C - 1 - c,
                          [[(2 * WIN_R - 1) * span_c, HC], [span_c, SPAN_R], [1, GRID_W]])
            K.spread.append(K.move(g, K.windows[c], src))


def neighbourhood_attention(K, hT, hdeps, oT):
    block = K.block
    rows_n = SEQ // GRID_W
    with ExitStack() as ctx:
        w = work_buffers(K, ctx, 0, 0)
        w["prob"] = K.turn(ctx, "prob", 3, [P, 512])
        w["probT"] = K.turn(ctx, "probT", 2, [P, 512])
        tok = K.turn(ctx, "tok", 3, [P, 512])
        bias = K.turn(ctx, "bias", 3, [P, TT, 512])
        qT = K.sb("qnT", [P, HC // 2, SEQ], ctx=ctx)
        kT = K.sb("knT", [P, HC // 2, NT2 * P], ctx=ctx)
        vn = K.sb("vn", [P, NT2, HC * HD2], ctx=ctx)
        ready = []
        for b in bias.bufs:
            @block.vector
            def _(v):
                b.free = [K.dve.mark(v.memset(b.t[:, :, 0:SEQ], 0.0).then_inc(K.dve.sem, 1))]

        def turned(dst, n):
            def use(i, bank, mk):
                b = tok.next()
                c = K.copy(1, b.t[:, :], bank, mk, *b.free)

                def put(bk, mk2):
                    mm = K.copy(0, dst[:, 4 * n:4 * n + 4, i * P:(i + 1) * P],
                                bk[:, :].rearrange("p (h t) -> p h t", h=4), mk2)
                    ready.append(mm)
                    return mm
                b.free = [K.transposed([b.t[:, j * P:(j + 1) * P] for j in range(4)], put, c)[0]]
                return c
            return use
        for n in range(2):
            K.tokens_out([("na", n)], lambda k, t: hT[:, k, (t + 2) * P:(t + 3) * P], TT, hdeps, turned(qT, n))
        for n in range(2):
            K.tokens_out([("na", 2 + n)], lambda k, t: hT[:, k, t * P:(t + 1) * P], NT2, hdeps, turned(kT, n))
        for n in range(2):
            def use_v(t, bank, mk):
                m = K.copy(1, vn[:, t, 512 * n:512 * n + 512], bank, mk)
                ready.append(m)
                return m
            K.tokens_out([("na", 4 + n)], lambda k, t: hT[:, k, t * P:(t + 1) * P], NT2, hdeps, use_v)
        w["done"] = []

        def head(h):
            b = bias.next()
            marks = []

            @block.gpsimd
            def _(g):
                for r in range(rows_n):
                    src = K.windows[:, h, rows_n - 1 - r:2 * rows_n - 1 - r, :]
                    q0 = GRID_W * (r % 2)
                    dst = b.t[q0:q0 + GRID_W, r // 2, SEQ:2 * SEQ].rearrange("p (a b) -> p a b", a=rows_n)
                    marks.append(K.move(g, dst, src, *b.free, *K.spread))

            @block.vector
            def _(v):
                for due in K.due(v, *marks):
                    v.wait_ge(*due)
                K.mv = K.dve.mark(v.tensor_tensor(b.t[:, :, SEQ:2 * SEQ], b.t[:, :, SEQ:2 * SEQ], K.c("window"), ALU.add).then_inc(K.dve.sem, 1))
            m = K.mv
            p0 = 64 * (h % 2)
            jobs = [K.attend(w, qT[p0:p0 + 64, h // 2, t * P:(t + 1) * P], kT[p0:p0 + 64, h // 2, :],
                             [vn[:, i, h * HD2:(h + 1) * HD2] for i in range(NT2)], 512, HD2 ** -0.5, b.t[:, t, :],
                             oT[p0:p0 + 64, h // 2, t * P:(t + 1) * P], [*ready, m]) for t in range(TT)]
            while jobs:
                for j in list(jobs):
                    try:
                        next(j)
                    except StopIteration:
                        jobs.remove(j)
                yield
            b.free = [(K.dve, K.dve.count)]
        pipeline([head(h) for h in range(HC)], 2)
        K.settle()


def run_experts(K, ctx, l, blocks, tokidx, routed, h_dram, y_dram):
    block = K.block
    xg = K.turn(ctx, "xg", 3, [CAP, D])
    xgT = K.turn(ctx, "xgT", 2, [P, KD, CAP])
    gs = K.turn(ctx, "gs", 2, [P, DE // P, CAP])
    aT = K.turn(ctx, "aT", 2, [P, DE // P, CAP])
    yo = K.turn(ctx, "yo", 2, [CAP, D])
    got, stored = {}, []

    def gather(b):
        x = xg.next()

        @block.gpsimd
        def _(g):
            sig = K.moved.next()
            for due in K.due(g, (sig, sig.count) if sig.count else None, *routed, *x.free):
                g.wait_ge(*due)
            got[b] = (x, sig.mark(g.indirect_dma_start(
                x.t[:, :], None, h_dram, bass.IndirectOffsetOnAxis(ap=tokidx[:, b:b + 1], axis=0)).then_inc(sig.sem, 16), 16))
    hidden = {}

    def widen(b):
        x, mk = got[b]
        xt = xgT.next()
        per = 512 // CAP
        ready = []
        for c in range(KD // per):
            bk = K.banks.next()

            @block.tensor
            def _(pe):
                for due in K.due(pe, mk, *bk.free):
                    pe.wait_ge(*due)
                for j in range(per):
                    kk = c * per + j
                    ins = pe.transpose(bk.t[:, j * CAP:(j + 1) * CAP], x.t[:, kk * P:(kk + 1) * P],
                                       K.ident[0:CAP, 0:CAP])
                K.mp = K.pe.mark(ins.then_inc(K.pe.sem, 1))
            m = K.copy(c, xt.t[:, c * per:(c + 1) * per, :],
                       bk.t[:, :].rearrange("p (k t) -> p k t", k=per), K.mp, *xt.free)
            bk.free = [m]
            ready.append(m)
        x.free = [K.mp]
        outs = []
        for key in ("eg", "eu"):
            i, wv, landed = K.take((key, l, b))
            bk = K.banks.next()

            @block.tensor
            def _(pe):
                for due in K.due(pe, landed, *ready, *bk.free):
                    pe.wait_ge(*due)
                for j in range(DE // P):
                    for k in range(KD):
                        ins = pe.matmul(bk.t[:, j * CAP:(j + 1) * CAP], wv[:, k, j * P:(j + 1) * P],
                                        xt.t[:, k, :], start=(k == 0), stop=(k == KD - 1))
                K.mp = K.pe.mark(ins.then_inc(K.pe.sem, 1))
            K.give(i, K.mp)
            outs.append((bk, K.mp))
        xt.free = [K.mp]
        (bg, mg), (bu, mu) = outs
        g_, a_ = gs.next(), aT.next()
        n = DE // P * CAP
        flat = lambda z: z.t[:, :, :].rearrange("p k t -> p (k t)")

        @block.scalar
        def _(act):
            for due in K.due(act, mg, *g_.free):
                act.wait_ge(*due)
            K.ml = K.act.mark(act.activation(flat(g_), bg.t[:, 0:n], ACT.Silu).then_inc(K.act.sem, 1))
        bg.free = [K.ml]

        @block.vector
        def _(v):
            for due in K.due(v, K.ml, mu, *a_.free):
                v.wait_ge(*due)
            K.mv = K.dve.mark(v.tensor_tensor(flat(a_), flat(g_), bu.t[:, 0:n], ALU.mult).then_inc(K.dve.sem, 1))
        bu.free = g_.free = [K.mv]
        hidden[b] = (a_, K.mv)

    def narrow(b):
        a_, m = hidden[b]
        i, wv, landed = K.take(("ed", l, b))
        y = yo.next()
        ms = []
        for n in range(2):
            bk = K.banks.next()

            @block.tensor
            def _(pe):
                for due in K.due(pe, landed, m, *bk.free):
                    pe.wait_ge(*due)
                for k in range(DE // P):
                    ins = pe.matmul(bk.t[0:CAP, :], a_.t[:, k, :], wv[:, k, 512 * n:512 * n + 512],
                                    start=(k == 0), stop=(k == DE // P - 1))
                K.mp = K.pe.mark(ins.then_inc(K.pe.sem, 1))
            mm = K.copy(n, y.t[:, 512 * n:512 * n + 512], bk.t[0:CAP, :], K.mp, *y.free)
            bk.free = [mm]
            ms.append(mm)
        K.give(i, K.mp)
        a_.free = [K.mp]

        @block.gpsimd
        def _(g):
            y.free = [K.move(g, y_dram[b * CAP:(b + 1) * CAP, :], y.t[:, :], *ms)]
        stored.append(y.free[0])
    for b in blocks[0:2]:
        gather(b)
    for b in blocks:
        if b + 2 in blocks:
            gather(b + 2)
        widen(b)
        if b != blocks[0]:
            narrow(b - 1)
    narrow(blocks[-1])


def further_blocks(K, l, nb, tokidx, xid, routed, h_dram, y_dram):
    nx = nb - EXPERTS
    used = xid[0:1, nx:nx + 1]
    with ExitStack() as ctx:
        X = K.apart(ctx, f"further{l}", 3)
        X.plan_experts(l, range(EXPERTS, nb))
        K.end()
        n = K.nc.values_load(used, min_val=0, max_val=nx)
        with K.nc.If(n > 0):
            X.begin()
            X.start_weights()
            run_experts(X, ctx, l, range(EXPERTS, nb), tokidx, routed, h_dram, y_dram)
            X.settle()
            X.end()
        K.begin()
        for bank in K.banks.bufs:
            bank.free = []


def moe(K, l, streams, hT, modrows, rowt, dram):
    block, A = K.block, K.A
    tiles, nb = blocks_of(l)
    nx = nb - EXPERTS
    deep = tiles * P // CAP
    ids_dram, h_dram, y_dram = dram
    row_of = {}
    x_of = lambda t: streams[t // 2][0][:, t % 2, :] if len(streams) == 2 else streams[0][0][:, t, :]
    s_of = lambda t: streams[t // 2][1] if len(streams) == 2 else streams[0][1]

    def broadcast_row(g, dst, a, s, *deps):
        return K.move(g, dst, modrows[l, a, s].partition_broadcast(P), *deps)

    with ExitStack() as octx:
        wts = K.sb("wts", [P, NT2, 2], ctx=octx)
        yrow = K.sb("yrow", [P, NT2, 2], U32, ctx=octx)
        xid = K.sb("xid", [P, nx + 1], U32, ctx=octx)
        tokidx = K.sb("tokidx", [CAP, nb], U32, ctx=octx)
        with ExitStack() as ctx:
            w = work_buffers(K, ctx, D, 2)
            gain = K.sb("gain2", [P, 2, D], ctx=ctx)
            shift = K.sb("shift2", [P, 2, D], ctx=ctx)
            nrow = K.sb("nrow", [P, D], ctx=ctx)
            router = K.sb("router", [P, KD, 36], ctx=ctx)
            lg = K.turn(ctx, "lg", 2, [P, 36])
            sm = K.turn(ctx, "rsm", 2, [P, 8, 8])
            ix = K.turn(ctx, "rix", 2, [P, 2, 8], U32)
            oh = K.sb("onehot", [P, NT2, 2, EXPERTS], ctx=ctx)
            both = K.sb("both", [P, NT2, EXPERTS], ctx=ctx)
            ek = K.sb("ek", [P, NT2, 2], ctx=ctx)
            cnt = K.sb("cnt", [P, 6, EXPERTS], ctx=ctx)
            cmp = K.sb("cmp", [P, max(nx, 1), EXPERTS], ctx=ctx)
            pos = K.turn(ctx, "pos", 2, [P, 12])
            scr = K.sb("scr", [P, 2, EXPERTS], ctx=ctx)
            tokpos = K.sb("tokpos", [P, NT2, 2], U32, ctx=ctx)
            tokid = K.sb("tokid", [P, NT2], U32, ctx=ctx)
            zero = K.sb("zero", [CAP, nb], U32, ctx=ctx)
            xidf = K.sb("xidf", [P, max(nx, 1)], ctx=ctx)

            @K.block.vector
            def _(v):
                for due in K.due(v, *K.settled):
                    v.wait_ge(*due)
                K.dve.mark(v.memset(zero[:, :], 0).then_inc(K.dve.sem, 1))
                K.mv = K.dve.mark(v.tensor_copy(tokid[:, :], K.c("token")).then_inc(K.dve.sem, 1))
            early = K.mv
            lm = []

            @K.block.gpsimd
            def _(g):
                for _, s in streams:
                    lm.append(broadcast_row(g, gain[:, s, :], MSC2, s, *K.settled))
                    lm.append(broadcast_row(g, shift[:, s, :], MSH2, s))
                lm.append(K.move(g, nrow[:, :], A["norm_ffn_2"][l].partition_broadcast(P)))
                lm.append(K.move(g, router[:, :, :], A["router_2"][l].rearrange("(k p) n -> p k n", p=P)))
                K.move(g, y_dram[EXPERTS * CAP:, :].rearrange("(b p) d -> p b d", p=CAP),
                       x_of(0)[0:CAP].unsqueeze(1).broadcast_to([CAP, nx, D]))
                K.mz = K.move(g, ids_dram.rearrange("(p n) a -> p (n a)", p=CAP), zero[:, :], early)

            @K.block.vector
            def _(v):
                for due in K.due(v, *lm):
                    v.wait_ge(*due)
                for _, s in streams:
                    K.mv = K.dve.mark(v.scalar_tensor_tensor(out=gain[:, s, :], in0=gain[:, s, :], scalar=1.0,
                                                             in1=nrow[:, :], op0=ALU.add, op1=ALU.mult).then_inc(K.dve.sem, 1))
            gm = K.mv
            hstored = []
            onehots = []
            for t in range(tiles):
                s = s_of(t)
                xn = w["xn"].next()
                m = K.norm_rows(w, x_of(t), xn.t[:, :], D, *K.settled, *xn.free)

                @K.block.vector
                def _(v):
                    for due in K.due(v, m, gm):
                        v.wait_ge(*due)
                    m2 = K.dve.mark(v.tensor_tensor(xn.t[:, :], xn.t[:, :], gain[:, s, :], ALU.mult).then_inc(K.dve.sem, 1))
                    for due in K.due(v, m2):
                        v.wait_ge(*due)
                    K.mv = K.dve.mark(v.tensor_tensor(xn.t[:, :], xn.t[:, :], shift[:, s, :], ALU.add).then_inc(K.dve.sem, 1))
                m = K.mv

                @K.block.gpsimd
                def _(g):
                    hstored.append(K.move(g, h_dram[t * P:(t + 1) * P, :], xn.t[:, :], m))
                hm = []
                for hh in range(2):
                    def put(bank, mk):
                        mm = K.copy(1, hT[:, 4 * hh:4 * hh + 4, t * P:(t + 1) * P],
                                    bank[:, :].rearrange("p (k t) -> p k t", k=4), mk, *K.settled)
                        hm.append(mm)
                        return mm
                    mp, _ = K.transposed([xn.t[:, (4 * hh + j) * P:(4 * hh + j + 1) * P] for j in range(4)], put, m)
                xn.free = [mp, hstored[-1]]
                b, L, S, I = K.banks.next(), lg.next(), sm.next(), ix.next()

                @K.block.tensor
                def _(pe):
                    for due in K.due(pe, *hm, *lm, *b.free):
                        pe.wait_ge(*due)
                    for k in range(KD):
                        ins = pe.matmul(b.t[:, 0:36], hT[:, k, t * P:(t + 1) * P], router[:, k, :],
                                        start=(k == 0), stop=(k == KD - 1))
                    K.mp = K.pe.mark(ins.then_inc(K.pe.sem, 1))
                G8, M8, SEL, V8, E4, OHG, F = (S.t[:, i, :] for i in range(7))

                @K.block.vector
                def _(v):
                    for due in K.due(v, K.mp, *L.free, *S.free, *I.free):
                        v.wait_ge(*due)
                    K.dve.mark(v.memset(G8, NEG).then_inc(K.dve.sem, 1))
                    m = K.dve.mark(v.tensor_tensor(L.t[:, :], b.t[:, 0:36],
                                                   rowt[:, PR["b_router"] + 36 * l:PR["b_router"] + 36 * l + 36], ALU.add).then_inc(K.dve.sem, 1))
                    b.free = [m]
                    for due in K.due(v, m):
                        v.wait_ge(*due)
                    for due in K.due(v, K.dve.mark(v.tensor_copy(G8[:, 0:NGR], L.t[:, 0:NGR]).then_inc(K.dve.sem, 1))):
                        v.wait_ge(*due)
                    for due in K.due(v, K.dve.mark(v.max(M8, G8).then_inc(K.dve.sem, 1))):
                        v.wait_ge(*due)
                    for due in K.due(v, K.dve.mark(v.max_index(I.t[:, 0, :], M8, G8).then_inc(K.dve.sem, 1))):
                        v.wait_ge(*due)
                    K.dve.mark(v.tensor_scalar(F[:, 0:1], M8[:, 0:1], -1.0, None, ALU.mult).then_inc(K.dve.sem, 1))
                    for due in K.due(v, K.dve.mark(v.tensor_copy(F[:, 1:2], I.t[:, 0, 0:1]).then_inc(K.dve.sem, 1))):
                        v.wait_ge(*due)
                    for due in K.due(v, K.dve.mark(v.tensor_scalar(OHG[:, 0:NGR], K.c("iota")[:, 0:NGR], F[:, 1:2], None,
                                                         ALU.is_equal).then_inc(K.dve.sem, 1))):
                        v.wait_ge(*due)
                    m = K.dve.mark(v.tensor_scalar(SEL, L.t[:, 4:12], OHG[:, 0:1], None, ALU.mult).then_inc(K.dve.sem, 1))
                    for j in range(1, NGR):
                        for due in K.due(v, m):
                            v.wait_ge(*due)
                        m = K.dve.mark(v.scalar_tensor_tensor(out=SEL, in0=L.t[:, 4 + 8 * j:12 + 8 * j],
                                                              scalar=OHG[:, j:j + 1], in1=SEL, op0=ALU.mult,
                                                              op1=ALU.add).then_inc(K.dve.sem, 1))
                    for due in K.due(v, m):
                        v.wait_ge(*due)
                    for due in K.due(v, K.dve.mark(v.max(V8, SEL).then_inc(K.dve.sem, 1))):
                        v.wait_ge(*due)
                    for due in K.due(v, K.dve.mark(v.max_index(I.t[:, 1, :], V8, SEL).then_inc(K.dve.sem, 1))):
                        v.wait_ge(*due)
                    K.dve.mark(v.tensor_tensor(F[:, 2:3], V8[:, 1:2], V8[:, 0:1], ALU.subtract).then_inc(K.dve.sem, 1))
                    for due in K.due(v, K.dve.mark(v.tensor_copy(ek[:, t, :], I.t[:, 1, 0:2]).then_inc(K.dve.sem, 1))):
                        v.wait_ge(*due)
                    m = K.dve.mark(v.scalar_tensor_tensor(out=ek[:, t, :], in0=F[:, 1:2].broadcast_to([P, 2]),
                                                          scalar=float(EG), in1=ek[:, t, :], op0=ALU.mult, op1=ALU.add).then_inc(K.dve.sem, 1))
                    for due in K.due(v, m):
                        v.wait_ge(*due)
                    for k in range(2):
                        m = K.dve.mark(v.tensor_scalar(oh[:, t, k, :], K.c("iota"), ek[:, t, k:k + 1], None,
                                                       ALU.is_equal).then_inc(K.dve.sem, 1))
                    for due in K.due(v, m):
                        v.wait_ge(*due)
                    K.mv = K.dve.mark(v.tensor_tensor(both[:, t, :], oh[:, t, 0, :], oh[:, t, 1, :], ALU.add).then_inc(K.dve.sem, 1))
                onehots.append(K.mv)

                @K.block.scalar
                def _(act):
                    for due in K.due(act, K.mv):
                        act.wait_ge(*due)
                    K.act.mark(act.activation(E4[:, 0:NGR], L.t[:, 0:NGR], ACT.Exp, bias=F[:, 0:1],
                                              accum_out=F[:, 3:4]).then_inc(K.act.sem, 1))
                    K.ml = K.act.mark(act.activation(F[:, 4:5], F[:, 2:3], ACT.Exp).then_inc(K.act.sem, 1))

                @K.block.vector
                def _(v):
                    for due in K.due(v, K.ml):
                        v.wait_ge(*due)
                    for due in K.due(v, K.dve.mark(v.scalar_tensor_tensor(out=F[:, 5:6], in0=F[:, 4:5], scalar=1.0,
                                                                in1=F[:, 3:4], op0=ALU.add, op1=ALU.mult).then_inc(K.dve.sem, 1))):
                        v.wait_ge(*due)
                    for due in K.due(v, K.dve.mark(v.reciprocal(wts[:, t, 0:1], F[:, 5:6]).then_inc(K.dve.sem, 1))):
                        v.wait_ge(*due)
                    K.mw = K.dve.mark(v.tensor_tensor(wts[:, t, 1:2], wts[:, t, 0:1], F[:, 4:5], ALU.mult).then_inc(K.dve.sem, 1))
                L.free = S.free = I.free = [K.mw, K.ml]
            b = K.banks.next()

            @K.block.tensor
            def _(pe):
                for due in K.due(pe, *onehots, *b.free):
                    pe.wait_ge(*due)
                for t in range(tiles):
                    ins = pe.matmul(b.t[:, 0:EXPERTS], K.c("ones"), both[:, t, :], start=(t == 0), stop=(t == tiles - 1))
                K.mp = K.pe.mark(ins.then_inc(K.pe.sem, 1))
            MORE, INCL, EXCL, ZERO, CNT = (cnt[:, i, :] for i in range(5))

            @K.block.vector
            def _(v):
                for due in K.due(v, K.mp):
                    v.wait_ge(*due)
                m = K.dve.mark(v.tensor_copy(CNT, b.t[:, 0:EXPERTS]).then_inc(K.dve.sem, 1))
                b.free = [m]
                for due in K.due(v, m):
                    v.wait_ge(*due)
                K.dve.mark(v.memset(ZERO, 0.0).then_inc(K.dve.sem, 1))
                m = K.dve.mark(v.tensor_scalar(MORE, CNT, float(CAP), None, ALU.is_gt).then_inc(K.dve.sem, 1))
                for j in range(2, deep):
                    for due in K.due(v, m):
                        v.wait_ge(*due)
                    m = K.dve.mark(v.scalar_tensor_tensor(out=MORE, in0=CNT, scalar=float(j * CAP), in1=MORE,
                                                          op0=ALU.is_gt, op1=ALU.add).then_inc(K.dve.sem, 1))
                for due in K.due(v, m):
                    v.wait_ge(*due)
                for due in K.due(v, K.dve.mark(v.tensor_tensor_scan(INCL, MORE, ZERO, 0.0, ALU.add, ALU.add).then_inc(K.dve.sem, 1))):
                    v.wait_ge(*due)
                m = K.dve.mark(v.tensor_tensor(EXCL, INCL, MORE, ALU.subtract).then_inc(K.dve.sem, 1))
                K.base = m
                m = K.dve.mark(v.tensor_tensor(cmp[:, :, :], INCL.unsqueeze(1).broadcast_to([P, nx, EXPERTS]),
                                               K.c("iota")[:, 0:nx].unsqueeze(2).broadcast_to([P, nx, EXPERTS]),
                                               ALU.is_le).then_inc(K.dve.sem, 1))
                for due in K.due(v, m):
                    v.wait_ge(*due)
                for due in K.due(v, K.dve.mark(v.tensor_reduce(xidf[:, :], cmp[:, :, :], AX.X, ALU.add).then_inc(K.dve.sem, 1))):
                    v.wait_ge(*due)
                for due in K.due(v, K.dve.mark(v.tensor_scalar(xidf[:, :], xidf[:, :], float(EXPERTS - 1), None, ALU.min).then_inc(K.dve.sem, 1))):
                    v.wait_ge(*due)
                K.dve.mark(v.tensor_copy(xid[:, nx:nx + 1], INCL[:, EXPERTS - 1:EXPERTS]).then_inc(K.dve.sem, 1))
                K.mx = K.dve.mark(v.tensor_copy(xid[:, 0:nx], xidf[:, :]).then_inc(K.dve.sem, 1))
            K.xid_ready, K.xid = K.mx, xid
            scattered = []
            prev = K.mx
            for t in range(tiles):
                b = K.banks.next()

                @K.block.tensor
                def _(pe):
                    for due in K.due(pe, *b.free):
                        pe.wait_ge(*due)
                    for u in range(t + 1):
                        ins = pe.matmul(b.t[:, 0:EXPERTS], K.c("before") if u == t else K.c("ones"), both[:, u, :],
                                        start=(u == 0), stop=(u == t))
                    K.mp = K.pe.mark(ins.then_inc(K.pe.sem, 1))
                for k in range(2):
                    q = pos.next()
                    R, XB, Q, REM, BLK, A1, A2, POS, TP = (q.t[:, i:i + 1] for i in range(9))

                    @K.block.vector
                    def _(v):
                        for due in K.due(v, K.mp, *q.free, prev):
                            v.wait_ge(*due)
                        K.dve.mark(v.scalar_tensor_tensor(out=scr[:, 0, :], in0=oh[:, t, k, :], scalar=1.0,
                                                          in1=b.t[:, 0:EXPERTS], op0=ALU.mult, op1=ALU.mult,
                                                          accum_out=R).then_inc(K.dve.sem, 1))
                        m = K.dve.mark(v.scalar_tensor_tensor(out=scr[:, 1, :], in0=oh[:, t, k, :], scalar=1.0, in1=EXCL,
                                                              op0=ALU.mult, op1=ALU.mult, accum_out=XB).then_inc(K.dve.sem, 1))
                        b.free = [m]
                        for due in K.due(v, m):
                            v.wait_ge(*due)
                        m = K.dve.mark(v.tensor_scalar(Q, R, float(CAP), None, ALU.is_ge).then_inc(K.dve.sem, 1))
                        for j in range(2, deep):
                            for due in K.due(v, m):
                                v.wait_ge(*due)
                            m = K.dve.mark(v.scalar_tensor_tensor(out=Q, in0=R, scalar=float(j * CAP), in1=Q,
                                                                  op0=ALU.is_ge, op1=ALU.add).then_inc(K.dve.sem, 1))
                        for due in K.due(v, m):
                            v.wait_ge(*due)
                        K.dve.mark(v.scalar_tensor_tensor(out=REM, in0=Q, scalar=-float(CAP), in1=R, op0=ALU.mult,
                                                          op1=ALU.add).then_inc(K.dve.sem, 1))
                        m = K.dve.mark(v.scalar_tensor_tensor(out=A1, in0=Q, scalar=float(EXPERTS - 1), in1=XB,
                                                              op0=ALU.add, op1=ALU.add).then_inc(K.dve.sem, 1))
                        for due in K.due(v, m):
                            v.wait_ge(*due)
                        m = K.dve.mark(v.tensor_tensor(A1, A1, ek[:, t, k:k + 1], ALU.subtract).then_inc(K.dve.sem, 1))
                        for due in K.due(v, m):
                            v.wait_ge(*due)
                        m = K.dve.mark(v.scalar_tensor_tensor(out=A2, in0=Q, scalar=0.5, in1=A1, op0=ALU.is_gt,
                                                              op1=ALU.mult).then_inc(K.dve.sem, 1))
                        for due in K.due(v, m):
                            v.wait_ge(*due)
                        m = K.dve.mark(v.tensor_tensor(BLK, A2, ek[:, t, k:k + 1], ALU.add).then_inc(K.dve.sem, 1))
                        for due in K.due(v, m):
                            v.wait_ge(*due)
                        K.dve.mark(v.scalar_tensor_tensor(out=POS, in0=BLK, scalar=float(CAP), in1=REM, op0=ALU.mult,
                                                          op1=ALU.add).then_inc(K.dve.sem, 1))
                        m = K.dve.mark(v.scalar_tensor_tensor(out=TP, in0=REM, scalar=float(nb), in1=BLK, op0=ALU.mult,
                                                              op1=ALU.add).then_inc(K.dve.sem, 1))
                        for due in K.due(v, m):
                            v.wait_ge(*due)
                        K.dve.mark(v.tensor_copy(yrow[:, t, k:k + 1], POS).then_inc(K.dve.sem, 1))
                        K.mv = K.dve.mark(v.tensor_copy(tokpos[:, t, k:k + 1], TP).then_inc(K.dve.sem, 1))
                    q.free = [K.mv]
                    prev = K.mv

                    @K.block.gpsimd
                    def _(g):
                        sig = K.moved.next()
                        for due in K.due(g, (sig, sig.count) if sig.count else None, K.mv, K.mz, early):
                            g.wait_ge(*due)
                        scattered.append(sig.mark(g.indirect_dma_start(
                            ids_dram, bass.IndirectOffsetOnAxis(ap=tokpos[:, t, k:k + 1], axis=0),
                            tokid[:, t:t + 1], None).then_inc(sig.sem, 16), 16))

            @K.block.gpsimd
            def _(g):
                K.mt = K.move(g, tokidx[:, :], ids_dram.rearrange("(p n) a -> p (n a)", n=nb), *scattered)
            routed = [K.mt, *hstored]
            K.settle()
        with ExitStack() as ctx:
            run_experts(K, ctx, l, range(EXPERTS), tokidx, routed, h_dram, y_dram)
            K.settle()
        further_blocks(K, l, nb, tokidx, xid, routed, h_dram, y_dram)
        with ExitStack() as ctx:
            yg = K.turn(ctx, "yg", 4, [P, D])
            gate = K.sb("gate2", [P, 2, D], ctx=ctx)
            gm = []

            @K.block.gpsimd
            def _(g):
                for _, s in streams:
                    gm.append(broadcast_row(g, gate[:, s, :], MG2, s, *K.settled))
            for t in range(tiles):
                ys = []
                for k in range(2):
                    y = yg.next()

                    @K.block.gpsimd
                    def _(g):
                        sig = K.moved.next()
                        for due in K.due(g, (sig, sig.count) if sig.count else None, *y.free):
                            g.wait_ge(*due)
                        ys.append((y, sig.mark(g.indirect_dma_start(
                            y.t[:, :], None, y_dram[0:nb * CAP, :],
                            bass.IndirectOffsetOnAxis(ap=yrow[:, t, k:k + 1], axis=0)).then_inc(sig.sem, 16), 16)))

                @K.block.vector
                def _(v):
                    (y0, m0), (y1, m1) = ys
                    for due in K.due(v, m0, m1, *gm):
                        v.wait_ge(*due)
                    for due in K.due(v, K.dve.mark(v.tensor_scalar(y0.t[:, :], y0.t[:, :], wts[:, t, 0:1], None, ALU.mult).then_inc(K.dve.sem, 1))):
                        v.wait_ge(*due)
                    for due in K.due(v, K.dve.mark(v.scalar_tensor_tensor(out=y0.t[:, :], in0=y1.t[:, :], scalar=wts[:, t, 1:2],
                                                                in1=y0.t[:, :], op0=ALU.mult, op1=ALU.add).then_inc(K.dve.sem, 1))):
                        v.wait_ge(*due)
                    for due in K.due(v, K.dve.mark(v.tensor_tensor(y0.t[:, :], y0.t[:, :], gate[:, s_of(t), :], ALU.mult).then_inc(K.dve.sem, 1))):
                        v.wait_ge(*due)
                    K.mv = K.dve.mark(v.tensor_tensor(x_of(t), x_of(t), y0.t[:, :], ALU.add).then_inc(K.dve.sem, 1))
                    y0.free = y1.free = [K.mv]
            K.settle()


def scaled_norm(K, x, row_src, dst):
    with ExitStack() as ctx:
        w = work_buffers(K, ctx, D, 2)
        row = K.sb("row", [P, D], ctx=ctx)

        @K.block.gpsimd
        def _(g):
            K.ms = K.move(g, row[:, :], row_src.partition_broadcast(P), *K.settled)
        rm = K.ms
        for t in range(TT):
            xn = w["xn"].next()
            m = K.norm_rows(w, x[:, t, :], xn.t[:, :], D, *K.settled, *xn.free)

            @K.block.vector
            def _(v):
                for due in K.due(v, m, rm):
                    v.wait_ge(*due)
                K.mv = K.dve.mark(v.tensor_tensor(dst[:, t, :], xn.t[:, :], row[:, :], ALU.mult).then_inc(K.dve.sem, 1))
            xn.free = [K.mv]
        K.settle()


def second_block(K, x, modrows, out):
    A, block, nc = K.A, K.block, K.nc
    with ExitStack() as ctx:
        hT = K.sb("hT", [P, KD, NT2 * P], ctx=ctx)
        colt = K.sb("cols2", [P, PDW], ctx=ctx)
        rowt = K.sb("rows2", [P, PRW], ctx=ctx)
        xc = K.sb("xc", [P, TT, D], ctx=ctx)

        @K.block.gpsimd
        def _(g):
            K.pm = [K.move(g, colt[:, :], A["cols2"]), K.move(g, rowt[:, :], A["rows"].partition_broadcast(P)),
                    K.move(g, xc[:, :, :], A["ctx_2"].rearrange("(t p) d -> p t d", p=P))]
        K.settle()
        cols = lambda n, i, c: colt[:, PD[n] + i:PD[n] + i + c]
        both = [K.sb("shiftgain", [P, 2, 2, KD], ctx=ctx) for l in range(2)]
        with ExitStack() as tmp:
            mods = [modulation_columns(K, l, tmp, both[l], cols, modrows) for l in range(2)]
            K.settle()
        scaled_norm(K, x, A["norm_final_w"], x)
        for l in range(2):
            shift, gain, mdeps = mods[l]
            x_of = lambda t: xc[:, t, :] if t < 2 else x[:, t - 2, :]
            s_of = lambda t: 1 if t < 2 else 0
            with ExitStack() as c2:
                w = work_buffers(K, c2)
                hdeps = rows_to_hT(K, w, x_of, range(NT2), hT, lambda k, t: gain[:, s_of(t), k:k + 1],
                                   lambda k, t: shift[:, s_of(t), k:k + 1], [*K.settled, *mdeps])
                K.settle()
            with ExitStack() as c2:
                oT = K.sb("oT2", [P, KD, NT2 * P if l == 0 else SEQ], ctx=c2)
                if l == 0:
                    latent_attention(K, c2, hT, hdeps, oT, cols)
                    grouped_attention(K, hT, hdeps, oT, rowt)
                else:
                    neighbourhood_attention(K, hT, hdeps, oT)
                g1 = K.sb("g1", [P, 2, D], ctx=c2)
                gm = []

                @K.block.gpsimd
                def _(g):
                    for s in range(2 - l):
                        src = modrows[l, MG1, s]
                        gm.append(K.move(g, g1[:, s, :], src.partition_broadcast(P), *K.settled))
                if l == 0:
                    add_gated(K, c2, x_of, [("abo", 0), ("abo", 1)], lambda k, t: oT[:, k, t * P:(t + 1) * P],
                              [0, 1, 2, 3], lambda t: g1[:, s_of(t), :], gm)
                else:
                    add_gated(K, c2, x_of, [("nao", 0), ("nao", 1)], lambda k, t: oT[:, k, (t - 2) * P:(t - 1) * P],
                              [2, 3], lambda t: g1[:, 0, :], gm)
                K.settle()
            nb = blocks_of(l)[1]
            dram = (nc.dram_tensor(f"slot_tokens{l}", [nb * CAP, 1], U32).ap(),
                    nc.dram_tensor(f"h_rows{l}", [blocks_of(l)[0] * P, D], F32).ap(),
                    nc.dram_tensor(f"y_rows{l}", [nb * CAP, D], F32).ap())
            moe(K, l, [(xc, 1), (x, 0)] if l == 0 else [(x, 0)], hT, modrows, rowt, dram)
        scaled_norm(K, x, A["norm_final_2"], x)

        @K.block.gpsimd
        def _(g):
            for due in K.due(g, K.move(g, out.rearrange("(t p) d -> p t d", p=P), x[:, :, :], *K.settled)):
                g.wait_ge(*due)


def laid_out(i):
    f = lambda a: np.ascontiguousarray(np.asarray(a))
    col = lambda a: f(a).reshape(-1, P).T
    cols1 = []
    for l in range(2):
        taps = lambda w: f(w).reshape(w.shape[0], -1, P).transpose(2, 1, 0).reshape(P, -1)
        cols1 += [col(i["norm_mix_w"][l]), taps(i["ssd_conv_w"][l]), col(i["ssd_conv_b"][l]),
                  col(i["ssd_norm_w"][l]), col(i["norm_ffn_w"][l]), taps(i["ffn_conv_w"][l]),
                  col(i["ffn_conv_b"][l])]
    both = f(np.stack([f(i["c_2"])[0], f(i["c_ctx_2"])])).reshape(2, KD, P).transpose(2, 1, 0).reshape(P, -1)
    cols2 = [both] + [col(i["b_ada_2"][l]) for l in range(2)] + [col(i["norm_mix_2"][l]) for l in range(2)]
    cols2 += [col(i["mla_q_norm_2"][0]), col(i["mla_kv_norm_2"][0])]
    rows = [f(i[n]).reshape(-1) for n in ("ssd_dt_bias", "ssd_a_log", "ssd_d", "gqa_q_norm_2", "gqa_k_norm_2")]
    for l in range(2):
        rows += [f(i["moe_b_rg_2"][l]), f(i["moe_b_re_2"][l])]
    out = {"cols1": np.concatenate(cols1, 1), "cols2": np.concatenate(cols2, 1), "rows": np.concatenate(rows),
           "constants": CONST}
    for n in ("w_in", "w_proj_attn", "w_proj_ssd", "w_out", "ffn_w_up", "ffn_w_down", "norm_final_w", "w_ada_2",
              "b_ada_2", "norm_ffn_2", "norm_final_2", "mla_w_q_up_2", "mla_w_kv_up_2", "ab_w_in_2", "ab_w_out_2",
              "na_w_in_2", "na_w_out_2", "moe_w_gate_2", "moe_w_up_2", "moe_w_down_2"):
        out[n] = f(i[n])
    out["router_2"] = np.concatenate([f(i["moe_w_rg_2"]), f(i["moe_w_re_2"])], 2)
    out["x"] = f(i["x"])[0]
    out["ctx_2"] = f(i["ctx_2"])[0]
    out["rpb_2"] = f(i["na_rpb_2"])[0]
    return {k: np.ascontiguousarray(v) for k, v in out.items()}


def build_program(nc, A, out):
    with ExitStack() as ctx:
        K = Core(nc, ctx, A)
        x = K.sb("x", [P, TT, D])
        modrows = nc.dram_tensor("mod_rows", [2, 6, 2, D], F32).ap()
        for l in range(2):
            plan_first(K, l)
        for l in range(2):
            plan_second(K, l)
        K.start_weights()

        @K.block.gpsimd
        def _(g):
            K.pm = [K.move(g, K.const[:, :], A["constants"]),
                    K.move(g, x[:, :, :], A["x"].rearrange("(t p) d -> p t d", p=P))]

        @K.block.vector
        def _(v):
            K.pm.append(K.dve.mark(v.memset(K.eps[:, :], EPS).then_inc(K.dve.sem, 1)))
        K.settle()
        first_block(K, x, K.settled, modrows)
        second_block(K, x, modrows, out)
        K.end()
        assert K.taken == len(K.plan)


INPUTS = ["constants", "cols1", "cols2", "rows", "x", "ctx_2", "rpb_2", "router_2", "b_ada_2", "w_in", "w_proj_attn",
          "w_proj_ssd", "w_out", "ffn_w_up", "ffn_w_down", "norm_final_w", "w_ada_2", "norm_ffn_2",
          "norm_final_2", "mla_w_q_up_2", "mla_w_kv_up_2", "ab_w_in_2", "ab_w_out_2", "na_w_in_2", "na_w_out_2",
          "moe_w_gate_2", "moe_w_up_2", "moe_w_down_2"]


def kernel(**inputs):
    import concourse.bacc as bacc
    from concourse.bass_utils import run_bass_kernel_spmd

    nc = bacc.Bacc("TRN2", target_bir_lowering=False, num_devices=1)
    data = laid_out(inputs)
    arrays, A = {}, {}
    for name in INPUTS:
        a = data[name]
        arrays[f"in_{name}"] = a
        A[name] = nc.dram_tensor(f"in_{name}", a.shape, mybir.dt.from_np(a.dtype), kind="ExternalInput").ap()
    out = nc.dram_tensor("out_rows", (SEQ, D), F32, kind="ExternalOutput").ap()
    build_program(nc, A, out)
    r = run_bass_kernel_spmd(nc, [arrays], core_ids=[0])
    return r.results[0]["out_rows"].reshape(1, SEQ, D)
```
